# Optimizing a Trainium2 kernel written in Bass

```python
import math
import jax, jax.numpy as jnp
from jax import lax
import numpy as np

D_MODEL = 1024
BATCH = 1
SEQ = 512
DEPTH = 2
DEC_BATCH = 1
DEC_SEQ = 32
PAST_LEN = 256

CHUNK = 64
HEAD_DIM = 64
H_A = 8
H_B = 4
H_C = 16
D_A = H_A * HEAD_DIM
D_B = H_B * 2 * HEAD_DIM
D_C = H_C * HEAD_DIM
IN_AB = 3 * D_A + 3 * D_B
IN_C = 3 * D_C + H_C
A_LEFT_CHUNKS = 8
A_PAST = A_LEFT_CHUNKS * CHUNK
A_BAND = A_PAST + CHUNK
REL_CLIP = 128
D_FF = 2816
N_SUB = 3
MACARON_W = 0.5
Q_BLOCK = 128
EPS = 1e-6
NEG_INF = -1e30
FORGET_BIAS_INIT = 3.0
ATTN_SCALE = HEAD_DIM ** -0.5

kernel_name = 'hybrid_chunk_stream_encoder_step'

def _rmsnorm(x, g):
    x32 = x.astype(jnp.float32)
    y = x32 * lax.rsqrt(jnp.mean(x32 * x32, axis=-1, keepdims=True) + EPS)
    return (y * g.astype(jnp.float32)).astype(x.dtype)

def _swiglu(h, wg, wu, wd):
    return (jax.nn.silu(h @ wg) * (h @ wu)) @ wd

def _alibi_slopes(n):
    return jnp.asarray([2.0 ** (-8.0 * (i + 1) / n) for i in range(n)], jnp.float32)

def _lambda_init(li):
    return 0.8 - 0.6 * math.exp(-0.3 * li)

def _ada(c, w, b):
    mod = jax.nn.silu(c) @ w + b
    return mod.reshape(c.shape[0], N_SUB, 3, c.shape[-1])

def _sub_in(x, mod, i, g_pre):
    return _rmsnorm(x, g_pre) * (1.0 + mod[:, i, 1][:, None]) + mod[:, i, 0][:, None]

def _sub_out(x, mod, i, g_post, out, res_w):
    return x + res_w * (1.0 + mod[:, i, 2][:, None]) * _rmsnorm(out, g_post)

def _blocks(a):
    b, s = a.shape[:2]
    return jnp.moveaxis(a.reshape((b, s // Q_BLOCK, Q_BLOCK) + a.shape[2:]), 1, 0)

def _unblocks(a):
    a = jnp.moveaxis(a, 0, 1)
    return a.reshape((a.shape[0], a.shape[1] * a.shape[2]) + a.shape[3:])

def _band(a):
    b, s = a.shape[:2]
    nc = s // CHUNK
    ap = jnp.pad(a, ((0, 0), (A_PAST, 0), (0, 0), (0, 0)))
    ac = ap.reshape((b, nc + A_LEFT_CHUNKS, CHUNK) + a.shape[2:])
    return jnp.concatenate([ac[:, j:j + nc] for j in range(A_LEFT_CHUNKS + 1)], axis=2)

def _chunk_relpos_core(q, k, v, q_pos, k_pos, valid, table):
    rel = jnp.clip(q_pos[:, None] - k_pos[None, :], -REL_CLIP, REL_CLIP) + REL_CLIP
    bias = table.astype(jnp.float32)[:, rel]
    s = jnp.einsum('bcqhd,bckhd->bchqk', q, k).astype(jnp.float32) * ATTN_SCALE + bias[None, None]
    s = jnp.where(valid[None, :, None, None, :], s, NEG_INF)
    p = jax.nn.softmax(s, axis=-1).astype(v.dtype)
    return jnp.einsum('bchqk,bckhd->bcqhd', p, v)

def _diff_core(q, k, v, q_pos, k_pos, lam, slopes):
    s = jnp.einsum('bqhid,bkhid->bhiqk', q, k).astype(jnp.float32) * ATTN_SCALE
    dist = jnp.abs(q_pos[:, None] - k_pos[None, :]).astype(jnp.float32)
    s = s - slopes[None, :, None, None, None] * dist[None, None, None]
    vis = (k_pos[None, :] // CHUNK) <= (q_pos[:, None] // CHUNK)
    s = jnp.where(vis, s, NEG_INF)
    p = jax.nn.softmax(s, axis=-1)
    attn = (p[:, :, 0] - lam * p[:, :, 1]).astype(v.dtype)
    return jnp.einsum('bhqk,bkhd->bqhd', attn, v)

def _forget_core(q, k, v, dq, dk, q_pos, k_pos):
    s = jnp.einsum('bqhd,bkhd->bhqk', q, k).astype(jnp.float32) * ATTN_SCALE
    s = s + jnp.swapaxes(dq, 1, 2)[..., :, None] - jnp.swapaxes(dk, 1, 2)[..., None, :]
    s = jnp.where(k_pos[None, :] <= q_pos[:, None], s, NEG_INF)
    p = jax.nn.softmax(s, axis=-1).astype(v.dtype)
    return jnp.einsum('bhqk,bkhd->bqhd', p, v)

def _mixer_ab(h, w_in, w_out, relpos, lam_vec, subln, lam_init, cache):
    bsz, t = h.shape[:2]
    proj = h @ w_in
    qa, ka, va, qb, kb, vb = jnp.split(
        proj, [D_A, 2 * D_A, 3 * D_A, 3 * D_A + D_B, 3 * D_A + 2 * D_B], axis=-1)
    qa = qa.reshape(bsz, t, H_A, HEAD_DIM)
    ka = ka.reshape(bsz, t, H_A, HEAD_DIM)
    va = va.reshape(bsz, t, H_A, HEAD_DIM)
    qb = qb.reshape(bsz, t, H_B, 2, HEAD_DIM)
    kb = kb.reshape(bsz, t, H_B, 2 * HEAD_DIM)
    vb = vb.reshape(bsz, t, H_B, 2 * HEAD_DIM)
    lv = lam_vec.astype(jnp.float32)
    lam = jnp.exp(jnp.sum(lv[0] * lv[1])) - jnp.exp(jnp.sum(lv[2] * lv[3])) + lam_init
    slopes = _alibi_slopes(H_B)
    if cache is None:
        nc = t // CHUNK
        valid = (jnp.arange(nc)[:, None] * CHUNK - A_PAST + jnp.arange(A_BAND)[None, :]) >= 0
        out_a = _chunk_relpos_core(qa.reshape(bsz, nc, CHUNK, H_A, HEAD_DIM), _band(ka), _band(va),
                                   A_PAST + jnp.arange(CHUNK), jnp.arange(A_BAND), valid, relpos)
        pos = jnp.arange(t)
        kb4 = kb.reshape(bsz, t, H_B, 2, HEAD_DIM)
        out_b = _unblocks(lax.map(lambda xs: _diff_core(xs[0], kb4, vb, xs[1], pos, lam, slopes),
                                  (_blocks(qb), pos.reshape(-1, Q_BLOCK))))
        w = min(A_PAST, t)
        new = (ka[:, t - w:], va[:, t - w:], kb, vb)
    else:
        cak, cav, cbk, cbv = cache
        past = cbk.shape[1]
        w = cak.shape[1]
        q_pos = past + jnp.arange(t)
        k_pos_a = jnp.concatenate([past - w + jnp.arange(w), q_pos])
        ka_all = jnp.concatenate([cak, ka], axis=1)[:, None]
        va_all = jnp.concatenate([cav, va], axis=1)[:, None]
        out_a = _chunk_relpos_core(qa[:, None], ka_all, va_all, q_pos, k_pos_a,
                                   jnp.ones((1, w + t), dtype=bool), relpos)
        kb_all = jnp.concatenate([cbk, kb], axis=1).reshape(bsz, past + t, H_B, 2, HEAD_DIM)
        vb_all = jnp.concatenate([cbv, vb], axis=1)
        out_b = _diff_core(qb, kb_all, vb_all, q_pos, jnp.arange(past + t), lam, slopes)
        new = (ka, va, kb, vb)
    out_a = out_a.reshape(bsz, t, D_A)
    out_b = (_rmsnorm(out_b, subln) * (1.0 - lam_init)).reshape(bsz, t, D_B)
    return jnp.concatenate([out_a, out_b], axis=-1) @ w_out, new

def _mixer_c(h, w_in, b_f, w_out, cache):
    bsz, t = h.shape[:2]
    proj = h @ w_in
    q, k, v, fl = jnp.split(proj, [D_C, 2 * D_C, 3 * D_C], axis=-1)
    q = q.reshape(bsz, t, H_C, HEAD_DIM)
    k = k.reshape(bsz, t, H_C, HEAD_DIM)
    v = v.reshape(bsz, t, H_C, HEAD_DIM)
    logf = jax.nn.log_sigmoid(fl.astype(jnp.float32) + b_f.astype(jnp.float32))
    if cache is None:
        dcum = jnp.cumsum(logf, axis=1)
        pos = jnp.arange(t)
        out = _unblocks(lax.map(lambda xs: _forget_core(xs[0], k, v, xs[1], dcum, xs[2], pos),
                                (_blocks(q), _blocks(dcum), pos.reshape(-1, Q_BLOCK))))
    else:
        ck, cv, clf = cache
        past = ck.shape[1]
        dpast = jnp.cumsum(clf.astype(jnp.float32), axis=1)
        dpast = dpast - dpast[:, -1:]
        dq = jnp.cumsum(logf, axis=1)
        out = _forget_core(q, jnp.concatenate([ck, k], axis=1), jnp.concatenate([cv, v], axis=1),
                           dq, jnp.concatenate([dpast, dq], axis=1),
                           past + jnp.arange(t), jnp.arange(past + t))
    return out.reshape(bsz, t, D_C) @ w_out, (k, v, logf)

def setup_inputs(seed: int = 0) -> dict:
    key = jax.random.key(seed)
    ks = jax.random.split(key, 32)
    n_even = (DEPTH + 1) // 2
    n_odd = DEPTH // 2
    a_win = min(A_PAST, PAST_LEN)

    def nrm(k, shape, s):
        return jax.random.normal(k, shape, jnp.float32) * s

    return {
        'x_prompt': nrm(ks[0], (BATCH, SEQ, D_MODEL), 1.0),
        'x_sample': nrm(ks[1], (DEC_BATCH, DEC_SEQ, D_MODEL), 1.0),
        'c_prompt': nrm(ks[2], (BATCH, D_MODEL), 1.0),
        'c_sample': nrm(ks[3], (DEC_BATCH, D_MODEL), 1.0),
        'cache_a_k': nrm(ks[4], (n_even, DEC_BATCH, a_win, H_A, HEAD_DIM), 1.0),
        'cache_a_v': nrm(ks[5], (n_even, DEC_BATCH, a_win, H_A, HEAD_DIM), 1.0),
        'cache_b_k': nrm(ks[6], (n_even, DEC_BATCH, PAST_LEN, H_B, 2 * HEAD_DIM), 1.0),
        'cache_b_v': nrm(ks[7], (n_even, DEC_BATCH, PAST_LEN, H_B, 2 * HEAD_DIM), 1.0),
        'cache_c_k': nrm(ks[8], (n_odd, DEC_BATCH, PAST_LEN, H_C, HEAD_DIM), 1.0),
        'cache_c_v': nrm(ks[9], (n_odd, DEC_BATCH, PAST_LEN, H_C, HEAD_DIM), 1.0),
        'cache_c_logf': jax.nn.log_sigmoid(FORGET_BIAS_INIT + nrm(ks[10], (n_odd, DEC_BATCH, PAST_LEN, H_C), 1.0)),
        'w_ada': nrm(ks[11], (DEPTH, D_MODEL, 3 * N_SUB * D_MODEL), 0.1 * D_MODEL ** -0.5),
        'b_ada': nrm(ks[12], (DEPTH, 3 * N_SUB * D_MODEL), 0.02),
        'norm_pre': 1.0 + nrm(ks[13], (DEPTH, N_SUB, D_MODEL), 0.05),
        'norm_post': 1.0 + nrm(ks[14], (DEPTH, N_SUB, D_MODEL), 0.05),
        'ffn_w_gate': nrm(ks[15], (DEPTH, 2, D_MODEL, D_FF), D_MODEL ** -0.5),
        'ffn_w_up': nrm(ks[16], (DEPTH, 2, D_MODEL, D_FF), D_MODEL ** -0.5),
        'ffn_w_down': nrm(ks[17], (DEPTH, 2, D_FF, D_MODEL), D_FF ** -0.5),
        'w_in_ab': nrm(ks[18], (n_even, D_MODEL, IN_AB), D_MODEL ** -0.5),
        'w_out_ab': nrm(ks[19], (n_even, D_A + D_B, D_MODEL), (D_A + D_B) ** -0.5),
        'relpos_a': nrm(ks[20], (n_even, H_A, 2 * REL_CLIP + 1), 0.2),
        'lambda_b': nrm(ks[21], (n_even, 4, HEAD_DIM), 0.1),
        'subln_b': 1.0 + nrm(ks[22], (n_even, 2 * HEAD_DIM), 0.05),
        'w_in_c': nrm(ks[23], (n_odd, D_MODEL, IN_C), D_MODEL ** -0.5),
        'b_f': FORGET_BIAS_INIT + nrm(ks[24], (n_odd, H_C), 0.5),
        'w_out_c': nrm(ks[25], (n_odd, D_C, D_MODEL), D_C ** -0.5),
    }

def reference(x_prompt, x_sample, c_prompt, c_sample,
              cache_a_k, cache_a_v, cache_b_k, cache_b_v, cache_c_k, cache_c_v, cache_c_logf,
              w_ada, b_ada, norm_pre, norm_post, ffn_w_gate, ffn_w_up, ffn_w_down,
              w_in_ab, w_out_ab, relpos_a, lambda_b, subln_b, w_in_c, b_f, w_out_c):

    def run(x, c, sample):
        a_k, a_v, b_k, b_v, c_k, c_v, c_lf = [], [], [], [], [], [], []
        for li in range(DEPTH):
            mod = _ada(c, w_ada[li], b_ada[li])
            h = _sub_in(x, mod, 0, norm_pre[li, 0])
            x = _sub_out(x, mod, 0, norm_post[li, 0],
                         _swiglu(h, ffn_w_gate[li, 0], ffn_w_up[li, 0], ffn_w_down[li, 0]), MACARON_W)
            h = _sub_in(x, mod, 1, norm_pre[li, 1])
            j = li // 2
            if li % 2 == 0:
                cache = (cache_a_k[j], cache_a_v[j], cache_b_k[j], cache_b_v[j]) if sample else None
                out, new = _mixer_ab(h, w_in_ab[j], w_out_ab[j], relpos_a[j], lambda_b[j], subln_b[j],
                                     _lambda_init(li), cache)
                a_k.append(new[0]); a_v.append(new[1]); b_k.append(new[2]); b_v.append(new[3])
            else:
                cache = (cache_c_k[j], cache_c_v[j], cache_c_logf[j]) if sample else None
                out, new = _mixer_c(h, w_in_c[j], b_f[j], w_out_c[j], cache)
                c_k.append(new[0]); c_v.append(new[1]); c_lf.append(new[2])
            x = _sub_out(x, mod, 1, norm_post[li, 1], out, 1.0)
            h = _sub_in(x, mod, 2, norm_pre[li, 2])
            x = _sub_out(x, mod, 2, norm_post[li, 2],
                         _swiglu(h, ffn_w_gate[li, 1], ffn_w_up[li, 1], ffn_w_down[li, 1]), MACARON_W)
        return (x, jnp.stack(a_k), jnp.stack(a_v), jnp.stack(b_k), jnp.stack(b_v),
                jnp.stack(c_k), jnp.stack(c_v), jnp.stack(c_lf))

    y_prompt, p_a_k, p_a_v, p_b_k, p_b_v, p_c_k, p_c_v, p_c_logf = run(x_prompt, c_prompt, False)
    y_sample, s_a_k, s_a_v, s_b_k, s_b_v, s_c_k, s_c_v, s_c_logf = run(x_sample, c_sample, True)
    return (y_prompt, y_sample,
            p_a_k, p_a_v, p_b_k, p_b_v, p_c_k, p_c_v, p_c_logf,
            s_a_k, s_a_v, s_b_k, s_b_v, s_c_k, s_c_v, s_c_logf)


_drawn_inputs = setup_inputs


def setup_inputs(seed=0):
    import zlib

    import numpy as np

    out = dict(_drawn_inputs(seed))
    spreads = {}
    factors = {'relpos_a': 2.927}
    for name, (base, spread) in spreads.items():
        noise = np.random.default_rng([zlib.crc32(name.encode()), seed]).standard_normal(out[name].shape)
        drawn = base * np.exp(spread * noise) if base else spread * noise
        out[name] = __import__('jax').numpy.asarray(drawn.astype(out[name].dtype))
    for name, factor in factors.items():
        out[name] = (out[name] * factor).astype(out[name].dtype)
    return out
```

```python
from contextlib import ExitStack

import numpy as np

import concourse.bass as bass
from concourse import mybir

F32 = mybir.dt.float32
F32R = mybir.dt.float32r
I32 = mybir.dt.int32
ALU = mybir.AluOpType
ACT = mybir.ActivationFunctionType
AX = mybir.AxisListType

P = 128
DM = 1024
KT = DM // P
SEQ, DEC, PAST = 512, 32, 256
TOK = SEQ + DEC
HALF = TOK // 2
QT = SEQ // P
D_FF = 2816
FT = D_FF // P
DK = FT // 2
HD = 64
REL = 128
NSUB = 6
EPS = 1e-6
NEG = -1e30
LAM_INIT = 0.2
PSLOTS = 4
NRAW, NHL = 4, 2
KIND = ["ffn", "ab", "ffn", "ffn", "c", "ffn"]
FL_DECAY = 14
STEPS = 14
LIN_STEPS = 12


class Stream:

    def __init__(self):
        self.units = []
        self.used = [0] * NRAW
        self.last = [None] * NRAW
        self.split = 0
        self.first = {}

    def add(self, name, n, split=True, ring=NRAW):
        self.first[name] = len(self.units)
        for k in range(n):
            slot = k % ring if ring != NRAW else (self.start + k) % NRAW
            prev = self.last[slot]
            self.used[slot] += 1
            self.last[slot] = len(self.units)
            self.units.append((slot, self.used[slot], self.split if split else None, prev))
            self.split += split
        if ring == NRAW:
            self.start = (self.start + n) % NRAW

    start = 0


def plan():
    s = Stream()
    s.add("ada_in0", 16, split=False)
    for j, kind in enumerate(KIND):
        if kind == "ffn":
            s.add(f"gu{j}", 2 * FT)
            if j == 0:
                s.add("ada_gate0", 8, split=False)
                s.add("ada_in1", 16, split=False)
            s.add(f"out{j}", 2 * KT)
        else:
            if kind == "c":
                s.add("forget", 1)
            s.add(f"qkv{j}", 3 * KT, ring=3)
            s.add(f"out{j}", KT)
        if j + 1 < NSUB:
            s.add(f"ada_gate{j + 1}", 8, split=False)
        if j + 2 < NSUB:
            s.add(f"ada_in{j + 2}", 16, split=False)
    return s


def unit_at(s, run, k, i=None, step=0, count=1):
    n = s.first[run] + k

    def prev_split(m):
        idx = s.units[m][2]
        if idx is None or idx < NHL:
            return 0
        return 1 + next(q for q in range(m, -1, -1) if s.units[q][2] == idx - NHL)

    slot, use, idx, prev = s.units[n]
    if i is None or isinstance(i, int):
        n += step * (i or 0)
        slot, use, idx, prev = s.units[n]
        return dict(n=n, slot=slot, landed=16 * use, idx=idx, hl=None if idx is None else idx % NHL,
                    raw_free=0 if prev is None else prev + 1, hl_free=prev_split(n))
    trips = [n + step * t for t in range(count)]
    us = [s.units[t] for t in trips]
    du = us[1][1] - us[0][1] if count > 1 else 0
    for t, u in enumerate(us):
        assert u[0] == slot and u[1] == use + du * t
        assert idx is None or (u[2] == idx + step * t and u[2] % NHL == idx % NHL)
    raw = max((0 if u[3] is None else u[3] + 1) - step * t for t, u in enumerate(us))
    hlf = max(prev_split(m) - step * t for t, m in enumerate(trips))
    return dict(n=n + step * i, slot=slot, landed=16 * (use + du * i), idx=None if idx is None else idx + step * i,
                hl=None if idx is None else idx % NHL, raw_free=max(raw, 0) + step * i, hl_free=max(hlf, 0) + step * i)


def program(nc, ins, outs):
    (x_prompt, x_sample, c_prompt, c_sample, ca_k, ca_v, cb_k, cb_v, cc_k, cc_v, cc_logf,
     w_ada, b_ada, norm_pre, norm_post, ffn_wg, ffn_wu, ffn_wd, w_in_ab, w_out_ab, relpos,
     lambda_b, subln_b, w_in_c, b_f, w_out_c) = ins
    (y_p, y_s, pa_k, pa_v, pb_k, pb_v, pc_k, pc_v, pc_lf, sa_k, sa_v, sb_k, sb_v, sc_k, sc_v, sc_lf) = outs
    ws = plan()

    def colblocks(w):
        return w.rearrange("(k p) (f n) -> f p k n", p=P, n=P)

    ada_d = [colblocks(w_ada[l]) for l in range(2)]
    gate_d = {j: colblocks(ffn_wg[j // 3, (j % 3) // 2]) for j in (0, 2, 3, 5)}
    up_d = {j: colblocks(ffn_wu[j // 3, (j % 3) // 2]) for j in (0, 2, 3, 5)}
    down_d = {j: ffn_wd[j // 3, (j % 3) // 2].rearrange("(h k p) (m n) -> m h p k n", p=P, n=P, h=2)
              for j in (0, 2, 3, 5)}
    inab_d = colblocks(w_in_ab[0])
    outab_d = colblocks(w_out_ab[0])
    inc_d = colblocks(w_in_c[0][:, 0:3 * DM])
    wfl_d = w_in_c[0][:, 3 * DM:3 * DM + 16].rearrange("(k p) n -> p k n", p=P)
    outc_d = colblocks(w_out_c[0])
    rel_scratch = nc.dram_tensor("rel_scratch", (8, P, 384), F32, kind="Internal").ap()
    dec_scratch = nc.dram_tensor("decay_scratch", (16, SEQ + PAST + DEC), F32, kind="Internal").ap()

    def tokcols(prompt, sample):
        p = prompt.rearrange("(t q) (f n) -> f q t n", q=P, n=P)
        s = sample.rearrange("q (f n) -> f q n", n=P)
        return p, s

    def flat(a):
        return a[0, 0].rearrange("t h d -> t (h d)")

    kv_out = {"a": (tokcols(flat(pa_k), flat(sa_k)), tokcols(flat(pa_v), flat(sa_v))),
              "b": (tokcols(flat(pb_k), flat(sb_k)), tokcols(flat(pb_v), flat(sb_v))),
              "c": (tokcols(flat(pc_k), flat(sc_k)), tokcols(flat(pc_v), flat(sc_v)))}
    cache_in = {n: [flat(a).rearrange("(t q) (f n) -> f q t n", q=P, n=P) for a in kv]
                for n, kv in (("a", (ca_k, ca_v)), ("b", (cb_k, cb_v)), ("c", (cc_k, cc_v)))}

    with ExitStack() as ctx:
        def sem(name):
            return ctx.enter_context(nc.semaphore(name))

        cursor = [((nc.sbuf_base + 63) // 64) * 64]

        def sb_at(name, shape, dt, offset):
            return nc.alloc_sbuf_tensor_at(name, shape, dt, offset=offset)

        def size(shape):
            return int(np.prod(shape[1:])) * 4

        def sb(name, shape, dt=F32):
            t = sb_at(name, shape, dt, cursor[0])
            cursor[0] += (size(shape) + 31) // 32 * 32
            return t

        raw = sb("raw", [P, NRAW, DK, P])
        w_hi = sb("w_hi", [P, NHL, DK, P], F32R)
        w_lo = sb("w_lo", [P, NHL, DK, P], F32R)
        x = sb("x", [P, KT, TOK])
        h_at = cursor[0]
        h_hi = sb("h_hi", [P, KT, TOK], F32R)
        h_lo = sb("h_lo", [P, KT, TOK], F32R)
        y = sb_at("y", [P, KT, TOK], F32, h_at)
        work = sb("work", [P, 2, TOK])
        prod = sb("prod", [P, 2, TOK])
        sq_sum = sb("sq_sum", [P, TOK])
        rstd = sb("rstd", [P, TOK])
        ident = sb("ident", [P, P])
        mean_w = sb("mean_w", [P, P])
        causal = sb("causal", [P, P])
        eps = sb("eps", [P, 1])
        silu_c = sb("silu_c", [P, 2, KT])
        norms = sb("norms", [P, 2, NSUB, KT])
        ada_b = sb("ada_b", [P, 2, 9 * KT])
        co_scale = sb("co_scale", [P, KT, 2])
        co_shift = sb("co_shift", [P, KT, 2])
        co_gate = sb("co_gate", [P, KT, 2])
        co_tmp = sb("co_tmp", [P, 2 * KT, 2])
        neg_max = sb("neg_max", [P, 10])
        row_sum = sb("row_sum", [P, 10])
        row_inv = sb("row_inv", [P, 10])
        neg_slope = sb("neg_slope", [P, 4])
        lam = sb("lam", [P, 8])
        sub_g = sb("sub_g", [P, P])
        b_sq = sb("b_sq", [P, 4, QT + 1])
        union = cursor[0]
        act_hi = sb("act_hi", [P, FT, TOK], F32R)
        act_lo = sb("act_lo", [P, FT, TOK], F32R)
        end = cursor[0]
        assert end <= nc.sbuf_usable_end, (end, nc.sbuf_usable_end)

        x_nat = sb_at("x_nat", [P, QT + 1, DM], F32, union)
        rows_at = union + size([1, QT + 1, DM])
        c_rows = sb_at("c_rows", [16, P], F32, rows_at)
        norm_rows = sb_at("norm_rows", [96, P], F32, rows_at + 512)
        ada_rows = sb_at("ada_rows", [72, 2, P], F32, rows_at + 1024)
        lam_in = sb_at("lam_in", [P, 4, HD], F32, rows_at + 2048)
        rel_in = sb_at("rel_in", [8, 257], F32, rows_at + 3072)
        rel_rev = sb_at("rel_rev", [8, 384], F32, rows_at + 3072 + 1056)

        cursor[0] = union
        o_hi = sb("o_hi", [P, KT, TOK], F32R)
        o_lo = sb("o_lo", [P, KT, TOK], F32R)
        qT = sb("qT", [P, 2, TOK])
        kT = sb("kT", [P, 2, TOK])
        vT = sb("vT", [P, TOK])
        k_nat = sb("k_nat", [P, 2, QT + 1, P])
        v_nat = sb("v_nat", [P, 2, QT + 1, P])
        ck_nat = sb("ck_nat", [P, 2, 2, P])
        cv_nat = sb("cv_nat", [P, 2, 2, P])
        ckT = sb("ckT", [P, 2, PAST])
        probs = sb("probs", [P, PSLOTS, SEQ])
        probsT = sb("probsT", [P, 2, QT, P])
        o_nat = sb("o_nat", [P, 2, P])
        mixer_top = cursor[0]
        rel_bias = sb("rel_bias", [P, 8, 2 * P])
        dist = sb("dist", [P, SEQ])
        b_nat = sb("b_nat", [P, 4, QT + 1, P])
        assert cursor[0] <= nc.sbuf_usable_end, (cursor[0], end)
        dist_i = sb_at("dist_i", [P, SEQ], I32, mixer_top + 8 * 1024 + 2048)
        cursor[0] = mixer_top
        dk_b = sb("dk_b", [P, 2, 2, SEQ + PAST + DEC])
        dqT = sb("dqT", [P, QT + 1, 16])
        lf_nat = sb("lf_nat", [P, QT + 1, 16])
        clf_nat = sb("clf_nat", [P, 2, 16])
        bf_col = sb("bf_col", [16, 1])
        logf = sb("logf", [16, TOK])
        decay = sb("decay", [16, SEQ + PAST + DEC])
        assert cursor[0] <= nc.sbuf_usable_end, (cursor[0], end)
        z_t = sb_at("z_t", [16, TOK], F32, mixer_top)
        e_t = sb_at("e_t", [16, TOK], F32, mixer_top + 2176)
        u_t = sb_at("u_t", [16, TOK], F32, mixer_top + 2 * 2176)
        l_t = sb_at("l_t", [16, TOK], F32, mixer_top + 3 * 2176)
        ones16 = sb_at("ones16", [16, TOK], F32, mixer_top + 4 * 2176)

        lin = ctx.enter_context(nc.psum_tensor("lin", [P, 4, 512], F32))
        ps_s = ctx.enter_context(nc.psum_tensor("ps_s", [P, 2, 512], F32))
        ps_t = ctx.enter_context(nc.psum_tensor("ps_t", [P, 512], F32))
        ps_o = ctx.enter_context(nc.psum_tensor("ps_o", [P, 512], F32))
        mod_ps = ps_o[:, 0:48].rearrange("p (q g) -> p q g", g=2)

        def pair(a):
            return lin[:, 2 * a:2 * a + 2, 0:HALF]

        def two(ap):
            return ap.rearrange("p (a n) -> p a n", a=2)

        raw_in = [sem(f"raw_in{k}") for k in range(NRAW)]
        unit_done = sem("unit_done")
        hi_done = sem("hi_done")
        lo_done = sem("lo_done")
        const_in = sem("const_in")
        x_in = sem("x_in")
        pool_const = sem("pool_const")
        const_tr = sem("const_tr")
        silu_c_done = sem("silu_c_done")
        vec_const = sem("vec_const")
        xt_ps = sem("xt_ps")
        x_ready = sem("x_ready")
        gate_read = sem("gate_read")
        prod_done = sem("prod_done")
        act_hi_done = sem("act_hi_done")
        act_lo_done = sem("act_lo_done")
        sq_done = sem("sq_done")
        y_copied = sem("y_copied")
        sq_added = sem("sq_added")
        sq_used = sem("sq_used")
        mean_done = sem("mean_done")
        std_done = sem("std_done")
        rstd_done = sem("rstd_done")
        y_norm = sem("y_norm")
        t_done = sem("t_done")
        h_hi_done = sem("h_hi_done")
        h_lo_done = sem("h_lo_done")
        coef = sem("coef")
        kv_evac = sem("kv_evac")
        tr_ps = sem("tr_ps")
        tr_out = sem("tr_out")
        cache_k = [sem(f"cache_k{k}") for k in range(2)]
        cache_v = [sem(f"cache_v{k}") for k in range(2)]
        kv_stored = [sem(f"kv_stored{k}") for k in range(2)]
        lf_stored = sem("lf_stored")
        s_ps = sem("s_ps")
        s_added = sem("s_added")
        s_maxed = sem("s_maxed")
        exp_done = sem("exp_done")
        inv_done = sem("inv_done")
        comb_half = sem("comb_half")
        comb_done = sem("comb_done")
        pt_used = sem("pt_used")
        pv_done = sem("pv_done")
        o_read = sem("o_read")
        ot_ps = sem("ot_ps")
        o_hi_done = sem("o_hi_done")
        o_lo_done = sem("o_lo_done")
        b_sq_done = sem("b_sq_done")
        b_std = sem("b_std")
        b_inv = sem("b_inv")
        b_scaled = sem("b_scaled")
        rel_done = sem("rel_done")
        rel_dram = sem("rel_dram")
        rel_loaded = sem("rel_loaded")
        dist_done = sem("dist_done")
        lam_landed = sem("lam_landed")
        lam_done = sem("lam_done")
        fl_done = sem("fl_done")
        fl_act = sem("fl_act")
        fl_in = sem("fl_in")
        fl_ps = sem("fl_ps")
        fl_dram = sem("fl_dram")
        dk_in = [sem(f"dk_in{k}") for k in range(2)]
        masked = sem("masked")
        settled = sem("settled")
        nat_a = sem("nat_a")
        nat_ps = sem("nat_ps")
        nat_out = sem("nat_out")
        stored = sem("stored")

        block = ctx.enter_context(nc.Block())

        sq_base = [8 + 16 * j for j in range(NSUB)]

        def loop(eng, n, body):
            if n == 1:
                body(0)
            elif n > 1:
                with eng.Fori(0, n) as i:
                    body(i)

        def mixer_counts(kind):
            c = [dict(s=0, tr=0, pv=0, ot=0, comb=0) for _ in range(10)]
            for st in range(9):
                n = dict(c[st])
                k = who(kind, st - 1)
                if st >= 1:
                    n["s"] += 10
                    n["tr"] += 5 if k == "b" else 10
                    n["pv"] += 5 if k == "b" else 10
                    n["ot"] += 0 if k == "b" else 5
                    n["comb"] += 5 if k == "b" else 0
                if st < 8:
                    n["tr"] += 3
                c[st + 1] = n
            return c

        def who(kind, p):
            return "c" if kind == "c" else "ab"[p % 2]

        counts = {k: mixer_counts(k) for k in ("ab", "c")}
        off = {"ab": dict(s=0, tr=0, pv=0, ot=0, comb=0, ev=0), "c": dict(counts["ab"][9])}
        off["c"]["ev"] = 24
        off["c"]["ot"] += 8

        class Stage:

            def __init__(self, kind, st, i=None, trips=1):
                self.kind, self.st, self.i, self.trips = kind, st, i, trips
                self.ii = 0 if i is None else i
                self.att = who(kind, st - 1) if st >= 1 else None
                self.par = (st - 1) % 2 if st >= 1 else None
                self.new = st % 2 if st < 8 else None
                half = 0 if kind == "ab" else 4
                self.same_new = half + st // 2 + self.ii
                self.same_att = half + (st - 1) // 2 + self.ii
                self.order = [(t, hh) for t in (3, 2, 1, 0, QT) for hh in (0, 1)]

            def at(self, key):
                c = counts[self.kind]
                d = c[self.st + 2][key] - c[self.st][key] if self.i is not None else 0
                return off[self.kind][key] + c[self.st][key] + d * self.ii

            def ev(self):
                return off[self.kind]["ev"] + 3 * self.st + 6 * self.ii

            def pairs(self):
                return (0 if self.kind == "ab" else 8) + self.st + 2 * self.ii

            def tile_of(self, p_off):
                p = self.st + p_off
                return (p // 2 if self.kind == "ab" else p) + (1 if self.kind == "ab" else 2) * self.ii

            def unit(self, k):
                run = "qkv1" if self.kind == "ab" else "qkv4"
                if self.i is None:
                    return unit_at(ws, run, 3 * self.st + k)
                return unit_at(ws, run, 3 * self.st + k, self.i, 6, self.trips)

        def stages(eng, kind, emit, after_first=None):
            emit(Stage(kind, 0))
            if after_first is not None:
                after_first()
            with eng.Fori(0, 3) as i:
                emit(Stage(kind, 1, i, 3))
                emit(Stage(kind, 2, i, 3))
            emit(Stage(kind, 7))
            emit(Stage(kind, 8))

        def settle(eng):
            eng.sem_inc(settled, 1)

        def next_unit(st):
            return st.unit(3) if st.st < 7 else None

        def tr_plan(st):
            lag = 3 if st.att == "b" else 2
            found = []
            for s in range(STEPS + 2):
                if st.new is not None and s in (5, 9, 12):
                    found.append((s, "turn"))
                j = s - lag
                if st.att is not None and 0 <= j < 10 and (st.att != "b" or j % 2):
                    found.append((s, "probs"))
            return found

        def ffn_index(j):
            return KIND[:j].count("ffn")

        def next_gu(j, i, a):
            return unit_at(ws, f"gu{j}", 2 * a + 2, i, 4, FT // 2 - 1)

        def next_down(j, i, a):
            return unit_at(ws, f"out{j}", 2 * a + 2, i, 4, KT // 2 - 1)

        def keys(t):
            return (t + 1) * P if t < QT else PAST + DEC

        def rows(t):
            return P if t < QT else DEC

        @block.sync
        def _(sp):
            def load(u, src, tiles, cols=P):
                sp.wait_ge(unit_done, u["raw_free"])
                sp.dma_start(raw[:, u["slot"], 0:tiles, 0:cols], src).then_inc(raw_in[u["slot"]], 16)

            def load_ada(run, n, j, c):
                src = ada_d[j // 3]
                f0 = (3 * (j % 3) + c) * KT

                def body(i):
                    for k in range(4):
                        load(unit_at(ws, run, k, i, 4, n // 4), src[f0 + k + 4 * i], KT)
                loop(sp, n // 4, body)

            sp.dma_start(c_rows[0:8, :], c_prompt.rearrange("g (k p) -> (g k) p", p=P)).then_inc(const_in, 16)
            sp.dma_start(c_rows[8:16, :], c_sample.rearrange("g (k p) -> (g k) p", p=P)).then_inc(const_in, 16)
            for k, src in enumerate((norm_pre, norm_post)):
                sp.dma_start(norm_rows[48 * k:48 * k + 48, :],
                             src.rearrange("l s (k p) -> (l s k) p", p=P)).then_inc(const_in, 16)
            for l in range(2):
                sp.dma_start(ada_rows[:, l, :], b_ada[l].rearrange("(f p) -> f p", p=P)).then_inc(const_in, 16)
            sp.dma_start(x_nat[:, 0:QT, :], x_prompt[0].rearrange("(t q) n -> q t n", q=P)).then_inc(x_in, 16)
            sp.dma_start(x_nat[0:DEC, QT, :], x_sample[0]).then_inc(x_in, 16)
            load_ada("ada_in0", 16, 0, 0)
            for j, kind in enumerate(KIND):
                if kind == "ffn":
                    def gu(i, j=j):
                        for k in range(4):
                            src = (gate_d, up_d)[k % 2][j][2 * i + k // 2]
                            load(unit_at(ws, f"gu{j}", k, i, 4, FT // 2), src, KT)
                    loop(sp, FT // 2, gu)
                    if j == 0:
                        load_ada("ada_gate0", 8, 0, 2)
                        load_ada("ada_in1", 16, 1, 0)

                    def down(i, j=j):
                        for k in range(4):
                            load(unit_at(ws, f"out{j}", k, i, 4, KT // 2), down_d[j][2 * i + k // 2, k % 2], DK)
                    loop(sp, KT // 2, down)
                else:
                    if kind == "c":
                        load(unit_at(ws, "forget", 0), wfl_d, KT, 16)

                    def qkv(st):
                        if st.st == 8:
                            return
                        if kind == "ab":
                            first = 12 * (st.new) + st.tile_of(0)
                            blocks = [first + 4, first + 8, first]
                            src = inab_d
                        else:
                            first = st.tile_of(0)
                            blocks = [first + 8, first + 16, first]
                            src = inc_d
                        for k in range(3):
                            load(st.unit(k), src[blocks[k]], KT)
                    stages(sp, kind, qkv)
                    for m in range(KT):
                        load(unit_at(ws, f"out{j}", m), (outab_d if kind == "ab" else outc_d)[m], KT)
                if j + 1 < NSUB:
                    load_ada(f"ada_gate{j + 1}", 8, j + 1, 2)
                if j + 2 < NSUB:
                    load_ada(f"ada_in{j + 2}", 16, j + 2, 0)
            for t in range(QT + 1):
                sp.wait_ge(nat_out, 2 * t + 2)
                if t < QT:
                    sp.dma_start(y_p[0, t * P:(t + 1) * P, :], x_nat[:, t, :]).then_inc(stored, 16)
                else:
                    sp.dma_start(y_s[0], x_nat[0:DEC, t, :]).then_inc(stored, 16)
            sp.wait_ge(stored, 16 * (QT + 1))
            for par in range(2):
                sp.wait_ge(kv_stored[par], 64 * 8)
            sp.wait_ge(lf_stored, 32)

        @block.gpsimd
        def _(pool):
            nc.gpsimd.memset(ident[:], 0.0).then_inc(pool_const, 1)
            nc.gpsimd.memset(mean_w[:], 1.0 / DM).then_inc(pool_const, 1)
            nc.gpsimd.memset(causal[:], 0.0).then_inc(pool_const, 1)
            nc.gpsimd.memset(eps[:], EPS).then_inc(pool_const, 1)
            for h in range(4):
                nc.gpsimd.memset(neg_slope[:, h:h + 1], -(2.0 ** (-8.0 * (h + 1) / 4))).then_inc(pool_const, 1)
            pool.wait_ge(pool_const, 8)
            nc.gpsimd.affine_select(out=ident[:], in_=ident[:], compare_op=ALU.not_equal, fill=1.0, base=0,
                                    pattern=[[-1, P]], channel_multiplier=1).then_inc(pool_const, 1)
            nc.gpsimd.affine_select(out=causal[:], in_=causal[:], compare_op=ALU.is_ge, fill=NEG, base=0,
                                    pattern=[[-1, P]], channel_multiplier=1).then_inc(pool_const, 1)
            pool.dma_start(lam_in[:].rearrange("p a d -> p (a d)"),
                           lambda_b[0].rearrange("(o a) d -> o (a d)", o=1).broadcast_to([P, 4 * HD])).then_inc(lam_landed, 16)
            pool.dma_start(sub_g[:], subln_b[0:1, :].broadcast_to([P, P])).then_inc(lam_landed, 16)
            pool.dma_start(rel_in[:], relpos[0]).then_inc(rel_dram, 16)
            pool.wait_ge(rel_done, 2)
            pool.dma_start(rel_scratch[:, :, :], rel_rev[:].rearrange("h (o n) -> h o n", o=1).broadcast_to([8, P, 384]))\
                .then_inc(rel_dram, 16)
            pool.wait_ge(rel_dram, 32)

            def kv(st):
                att = st.kind
                if st.st < 8:
                    n = who(st.kind, st.st)
                    pool.wait_ge(pv_done, st.at("pv"))
                    settle(pool)
                    pool.dma_start(ck_nat[:, st.new], cache_in[n][0][st.tile_of(0)]).then_inc(cache_k[st.new], 16)
                    pool.dma_start(cv_nat[:, st.new], cache_in[n][1][st.tile_of(0)]).then_inc(cache_v[st.new], 16)
                    if n == "c":
                        for hh in range(2):
                            pool.dma_start(dk_b[:, st.new, hh, :],
                                           dec_rows[2 * st.tile_of(0) + hh].broadcast_to([P, SEQ + PAST + DEC])
                                           ).then_inc(dk_in[st.new], 16)
                    pool.wait_ge(tr_out, st.at("tr") + (counts[st.kind][st.st + 1]["tr"] - counts[st.kind][st.st]["tr"]))
                    settle(pool)
                    for src, (dp, ds) in zip((k_nat, v_nat), kv_out[n]):
                        pool.dma_start(dp[st.tile_of(0)], src[:, st.new, 0:QT, :]).then_inc(kv_stored[st.new], 16)
                        pool.dma_start(ds[st.tile_of(0)], src[0:DEC, st.new, QT, :]).then_inc(kv_stored[st.new], 16)

            dec_rows = dec_scratch.rearrange("h (o n) -> h o n", o=1)
            pool.wait_ge(mean_done, 2)
            for hd in range(8):
                src = bass.AP(rel_scratch.tensor, 384 * P * hd + P - 1, [[384 - 1, P], [1, 2 * P]])
                pool.dma_start(rel_bias[:, hd, :], src).then_inc(rel_loaded, 16)
            nc.gpsimd.iota(dist_i[:], pattern=[[-1, SEQ]], base=SEQ - P, channel_multiplier=1).then_inc(pool_const, 1)
            stages(pool, "ab", kv)
            pool.wait_ge(mean_done, 8)
            pool.dma_start(clf_nat[:], cc_logf[0, 0].rearrange("(t q) h -> q t h", q=P)).then_inc(fl_in, 16)
            pool.dma_start(bf_col[:], b_f.rearrange("a h -> h a")).then_inc(fl_in, 16)
            pool.wait_ge(fl_done, FL_DECAY)
            pool.dma_start(dec_scratch[:, :], decay[:]).then_inc(fl_dram, 16)
            pool.wait_ge(fl_dram, 16)
            stages(pool, "c", kv)
            pool.wait_ge(fl_act, 4)
            pool.dma_start(pc_lf[0, 0].rearrange("(t q) h -> q t h", q=P), lf_nat[:, 0:QT, :]).then_inc(lf_stored, 16)
            pool.dma_start(sc_lf[0, 0], lf_nat[0:DEC, QT, :]).then_inc(lf_stored, 16)

        @block.tensor
        def _(pe):
            def products(u, out, k, moving_hi, moving_lo, first, last):
                hl = u["hl"]
                m = None
                for n, (w, mv) in enumerate(((w_hi, moving_hi), (w_hi, moving_lo), (w_lo, moving_hi))):
                    for a in range(2):
                        m = nc.tensor.matmul(lin[:, 2 * out + a, 0:HALF], w[:, hl, k, :],
                                             mv[:, a * HALF:(a + 1) * HALF],
                                             start=first and n == 0, stop=last and n == 2)
                return m

            def unit(u, out, tiles, hi, lo, k0=0, first=True, last=True, gradual=None):
                pe.wait_ge(lo_done, u["idx"] + 1)
                for k in range(tiles):
                    if gradual is not None:
                        pe.wait_ge(h_lo_done, gradual + k + 1)
                    m = products(u, out, k, hi[:, k0 + k, :], lo[:, k0 + k, :],
                                 first and k == 0, last and k == tiles - 1)
                m.then_inc(unit_done, 1)

            def ada(run, n, q0):
                def body(i):
                    for k in range(4):
                        u = unit_at(ws, run, k, i, 4, n // 4)
                        pe.wait_ge(raw_in[u["slot"]], u["landed"])
                        for kt in range(KT):
                            m = nc.tensor.matmul(mod_ps[:, q0 + k + 4 * i, :], raw[:, u["slot"], kt, :],
                                                 silu_c[:, :, kt], start=kt == 0, stop=kt == KT - 1)
                        m.then_inc(unit_done, 1)
                loop(pe, n // 4, body)

            def mean(src, first, last):
                for a in range(2):
                    m = nc.tensor.matmul(ps_s[:, a, 0:HALF], mean_w[:], src[:, a * HALF:(a + 1) * HALF],
                                         start=first, stop=last)
                return m

            def post_norm(j):
                pe.wait_ge(sq_added, 9 * (j + 1))
                mean(sq_sum[:], True, True).then_inc(mean_done, 1)

            def pre_norm(j):
                for m in range(KT):
                    pe.wait_ge(sq_done, sq_base[j] - 8 + m + 1)
                    mm = mean(work[:, m % 2, :], m == 0, m == KT - 1)
                    if m < KT - 1:
                        mm.then_inc(sq_used, 1)
                mm.then_inc(mean_done, 1)

            pe.wait_ge(pool_const, 10)
            pe.wait_ge(const_in, 16 * 6)
            nc.tensor.transpose(ps_s[:, 0, 0:16], c_rows[:], ident[0:16, 0:16])
            nc.tensor.transpose(ps_s[:, 0, 16:112], norm_rows[:], ident[0:96, 0:96]).then_inc(const_tr, 1)
            nc.tensor.transpose(ps_s[:, 1, 0:72], ada_rows[:, 0, :], ident[0:72, 0:72])
            nc.tensor.transpose(ps_s[:, 1, 72:144], ada_rows[:, 1, :], ident[0:72, 0:72]).then_inc(const_tr, 1)
            pe.wait_ge(x_in, 32)
            for m in range(KT):
                if m >= 2:
                    pe.wait_ge(x_ready, m - 1)
                for t in range(QT):
                    nc.tensor.transpose(lin[:, 2 * (m % 2), t * P:(t + 1) * P], x_nat[:, t, m * P:(m + 1) * P], ident[:])
                nc.tensor.transpose(lin[:, 2 * (m % 2) + 1, 0:DEC], x_nat[0:DEC, QT, m * P:(m + 1) * P],
                                    ident[0:DEC, 0:DEC]).then_inc(xt_ps, 1)
            pe.wait_ge(silu_c_done, 1)
            ada("ada_in0", 16, 8)
            pe.wait_ge(vec_const, 2)
            pre_norm(0)

            def stage(st):
                order = st.order
                att = st.att
                evs = st.ev()
                lag = 3 if att == "b" else 2

                def lin_chunk(s):
                    k, part = divmod(s, 4)
                    u = st.unit(k)
                    out = (0, 1, 0)[k]
                    if part == 0:
                        pe.wait_ge(lo_done, u["idx"] + 1)
                        if k == 2 or st.st > 0:
                            pe.wait_ge(kv_evac, evs + (0, -1, 1)[k])
                        elif k == 1 and st.kind == "c":
                            pe.wait_ge(fl_done, 1)
                    for kt in (2 * part, 2 * part + 1):
                        if st.st == 0 and k == 0 and st.i is None and (st.kind == "ab"):
                            pe.wait_ge(h_lo_done, 8 + kt + 1)
                        m = products(u, out, kt, h_hi[:, kt, :], h_lo[:, kt, :], kt == 0, kt == KT - 1)
                    if part == 3:
                        m.then_inc(unit_done, 1)

                def turn(step):
                    new, base = st.new, st.at("tr")
                    if st.st == 0 and st.kind == "c" and step == 5:
                        pe.wait_ge(fl_done, FL_DECAY - 2)
                    if step == 5:
                        pe.wait_ge(kv_evac, evs + 1)
                        src = kT[:, new, :]
                    elif step == 9:
                        pe.wait_ge(kv_evac, evs + 2)
                        src = vT[:, :]
                    n = tr_plan(st).index((step, "turn"))
                    wait_tr(base + n)
                    if step in (5, 9):
                        for t in range(QT):
                            m = nc.tensor.transpose(ps_t[:, t * P:(t + 1) * P], src[:, t * P:(t + 1) * P], ident[:])
                    else:
                        pe.wait_ge(cache_k[new], 16 * (st.same_new + 1))
                        nc.tensor.transpose(ps_t[0:DEC, 0:P], kT[:, new, SEQ:TOK], ident[:])
                        nc.tensor.transpose(ps_t[0:DEC, P:2 * P], vT[:, SEQ:TOK], ident[:])
                        for c in range(2):
                            m = nc.tensor.transpose(ps_t[:, (2 + c) * P:(3 + c) * P], ck_nat[:, new, c, :], ident[:])
                    m.then_inc(tr_ps, 1)

                def wait_tr(n):
                    pe.wait_ge(tr_out, n)

                def scores(j):
                    t, hh = order[j]
                    par, r = st.par, rows(order[j][0])
                    hs = slice(HD * hh, HD * hh + HD)
                    q0 = t * P if t < QT else SEQ
                    if j == 0:
                        pe.wait_ge(kv_evac, evs)
                        pe.wait_ge(tr_out, st.at("tr"))
                    if j >= 2:
                        pe.wait_ge(s_added, st.at("s") + j - 1)
                    lhs = qT[hs, par, q0:q0 + r]
                    if t == QT:
                        settle(pe)
                    if t < QT:
                        m = nc.tensor.matmul(ps_s[0:r, j % 2, 0:keys(t)], lhs, kT[hs, par, 0:keys(t)],
                                             start=True, stop=True)
                    else:
                        nc.tensor.matmul(ps_s[0:r, j % 2, 0:PAST], lhs, ckT[hs, par, :], start=True, stop=True)
                        m = nc.tensor.matmul(ps_s[0:r, j % 2, PAST:PAST + DEC], lhs, kT[hs, par, SEQ:TOK],
                                             start=True, stop=True)
                    m.then_inc(s_ps, 1)

                def transpose_probs(j, q):
                    t = order[j][0]
                    slot = (j - 1 if att == "b" else j) % PSLOTS
                    if att == "b":
                        pe.wait_ge(comb_done, st.at("comb") + q + 1)
                    else:
                        pe.wait_ge(exp_done, st.at("s") + j + 1)
                    wait_tr(st.at("tr") + tr_plan(st).index((j + lag, "probs")))
                    if t == QT:
                        settle(pe)
                    if t < QT:
                        for b in range(t + 1):
                            m = nc.tensor.transpose(ps_t[:, b * P:(b + 1) * P], probs[:, slot, b * P:(b + 1) * P], ident[:])
                    else:
                        for b in range(2):
                            nc.tensor.transpose(ps_t[:, b * P:b * P + DEC], probs[0:DEC, slot, b * P:(b + 1) * P],
                                                ident[0:DEC, 0:DEC])
                        m = nc.tensor.transpose(ps_t[0:DEC, 2 * P:2 * P + DEC], probs[0:DEC, slot, PAST:PAST + DEC],
                                                ident[0:DEC, 0:DEC])
                    m.then_inc(tr_ps, 1)

                def values(j, q):
                    t, hh = order[j]
                    r, par = rows(t), st.par
                    cols = slice(0, P) if att == "b" else slice(HD * hh, HD * hh + HD)
                    width = P if att == "b" else HD
                    pe.wait_ge(tr_out, st.at("tr") + tr_plan(st).index((j + lag, "probs")) + 1)
                    if q >= 1:
                        pe.wait_ge(o_read, st.at("pv") + q)
                    if att != "b" and j >= 2:
                        pe.wait_ge(o_lo_done, st.at("ot") + j // 2)
                    if t == QT:
                        pe.wait_ge(cache_v[par], 16 * (st.same_att + 1))
                    out = ps_o[0:r, (q % 2) * P:(q % 2) * P + width]
                    n = t + 1 if t < QT else 3
                    for b in range(n):
                        if t < QT:
                            lhs, rhs = probsT[:, q % 2, b, :], v_nat[:, par, b, cols]
                        elif b < 2:
                            lhs, rhs = probsT[:, q % 2, b, 0:DEC], cv_nat[:, par, b, cols]
                        else:
                            lhs, rhs = probsT[0:DEC, q % 2, b, 0:DEC], v_nat[0:DEC, par, QT, cols]
                        m = nc.tensor.matmul(out, lhs, rhs, start=b == 0, stop=b == n - 1)
                    m.then_inc(pv_done, 1)

                def turn_out(q):
                    t = order[2 * q][0]
                    r = rows(t)
                    pe.wait_ge(o_read, st.at("pv") + 2 * q + 2)
                    settle(pe)
                    nc.tensor.transpose(ps_o[:, (2 + q % 2) * P:(2 + q % 2) * P + r], o_nat[0:r, q % 2, :],
                                        ident[0:r, 0:r]).then_inc(ot_ps, 1)

                for s in range(STEPS + 2):
                    j = s - lag - 2
                    if att in ("a", "c") and 0 <= j < 10 and j % 2:
                        turn_out(j // 2)
                    if st.new is not None and s < LIN_STEPS:
                        lin_chunk(s)
                    if st.new is not None and s in (5, 9, 12):
                        turn(s)
                    if att is None:
                        continue
                    j = s - lag
                    if 0 <= j < 10 and (att != "b" or j % 2):
                        transpose_probs(j, j // 2 if att == "b" else j)
                    j = s - lag - 1
                    if 0 <= j < 10 and (att != "b" or j % 2):
                        values(j, j // 2 if att == "b" else j)
                    if s < 10:
                        scores(s)

            for j, kind in enumerate(KIND):
                if kind == "ffn":
                    np_ = 8 * j

                    def gu(i, j=j, first=False):
                        for k in range(4):
                            f = 2 * i + k // 2
                            u = unit_at(ws, f"gu{j}", k, i, 4, FT // 2)
                            base = FT * ffn_index(j)
                            pe.wait_ge(gate_read if k % 2 == 0 else prod_done, base + f)
                            unit(u, k % 2, KT, h_hi, h_lo, gradual=8 * j if first and k == 0 else None)
                    gu(0, first=True)
                    with pe.Fori(1, FT // 2) as i:
                        gu(i)
                    if j == 0:
                        ada("ada_gate0", 8, 0)
                        ada("ada_in1", 16, 8)
                    pe.wait_ge(act_lo_done, FT * (ffn_index(j) + 1) - 0)

                    def down(i, j=j):
                        for k in range(4):
                            m = 2 * i + k // 2
                            if k % 2 == 0:
                                pe.wait_ge(y_copied, 1 + 8 * j + m - 1)
                            unit(unit_at(ws, f"out{j}", k, i, 4, KT // 2), k // 2, DK, act_hi, act_lo,
                                 k0=DK * (k % 2), first=k % 2 == 0, last=k % 2 == 1)
                    loop(pe, KT // 2, down)
                else:
                    if kind == "c":
                        unit(unit_at(ws, "forget", 0), 1, KT, h_hi, h_lo, gradual=8 * j)
                        pe.wait_ge(fl_in, 32)
                        for t in range(2):
                            m = nc.tensor.transpose(ps_t[0:16, t * P:(t + 1) * P], clf_nat[:, t, :], ident[:])
                        m.then_inc(fl_ps, 1)

                    def turn_forget():
                        pe.wait_ge(fl_done, FL_DECAY)
                        for t in range(QT + 1):
                            m = nc.tensor.transpose(ps_s[0:rows(t), 0, 16 * t:16 * t + 16],
                                                    logf[:, t * P:t * P + rows(t)], ident[0:16, 0:16])
                        m.then_inc(fl_ps, 1)
                        for t in range(QT + 1):
                            t0 = t * P if t < QT else SEQ + PAST
                            m = nc.tensor.transpose(ps_s[0:rows(t), 1, 16 * t:16 * t + 16],
                                                    decay[:, t0:t0 + rows(t)], ident[0:16, 0:16])
                        m.then_inc(fl_ps, 1)
                        pe.wait_ge(fl_act, 6)
                    stages(pe, kind, stage, turn_forget if kind == "c" else None)
                    if kind == "ab":
                        for hd in range(4):
                            pe.wait_ge(b_scaled, hd + 1)
                            if hd >= 1:
                                pe.wait_ge(o_lo_done, 20 + 2 * hd)
                            for t in range(QT):
                                m = nc.tensor.transpose(ps_s[:, 0, t * P:(t + 1) * P], b_nat[:, hd, t, :], ident[:])
                            m.then_inc(ot_ps, 1)
                            nc.tensor.transpose(ps_s[:, 1, 0:DEC], b_nat[0:DEC, hd, QT, :],
                                                ident[0:DEC, 0:DEC]).then_inc(ot_ps, 1)
                    n_ot = off["c"]["ot"] if kind == "ab" else off["c"]["ot"] + 40
                    pe.wait_ge(o_lo_done, n_ot)
                    for m in range(KT):
                        pe.wait_ge(y_copied, 1 + 8 * j + m - 1)
                        unit(unit_at(ws, f"out{j}", m), m % 2, KT, o_hi, o_lo)
                post_norm(j)
                if j + 1 < NSUB:
                    if j == 0:
                        pe.wait_ge(rstd_done, 2)
                    ada(f"ada_gate{j + 1}", 8, 0)
                    pe.wait_ge(std_done, 2 * j + 2)
                    pre_norm(j + 1)
                if j + 2 < NSUB:
                    ada(f"ada_in{j + 2}", 16, 8)

            pe.wait_ge(x_ready, 8 * (NSUB + 1))
            for t in range(QT + 1):
                for a in range(2):
                    n = 2 * t + a
                    if n >= 4:
                        pe.wait_ge(nat_out, 2 * (n // 2) - 2)
                    for k in range(4):
                        m = nc.tensor.transpose(lin[0:rows(t), n % 4, k * P:(k + 1) * P],
                                                x[:, 4 * a + k, t * P:t * P + rows(t)], ident[:])
                    m.then_inc(nat_ps, 1)

        @block.scalar
        def _(act):
            def w_split(u, tiles):
                act.wait_ge(raw_in[u["slot"]], u["landed"])
                act.wait_ge(unit_done, u["hl_free"])
                nc.scalar.activation(w_hi[:, u["hl"], 0:tiles, :], raw[:, u["slot"], 0:tiles, :], ACT.Copy)\
                    .then_inc(hi_done, 1)

            def std(n):
                act.wait_ge(mean_done, n)
                if n > 1:
                    act.wait_ge(rstd_done, n - 1)
                nc.scalar.activation(two(rstd[:]), ps_s[:, :, 0:HALF], ACT.Sqrt, bias=eps[:, 0:1]).then_inc(std_done, 1)

            def pre_norm(j):
                for m in range(KT):
                    act.wait_ge(x_ready, 8 * j + m + 1)
                    if m >= 2:
                        act.wait_ge(sq_used, 7 * j + m - 1)
                    nc.scalar.activation(work[:, m % 2, :], x[:, m, :], ACT.Square).then_inc(sq_done, 1)
                std(2 * j + 1)
                for m in range(KT):
                    act.wait_ge(t_done, 8 * j + m + 1)
                    for g, c in ((0, slice(0, SEQ)), (1, slice(SEQ, TOK))):
                        i = nc.scalar.activation(h_hi[:, m, c], prod[:, m % 2, c], ACT.Identity,
                                                 bias=co_shift[:, m, g:g + 1])
                    i.then_inc(h_hi_done, 1)

            def square_out(j, m, a):
                act.wait_ge(y_copied, 1 + 8 * j + m + 1)
                act.wait_ge(sq_added, 9 * j + 1 + m - 1)
                nc.scalar.activation(work[:, a, :], y[:, m, :], ACT.Square).then_inc(sq_done, 1)

            act.wait_ge(const_tr, 1)
            nc.scalar.activation(silu_c[:].rearrange("p g k -> p (g k)"), ps_s[:, 0, 0:16], ACT.Silu)\
                .then_inc(silu_c_done, 1)
            act.wait_ge(lam_done, 2)
            nc.scalar.activation(lam[:, 2:4], lam[:, 0:2], ACT.Exp).then_inc(lam_done, 1)
            act.wait_ge(pool_const, 4)
            pre_norm(0)
            act.wait_ge(rel_dram, 32)

            def stage(st):
                order, att = st.order, st.att
                evs = st.ev()
                plan_t = tr_plan(st)

                def evac(k):
                    u = st.unit(k)
                    act.wait_ge(unit_done, u["n"] + 1)
                    dst = (kT[:, st.new, :], vT[:], qT[:, st.new, :])[k]
                    nc.scalar.activation(two(dst), pair((0, 1, 0)[k]), ACT.Copy,
                                         scale=HD ** -0.5 if k == 2 else 1.0).then_inc(kv_evac, 1)

                def empty_turn(step):
                    n = plan_t.index((step, "turn"))
                    act.wait_ge(tr_ps, st.at("tr") + n + 1)
                    if step in (5, 9):
                        if step == 5:
                            act.wait_ge(kv_stored[st.new], 64 * st.same_new)
                        dst = (k_nat if step == 5 else v_nat)[:, st.new, 0:QT, :].rearrange("p t n -> p (t n)")
                        nc.scalar.activation(dst, ps_t[:, :], ACT.Copy).then_inc(tr_out, 1)
                    else:
                        nc.scalar.activation(k_nat[0:DEC, st.new, QT, :], ps_t[0:DEC, 0:P], ACT.Copy)
                        nc.scalar.activation(v_nat[0:DEC, st.new, QT, :], ps_t[0:DEC, P:2 * P], ACT.Copy)
                        nc.scalar.activation(ckT[:, st.new, :], ps_t[:, 2 * P:4 * P], ACT.Copy).then_inc(tr_out, 1)

                def empty_probs(j, q, lag):
                    t = order[j][0]
                    act.wait_ge(tr_ps, st.at("tr") + plan_t.index((j + lag, "probs")) + 1)
                    if q >= 2:
                        act.wait_ge(pv_done, st.at("pv") + q - 1)
                    if t < QT:
                        nc.scalar.activation(probsT[:, q % 2, 0:t + 1, :].rearrange("p b n -> p (b n)"),
                                             ps_t[:, 0:(t + 1) * P], ACT.Copy).then_inc(tr_out, 1)
                    else:
                        nc.scalar.activation(probsT[:, q % 2, 0:2, 0:DEC],
                                             ps_t[:, 0:2 * P].rearrange("p (b n) -> p b n", b=2)[:, :, 0:DEC], ACT.Copy)
                        nc.scalar.activation(probsT[0:DEC, q % 2, 2, 0:DEC], ps_t[0:DEC, 2 * P:2 * P + DEC], ACT.Copy)\
                            .then_inc(tr_out, 1)

                def exps(j):
                    t = order[j][0]
                    r, n = rows(t), keys(t)
                    act.wait_ge(s_maxed, st.at("s") + j + 1)
                    nc.scalar.activation(probs[0:r, j % PSLOTS, 0:n], probs[0:r, j % PSLOTS, 0:n], ACT.Exp,
                                         bias=neg_max[0:r, j:j + 1], accum_out=row_sum[0:r, j:j + 1])\
                        .then_inc(exp_done, 1)

                def out_hi(q):
                    t = order[2 * q][0]
                    r = rows(t)
                    act.wait_ge(ot_ps, st.at("ot") + q + 1)
                    nc.scalar.activation(o_hi[:, st.tile_of(-1), t * P:t * P + r],
                                         ps_o[:, (2 + q % 2) * P:(2 + q % 2) * P + r], ACT.Copy).then_inc(o_hi_done, 1)

                def b_square(q):
                    t = order[2 * q][0]
                    r = rows(t)
                    act.wait_ge(o_read, st.at("pv") + q + 1)
                    act.wait_ge(b_sq_done, 5 * st.tile_of(-1) + q)
                    nc.scalar.activation(o_nat[0:r, 0, :], b_nat[0:r, st.tile_of(-1), t, :], ACT.Square,
                                         accum_out=b_sq[0:r, st.tile_of(-1), t:t + 1]).then_inc(b_sq_done, 1)

                lag = 3 if att == "b" else 2
                for s in range(STEPS + 2):
                    j = s - lag - 2
                    if att in ("a", "c") and 0 <= j < 10 and j % 2:
                        out_hi(j // 2)
                    if st.new is not None:
                        if s in (4, 8, 12):
                            evac(s // 4 - 1)
                        if s in (0, 4):
                            w_split(st.unit(s // 4 + 1), KT)
                        if s == 8:
                            nxt = next_unit(st)
                            if nxt is not None:
                                w_split(nxt, KT)
                        if s in (5, 9, 12):
                            empty_turn(s)
                    if att is None:
                        continue
                    j = s - lag
                    if 0 <= j < 10 and (att != "b" or j % 2):
                        empty_probs(j, j // 2 if att == "b" else j, lag)
                    j = s - lag - 2
                    if 0 <= j < 10 and j % 2 and att == "b":
                        b_square(j // 2)
                    if s < 10:
                        exps(s)

            for j, kind in enumerate(KIND):
                if kind == "ffn":
                    w_split(unit_at(ws, f"gu{j}", 0), KT)
                    base = FT * ffn_index(j)

                    if j in (2, 5):
                        for par in range(2):
                            act.wait_ge(kv_stored[par], 256 * (1 + (j == 5)))
                    if j == 5:
                        act.wait_ge(lf_stored, 32)

                    def gu(i, last=False, j=j, base=base):
                        for a in range(2):
                            f = 2 * i + a
                            w_split(unit_at(ws, f"gu{j}", 2 * a + 1, i, 4, FT // 2 - 1), KT)
                            act.wait_ge(unit_done, unit_at(ws, f"gu{j}", 2 * a, i, 4, FT // 2 - 1)["n"] + 1)
                            nc.scalar.activation(two(work[:, a, :]), pair(0), ACT.Silu).then_inc(gate_read, 1)
                            if not (last and a == 1):
                                w_split(next_gu(j, i, a), KT)
                            elif j > 0:
                                w_split(unit_at(ws, f"out{j}", 0), DK)
                            act.wait_ge(prod_done, base + f + 1)
                            nc.scalar.activation(act_hi[:, f, :], prod[:, a, :], ACT.Copy).then_inc(act_hi_done, 1)
                    with act.Fori(0, FT // 2 - 1) as i:
                        gu(i)
                    gu(FT // 2 - 1, last=True)
                    if j == 0:
                        w_split(unit_at(ws, f"out{j}", 0), DK)

                    def down(i, last=False, j=j):
                        for a in range(2):
                            w_split(unit_at(ws, f"out{j}", 2 * a + 1, i, 4, KT // 2 - 1), DK)
                            if not (last and a == 1):
                                w_split(next_down(j, i, a), DK)
                            square_out(j, 2 * i + a, a)
                    with act.Fori(0, KT // 2 - 1) as i:
                        down(i)
                    down(KT // 2 - 1, last=True)
                else:
                    if kind == "c":
                        w_split(unit_at(ws, "forget", 0), KT)
                        w_split(unit_at(ws, "qkv4", 0), KT)
                        act.wait_ge(fl_done, 2)
                        nc.scalar.activation(e_t[:], e_t[:], ACT.Exp).then_inc(fl_act, 1)
                        act.wait_ge(fl_done, 3)
                        nc.scalar.activation(l_t[:], u_t[:], ACT.Ln).then_inc(fl_act, 1)
                    else:
                        w_split(unit_at(ws, "qkv1", 0), KT)

                    def empty_forget():
                        for n, (dst, k) in enumerate(((lf_nat, 0), (dqT, 1))):
                            act.wait_ge(fl_ps, 2 + n)
                            nc.scalar.activation(dst[:, 0:QT, :], ps_s[:, k, 0:64].rearrange("p (t h) -> p t h", h=16),
                                                 ACT.Copy).then_inc(fl_act, 1)
                            nc.scalar.activation(dst[0:DEC, QT, :], ps_s[0:DEC, k, 64:80], ACT.Copy).then_inc(fl_act, 1)
                    stages(act, kind, stage, empty_forget if kind == "c" else None)
                    if kind == "ab":
                        act.wait_ge(b_sq_done, 20)
                        act.wait_ge(b_inv, 1)
                        nc.scalar.activation(b_sq[:].rearrange("p h t -> p (h t)"), b_sq[:].rearrange("p h t -> p (h t)"),
                                             ACT.Sqrt, scale=1.0 / P, bias=eps[:, 0:1]).then_inc(b_std, 1)
                        for hd in range(4):
                            act.wait_ge(ot_ps, 20 + 2 * hd + 1)
                            nc.scalar.activation(o_hi[:, 4 + hd, 0:SEQ], ps_s[:, 0, :], ACT.Copy).then_inc(o_hi_done, 1)
                            act.wait_ge(ot_ps, 20 + 2 * hd + 2)
                            nc.scalar.activation(o_hi[:, 4 + hd, SEQ:TOK], ps_s[:, 1, 0:DEC], ACT.Copy)\
                                .then_inc(o_hi_done, 1)
                    w_split(unit_at(ws, f"out{j}", 0), KT)
                    for m in range(KT):
                        if m + 1 < KT:
                            w_split(unit_at(ws, f"out{j}", m + 1), KT)
                        square_out(j, m, m % 2)
                std(2 * j + 2)
                if j + 1 < NSUB:
                    pre_norm(j + 1)
            for n in range(0, 2 * QT + 2, 2):
                r = rows(n // 2)
                act.wait_ge(nat_ps, n + 1)
                nc.scalar.activation(x_nat[0:r, n // 2, 0:SEQ], lin[0:r, n % 4, :], ACT.Copy).then_inc(nat_a, 1)

        @block.vector
        def _(dve):
            def w_split(u, tiles):
                dve.wait_ge(hi_done, u["idx"] + 1)
                nc.vector.tensor_tensor(w_lo[:, u["hl"], 0:tiles, :], raw[:, u["slot"], 0:tiles, :],
                                        w_hi[:, u["hl"], 0:tiles, :].bitcast(F32), ALU.subtract).then_inc(lo_done, 1)

            coef_n = [0]

            def step(ins):
                ins.then_inc(coef, 1)
                coef_n[0] += 1
                dve.wait_ge(coef, coef_n[0])

            def bias(j, c, n):
                f0 = (3 * (j % 3) + c) * KT
                return ada_b[:, j // 3, f0:f0 + n].rearrange("p (k o) -> p k o", o=1).broadcast_to([P, n, 2])

            def gain(a, j):
                return norms[:, a, j, :].rearrange("p (k o) -> p k o", o=1).broadcast_to([P, KT, 2])

            def coef_in(j):
                dve.wait_ge(unit_done, ws.first[f"ada_in{j}"] + 16)
                dve.wait_ge(h_hi_done, 8 * j)
                step(nc.vector.tensor_tensor(co_tmp[:], mod_ps[:, 8:24, :], bias(j, 0, 16), ALU.add))
                step(nc.vector.tensor_copy(co_shift[:], co_tmp[:, 0:KT, :]))
                step(nc.vector.scalar_tensor_tensor(co_scale[:], co_tmp[:, KT:2 * KT, :], 1.0, gain(0, j), ALU.add, ALU.mult))

            def coef_gate(j):
                dve.wait_ge(unit_done, ws.first[f"ada_gate{j}"] + 8)
                step(nc.vector.tensor_tensor(co_tmp[:, 0:KT, :], mod_ps[:, 0:8, :], bias(j, 2, 8), ALU.add))
                step(nc.vector.scalar_tensor_tensor(co_gate[:], co_tmp[:, 0:KT, :], 1.0, gain(1, j), ALU.add, ALU.mult))
                if KIND[j] == "ffn":
                    step(nc.vector.tensor_scalar(co_gate[:], co_gate[:], 0.5, None, ALU.mult))

            groups = ((0, slice(0, SEQ)), (1, slice(SEQ, TOK)))

            def inverse(n):
                dve.wait_ge(std_done, n)
                nc.vector.reciprocal(rstd[:], rstd[:]).then_inc(rstd_done, 1)
                dve.wait_ge(rstd_done, n)

            def pre_norm(j):
                inverse(2 * j + 1)
                for m in range(KT + 1):
                    if m < KT:
                        if m >= 2:
                            dve.wait_ge(h_lo_done, 8 * j + m - 1)
                        for g, c in groups:
                            i = nc.vector.scalar_tensor_tensor(prod[:, m % 2, c], x[:, m, c], co_scale[:, m, g:g + 1],
                                                               rstd[:, c], ALU.mult, ALU.mult)
                        i.then_inc(t_done, 1)
                    if m > 0:
                        dve.wait_ge(h_hi_done, 8 * j + m)
                        dve.wait_ge(t_done, 8 * j + m)
                        for g, c in groups:
                            i = nc.vector.scalar_tensor_tensor(h_lo[:, m - 1, c], prod[:, (m - 1) % 2, c],
                                                               co_shift[:, m - 1, g:g + 1],
                                                               h_hi[:, m - 1, c].bitcast(F32), ALU.add, ALU.subtract)
                        i.then_inc(h_lo_done, 1)

            def post_norm(j):
                inverse(2 * j + 2)
                for m in range(KT + 1):
                    if m < KT:
                        nc.vector.tensor_tensor(y[:, m, :], y[:, m, :], rstd[:], ALU.mult).then_inc(y_norm, 1)
                    if m > 0:
                        dve.wait_ge(y_norm, 8 * j + m)
                        for g, c in groups:
                            i = nc.vector.scalar_tensor_tensor(x[:, m - 1, c], y[:, m - 1, c], co_gate[:, m - 1, g:g + 1],
                                                               x[:, m - 1, c], ALU.mult, ALU.add)
                        i.then_inc(x_ready, 1)

            def take_out(j, m, a):
                dve.wait_ge(unit_done, take_out.n + 1)
                nc.vector.tensor_copy(two(y[:, m, :]), pair(a)).then_inc(y_copied, 1)
                dve.wait_ge(sq_done, sq_base[j] + m + 1)
                dve.wait_ge(sq_added, 9 * j + 1 + m)
                nc.vector.tensor_tensor(sq_sum[:], sq_sum[:], work[:, a, :], ALU.add).then_inc(sq_added, 1)

            dve.wait_ge(silu_c_done, 1)
            nc.vector.tensor_copy(norms[:].rearrange("p a s k -> p (a s k)"), ps_s[:, 0, 16:112]).then_inc(vec_const, 1)
            dve.wait_ge(const_tr, 2)
            nc.vector.tensor_copy(ada_b[:].rearrange("p l f -> p (l f)"), ps_s[:, 1, 0:144]).then_inc(vec_const, 1)
            dve.wait_ge(vec_const, 2)
            for m in range(KT):
                dve.wait_ge(xt_ps, m + 1)
                nc.vector.tensor_copy(x[:, m, 0:SEQ], lin[:, 2 * (m % 2), :])
                nc.vector.tensor_copy(x[:, m, SEQ:TOK], lin[:, 2 * (m % 2) + 1, 0:DEC]).then_inc(x_ready, 1)
            dve.wait_ge(lam_landed, 32)
            lam_p = prod[:, 0, 0:2 * HD].rearrange("p (a d) -> p a d", a=2)
            nc.vector.tensor_tensor(lam_p, lam_in[:, 0:4:2, :], lam_in[:, 1:4:2, :], ALU.mult).then_inc(lam_done, 1)
            dve.wait_ge(lam_done, 1)
            nc.vector.tensor_reduce(lam[:, 0:2], lam_p, AX.X, ALU.add).then_inc(lam_done, 1)
            dve.wait_ge(lam_done, 3)
            step(nc.vector.tensor_tensor(lam[:, 4:5], lam[:, 3:4], lam[:, 2:3], ALU.subtract))
            step(nc.vector.tensor_scalar(lam[:, 7:8], lam[:, 4:5], -LAM_INIT, None, ALU.add))
            step(nc.vector.tensor_scalar(sub_g[:], sub_g[:], 1.0 - LAM_INIT, None, ALU.mult))
            dve.wait_ge(rel_dram, 16)
            nc.vector.tensor_copy(rel_rev[:, P - 1:3 * P], rel_in[:, ::-1]).then_inc(rel_done, 1)
            nc.vector.tensor_copy(rel_rev[:, 0:P - 1], rel_in[:, 2 * REL:2 * REL + 1].broadcast_to([8, P - 1]))\
                .then_inc(rel_done, 1)
            coef_in(0)
            pre_norm(0)

            def stage(st):
                order, att = st.order, st.att
                lag = 3 if att == "b" else 2

                def add_bias(j):
                    t, hh = order[j]
                    r, n = rows(t), keys(t)
                    dst = probs[0:r, j % PSLOTS, :]
                    src = ps_s[0:r, j % 2, :]
                    dve.wait_ge(s_ps, st.at("s") + j + 1)
                    if j >= PSLOTS and (att != "b" or j % 2 == 0):
                        at = j - PSLOTS + lag + (att == "b")
                        dve.wait_ge(tr_ps, st.at("tr") + tr_plan(st).index((at, "probs")) + 1)
                    if att == "a":
                        hd = 2 * st.tile_of(-1) + hh
                        near = 2 * P if 0 < t < QT else P if t == 0 else P + DEC
                        if n > near:
                            nc.vector.tensor_scalar(dst[:, 0:n - near], src[:, 0:n - near], rel_bias[0:r, hd, 0:1],
                                                    None, ALU.add)
                        lo = 0 if t else P
                        i = nc.vector.tensor_tensor(dst[:, n - near:n], src[:, n - near:n],
                                                    rel_bias[0:r, hd, lo:lo + near], ALU.add)
                    elif att == "b":
                        d0 = SEQ - P - (t * P if t < QT else PAST)
                        i = nc.vector.scalar_tensor_tensor(dst[:, 0:n], dist[0:r, d0:d0 + n],
                                                           neg_slope[0:r, bass.ds(st.tile_of(-1), 1)],
                                                           src[:, 0:n], ALU.mult, ALU.add)
                    else:
                        hd = 2 * st.tile_of(-1) + hh
                        k0 = 0 if t < QT else SEQ
                        if j == 0:
                            dve.wait_ge(dk_in[st.par], 32 * (st.same_att - 3))
                        i = nc.vector.scalar_tensor_tensor(dst[:, 0:n], src[:, 0:n], dqT[0:r, t, bass.ds(hd, 1)],
                                                           dk_b[0:r, st.par, hh, k0:k0 + n], ALU.add, ALU.subtract)
                    i.then_inc(s_added, 1)
                    dve.wait_ge(s_added, st.at("s") + j + 1)
                    if att == "c":
                        nc.vector.tensor_tensor(dst[:, n - r:n], dst[:, n - r:n], causal[0:r, 0:r], ALU.add)\
                            .then_inc(masked, 1)
                        dve.wait_ge(masked, st.at("s") - off["c"]["s"] + j + 1)
                    nc.vector.tensor_reduce(neg_max[0:r, j:j + 1], dst[:, 0:n], AX.X, ALU.max, negate=True)\
                        .then_inc(s_maxed, 1)

                def invert(j):
                    r = rows(order[j][0])
                    dve.wait_ge(exp_done, st.at("s") + j + 1)
                    nc.vector.reciprocal(row_inv[0:r, j:j + 1], row_sum[0:r, j:j + 1]).then_inc(inv_done, 1)

                def combine(q):
                    t = order[2 * q][0]
                    r, n = rows(t), keys(t)
                    a, b = (2 * q) % PSLOTS, (2 * q + 1) % PSLOTS
                    dve.wait_ge(inv_done, st.at("s") + 2 * q + 2)
                    nc.vector.tensor_scalar(probs[0:r, b, 0:n], probs[0:r, b, 0:n], row_inv[0:r, 2 * q + 1:2 * q + 2],
                                            lam[0:r, 7:8], ALU.mult, ALU.mult).then_inc(comb_half, 1)
                    dve.wait_ge(comb_half, st.at("comb") + q + 1)
                    nc.vector.scalar_tensor_tensor(probs[0:r, a, 0:n], probs[0:r, a, 0:n], row_inv[0:r, 2 * q:2 * q + 1],
                                                   probs[0:r, b, 0:n], ALU.mult, ALU.add).then_inc(comb_done, 1)

                def take(j, q):
                    t, hh = order[j]
                    r = rows(t)
                    dve.wait_ge(pv_done, st.at("pv") + q + 1)
                    if att == "b":
                        nc.vector.tensor_copy(b_nat[0:r, st.tile_of(-1), t, :], ps_o[0:r, (q % 2) * P:(q % 2) * P + P])\
                            .then_inc(o_read, 1)
                        return
                    nq = q // 2
                    if nq >= 2:
                        dve.wait_ge(ot_ps, st.at("ot") + nq - 1)
                    dve.wait_ge(inv_done, st.at("s") + j + 1)
                    nc.vector.tensor_scalar(o_nat[0:r, nq % 2, HD * hh:HD * hh + HD],
                                            ps_o[0:r, (q % 2) * P:(q % 2) * P + HD], row_inv[0:r, j:j + 1],
                                            None, ALU.mult).then_inc(o_read, 1)

                def out_lo(q):
                    t = order[2 * q][0]
                    r = rows(t)
                    dve.wait_ge(o_hi_done, st.at("ot") + q + 1)
                    c = slice(t * P, t * P + r)
                    nc.vector.tensor_tensor(o_lo[:, st.tile_of(-1), c], ps_o[:, (2 + q % 2) * P:(2 + q % 2) * P + r],
                                            o_hi[:, st.tile_of(-1), c].bitcast(F32), ALU.subtract).then_inc(o_lo_done, 1)

                lag = 3 if att == "b" else 2
                for s in range(STEPS + 2):
                    if st.new is not None:
                        if s in (0, 4):
                            w_split(st.unit(s // 4 + 1), KT)
                        if s == 8:
                            nxt = next_unit(st)
                            if nxt is not None:
                                w_split(nxt, KT)
                    if att is None:
                        continue
                    j = s - 2
                    if 0 <= j < 10:
                        invert(j)
                        if att == "b" and j % 2:
                            combine(j // 2)
                    j = s - lag - 2
                    if att != "b" and 0 <= j < 10 and j % 2:
                        out_lo(j // 2)
                    j = s - lag - 1
                    if 0 <= j < 10 and (att != "b" or j % 2):
                        take(j, j // 2 if att == "b" else j)
                    if s < 10:
                        add_bias(s)

            def forget_gate():
                count = [0]

                def fl(ins, wait=True):
                    count[0] += 1
                    ins.then_inc(fl_done, 1)
                    if wait:
                        dve.wait_ge(fl_done, count[0])
                dve.wait_ge(fl_in, 32)
                dve.wait_ge(unit_done, unit_at(ws, "forget", 0)["n"] + 1)
                fl(nc.vector.tensor_scalar(two(z_t[:]), pair(1)[0:16], bf_col[:, 0:1], None, ALU.add))
                fl(nc.vector.scalar_tensor_tensor(e_t[:], z_t[:], -1.0, z_t[:], ALU.mult, ALU.min))
                dve.wait_ge(fl_act, 1)
                fl(nc.vector.tensor_scalar(u_t[:], e_t[:], 1.0, None, ALU.add))
                fl(nc.vector.scalar_tensor_tensor(logf[:], u_t[:], -1.0, e_t[:], ALU.add, ALU.subtract))
                dve.wait_ge(fl_act, 2)
                fl(nc.vector.reciprocal(u_t[:], u_t[:]))
                fl(nc.vector.tensor_tensor(logf[:], logf[:], u_t[:], ALU.mult))
                fl(nc.vector.tensor_tensor(l_t[:], l_t[:], logf[:], ALU.subtract))
                fl(nc.vector.scalar_tensor_tensor(logf[:], z_t[:], 0.0, l_t[:], ALU.min, ALU.subtract))
                fl(nc.vector.memset(ones16[:], 1.0))
                fl(nc.vector.tensor_tensor_scan(decay[:, 0:SEQ], ones16[:, 0:SEQ], logf[:, 0:SEQ], 0.0,
                                                ALU.mult, ALU.add), False)
                fl(nc.vector.tensor_tensor_scan(decay[:, SEQ + PAST:], ones16[:, 0:DEC], logf[:, SEQ:TOK], 0.0,
                                                ALU.mult, ALU.add), False)
                dve.wait_ge(fl_ps, 1)
                fl(nc.vector.tensor_tensor_scan(decay[:, SEQ:SEQ + PAST], ones16[:, 0:PAST], ps_t[0:16, 0:PAST], 0.0,
                                                ALU.mult, ALU.add))
                fl(nc.vector.tensor_copy(l_t[:, 0:1], decay[:, SEQ + PAST - 1:SEQ + PAST]))
                fl(nc.vector.tensor_scalar(decay[:, SEQ:SEQ + PAST], decay[:, SEQ:SEQ + PAST], l_t[:, 0:1], None,
                                           ALU.subtract))
                assert count[0] == FL_DECAY

            def coefs_after(j):
                if j + 1 < NSUB:
                    coef_in(j + 1)
                coef_gate(j)

            for j, kind in enumerate(KIND):
                if kind == "ffn":
                    w_split(unit_at(ws, f"gu{j}", 0), KT)
                    if j > 0:
                        coefs_after(j)
                    base = FT * ffn_index(j)

                    def gu(i, last=False, j=j, base=base):
                        for a in range(2):
                            f = 2 * i + a
                            u = unit_at(ws, f"gu{j}", 2 * a + 1, i, 4, FT // 2 - 1)
                            w_split(u, KT)
                            if not (last and a == 1):
                                w_split(next_gu(j, i, a), KT)
                            elif j > 0:
                                w_split(unit_at(ws, f"out{j}", 0), DK)
                            dve.wait_ge(gate_read, base + f + 1)
                            dve.wait_ge(unit_done, u["n"] + 1)
                            dve.wait_ge(act_lo_done, base + f)
                            nc.vector.tensor_tensor(two(prod[:, a, :]), two(work[:, a, :]), pair(1), ALU.mult)\
                                .then_inc(prod_done, 1)
                            dve.wait_ge(act_hi_done, base + f + 1)
                            dve.wait_ge(prod_done, base + f + 1)
                            nc.vector.tensor_tensor(act_lo[:, f, :], prod[:, a, :], act_hi[:, f, :].bitcast(F32),
                                                    ALU.subtract).then_inc(act_lo_done, 1)
                    with dve.Fori(0, FT // 2 - 1) as i:
                        gu(i)
                    gu(FT // 2 - 1, last=True)
                    if j == 0:
                        w_split(unit_at(ws, f"out{j}", 0), DK)
                    nc.vector.memset(sq_sum[:], 0.0).then_inc(sq_added, 1)
                    if j == 0:
                        nc.vector.memset(co_tmp[:], 0.0).then_inc(y_copied, 1)

                    def down(i, last=False, j=j):
                        for a in range(2):
                            u = unit_at(ws, f"out{j}", 2 * a + 1, i, 4, KT // 2 - 1)
                            w_split(u, DK)
                            if not (last and a == 1):
                                w_split(next_down(j, i, a), DK)
                            take_out.n = u["n"]
                            take_out(j, 2 * i + a, a)
                    with dve.Fori(0, KT // 2 - 1) as i:
                        down(i)
                    down(KT // 2 - 1, last=True)
                    if j == 0:
                        coefs_after(0)
                else:
                    if kind == "ab":
                        w_split(unit_at(ws, "qkv1", 0), KT)
                        coefs_after(j)
                        dve.wait_ge(rel_loaded, 16 * 8)
                        dve.wait_ge(pool_const, 11)
                        step(nc.vector.memset(rel_bias[0:HD, :, 2 * P - HD:2 * P], NEG))
                        step(nc.vector.tensor_copy(dist[:], dist_i[:]))
                        step(nc.vector.scalar_tensor_tensor(dist[:], dist[:], -1.0, dist[:], ALU.mult, ALU.max))
                        step(nc.vector.memset(dist[0:HD, SEQ - HD:SEQ], 1e35))
                        nc.vector.memset(b_sq[:], 1.0).then_inc(b_inv, 1)
                        dve.wait_ge(b_inv, 1)
                    else:
                        w_split(unit_at(ws, "forget", 0), KT)
                        w_split(unit_at(ws, "qkv4", 0), KT)
                        coefs_after(j)
                        forget_gate()
                    stages(dve, kind, stage)
                    if kind == "ab":
                        dve.wait_ge(b_std, 1)
                        nc.vector.reciprocal(b_sq[:].rearrange("p h t -> p (h t)"), b_sq[:].rearrange("p h t -> p (h t)"))\
                            .then_inc(b_inv, 1)
                        dve.wait_ge(b_inv, 2)
                        for hd in range(5):
                            if hd < 4:
                                for t in range(QT + 1):
                                    r = rows(t)
                                    i = nc.vector.scalar_tensor_tensor(b_nat[0:r, hd, t, :], b_nat[0:r, hd, t, :],
                                                                       b_sq[0:r, hd, t:t + 1], sub_g[0:r, :],
                                                                       ALU.mult, ALU.mult)
                                i.then_inc(b_scaled, 1)
                            if hd > 0:
                                p = hd - 1
                                dve.wait_ge(o_hi_done, 20 + 2 * p + 1)
                                nc.vector.tensor_tensor(o_lo[:, 4 + p, 0:SEQ], ps_s[:, 0, :],
                                                        o_hi[:, 4 + p, 0:SEQ].bitcast(F32), ALU.subtract)\
                                    .then_inc(o_lo_done, 1)
                                dve.wait_ge(o_hi_done, 20 + 2 * p + 2)
                                nc.vector.tensor_tensor(o_lo[:, 4 + p, SEQ:TOK], ps_s[:, 1, 0:DEC],
                                                        o_hi[:, 4 + p, SEQ:TOK].bitcast(F32), ALU.subtract)\
                                    .then_inc(o_lo_done, 1)
                    w_split(unit_at(ws, f"out{j}", 0), KT)
                    nc.vector.memset(sq_sum[:], 0.0).then_inc(sq_added, 1)
                    for m in range(KT):
                        if m + 1 < KT:
                            w_split(unit_at(ws, f"out{j}", m + 1), KT)
                        take_out.n = unit_at(ws, f"out{j}", m)["n"]
                        take_out(j, m, m % 2)
                post_norm(j)
                if j + 1 < NSUB:
                    pre_norm(j + 1)
            for n in range(1, 2 * QT + 2, 2):
                r = rows(n // 2)
                dve.wait_ge(nat_ps, n + 1)
                dve.wait_ge(nat_a, n // 2 + 1)
                nc.vector.tensor_copy(x_nat[0:r, n // 2, SEQ:DM], lin[0:r, n % 4, :]).then_inc(nat_out, 2)


_INS = ["x_prompt", "x_sample", "c_prompt", "c_sample", "cache_a_k", "cache_a_v", "cache_b_k", "cache_b_v",
        "cache_c_k", "cache_c_v", "cache_c_logf", "w_ada", "b_ada", "norm_pre", "norm_post", "ffn_w_gate",
        "ffn_w_up", "ffn_w_down", "w_in_ab", "w_out_ab", "relpos_a", "lambda_b", "subln_b", "w_in_c", "b_f",
        "w_out_c"]
_OUTS = [(1, SEQ, DM), (1, DEC, DM),
         (1, 1, SEQ, 8, HD), (1, 1, SEQ, 8, HD), (1, 1, SEQ, 4, 2 * HD), (1, 1, SEQ, 4, 2 * HD),
         (1, 1, SEQ, 16, HD), (1, 1, SEQ, 16, HD), (1, 1, SEQ, 16),
         (1, 1, DEC, 8, HD), (1, 1, DEC, 8, HD), (1, 1, DEC, 4, 2 * HD), (1, 1, DEC, 4, 2 * HD),
         (1, 1, DEC, 16, HD), (1, 1, DEC, 16, HD), (1, 1, DEC, 16)]


def kernel(**inputs):
    import concourse.bacc as bacc
    from concourse.bass_utils import run_bass_kernel_spmd

    nc = bacc.Bacc("TRN2", target_bir_lowering=False, num_devices=1)
    arrays, ins = {}, []
    for name in _INS:
        a = np.ascontiguousarray(inputs[name])
        arrays[f"in_{name}"] = a
        ins.append(nc.dram_tensor(f"in_{name}", a.shape, mybir.dt.from_np(a.dtype), kind="ExternalInput").ap())
    outs = [nc.dram_tensor(f"out_{i}", shape, F32, kind="ExternalOutput").ap() for i, shape in enumerate(_OUTS)]
    program(nc, ins, outs)
    r = run_bass_kernel_spmd(nc, [arrays], core_ids=[0])
    return tuple(r.results[0][f"out_{i}"] for i in range(len(_OUTS)))
```

```python
from contextlib import ExitStack

import numpy as np

import concourse.bass as bass
from concourse import mybir

F32 = mybir.dt.float32
F32R = mybir.dt.float32r
I32 = mybir.dt.int32
ALU = mybir.AluOpType
ACT = mybir.ActivationFunctionType
AX = mybir.AxisListType

P = 128
DM = 1024
KT = DM // P
SEQ, DEC, PAST = 512, 32, 256
TOK = SEQ + DEC
HALF = TOK // 2
QT = SEQ // P
D_FF = 2816
FT = D_FF // P
DK = FT // 2
HD = 64
REL = 128
NSUB = 6
EPS = 1e-6
NEG = -1e30
LAM_INIT = 0.2
PSLOTS = 4
NRAW, NHL = 4, 2
KIND = ["ffn", "ab", "ffn", "ffn", "c", "ffn"]
JOB = 512
JOB_U = 4
JOBS = 2 * 9 * DM // JOB
FIRST_JOBS = 2 * DM // JOB
GU_TRIPS = {0: (11, 0), 2: (11, 0), 3: (9, 2), 5: (0, 11)}
GU_JOB0 = {0: 4, 2: 16, 3: 27, 5: 36}
TRIP = {True: ["gate0", "ada0", "up0", "ada1", "gate1", "ada2", "ada3", "up1"],
        False: ["gate0", "up0", "gate1", "up1"]}
FL_DECAY = 14
STEPS = 14
LIN_STEPS = 12


class Stream:

    def __init__(self):
        self.units = []
        self.used = [0] * NRAW
        self.last = [None] * NRAW
        self.split = 0
        self.first = {}

    def add(self, name, n, split=True, ring=NRAW):
        self.first[name] = len(self.units)
        for k in range(n):
            slot = k % ring if ring != NRAW else (self.start + k) % NRAW
            prev = self.last[slot]
            self.used[slot] += 1
            self.last[slot] = len(self.units)
            self.units.append((slot, self.used[slot], self.split if split else None, prev))
            self.split += split
        if ring == NRAW:
            self.start = (self.start + n) % NRAW

    start = 0


def plan():
    s = Stream()
    s.add("ada_start", JOB_U * FIRST_JOBS, split=False)
    for j, kind in enumerate(KIND):
        if kind == "ffn":
            for seg, job in enumerate((True, False)):
                for t in range(GU_TRIPS[j][seg]):
                    for name in TRIP[job]:
                        s.add(f"gu{j}_{seg}_{t}_{name}", 1, split=not name.startswith("ada"))
            if j == 0:
                s.add("ada_15", JOB_U, split=False)
            s.add(f"out{j}", 2 * KT)
        else:
            if kind == "c":
                s.add("forget", 1)
            s.add(f"qkv{j}", 3 * KT, ring=3)
            s.add(f"out{j}", KT)
    return s


def unit_at(s, run, k, i=None, step=0, count=1):
    n = (s.first[run] if isinstance(run, str) else run) + k

    def prev_split(m):
        idx = s.units[m][2]
        if idx is None or idx < NHL:
            return 0
        return 1 + next(q for q in range(m, -1, -1) if s.units[q][2] == idx - NHL)

    slot, use, idx, prev = s.units[n]
    if i is None or isinstance(i, int):
        n += step * (i or 0)
        slot, use, idx, prev = s.units[n]
        return dict(n=n, slot=slot, landed=16 * use, idx=idx, hl=None if idx is None else idx % NHL,
                    raw_free=0 if prev is None else prev + 1, hl_free=prev_split(n))
    trips = [n + step * t for t in range(count)]
    us = [s.units[t] for t in trips]
    du = us[1][1] - us[0][1] if count > 1 else 0
    di = us[1][2] - us[0][2] if count > 1 and idx is not None else 0
    for t, u in enumerate(us):
        assert u[0] == slot and u[1] == use + du * t
        assert idx is None or (u[2] == idx + di * t and u[2] % NHL == idx % NHL)
    raw = max((0 if u[3] is None else u[3] + 1) - step * t for t, u in enumerate(us))
    hlf = max(prev_split(m) - step * t for t, m in enumerate(trips))
    return dict(n=n + step * i, slot=slot, landed=16 * (use + du * i), idx=None if idx is None else idx + di * i,
                hl=None if idx is None else idx % NHL, raw_free=max(raw, 0) + step * i, hl_free=max(hlf, 0) + step * i)


def gu_unit(s, j, seg, name, i, more=0):
    trip = TRIP[seg == 0]
    first = s.first[f"gu{j}_{seg}_0_{name}"] + more
    return unit_at(s, first, 0, i, len(trip), GU_TRIPS[j][seg] - 1)


def program(nc, ins, outs):
    (x_prompt, x_sample, c_prompt, c_sample, ca_k, ca_v, cb_k, cb_v, cc_k, cc_v, cc_logf,
     w_ada, b_ada, norm_pre, norm_post, ffn_wg, ffn_wu, ffn_wd, w_in_ab, w_out_ab, relpos,
     lambda_b, subln_b, w_in_c, b_f, w_out_c) = ins
    (y_p, y_s, pa_k, pa_v, pb_k, pb_v, pc_k, pc_v, pc_lf, sa_k, sa_v, sb_k, sb_v, sc_k, sc_v, sc_lf) = outs
    ws = plan()

    def colblocks(w):
        return w.rearrange("(k p) (f n) -> f p k n", p=P, n=P)

    ada_d = [w_ada[l].rearrange("(u k p) (c n) -> c u p k n", p=P, n=JOB, k=2) for l in range(2)]
    mod_dram = nc.dram_tensor("mod_rows", (2, JOBS * JOB), F32, kind="Internal").ap()
    gate_d = {j: colblocks(ffn_wg[j // 3, (j % 3) // 2]) for j in (0, 2, 3, 5)}
    up_d = {j: colblocks(ffn_wu[j // 3, (j % 3) // 2]) for j in (0, 2, 3, 5)}
    down_d = {j: ffn_wd[j // 3, (j % 3) // 2].rearrange("(h k p) (m n) -> m h p k n", p=P, n=P, h=2)
              for j in (0, 2, 3, 5)}
    inab_d = colblocks(w_in_ab[0])
    outab_d = colblocks(w_out_ab[0])
    inc_d = colblocks(w_in_c[0][:, 0:3 * DM])
    wfl_d = w_in_c[0][:, 3 * DM:3 * DM + 16].rearrange("(k p) n -> p k n", p=P)
    outc_d = colblocks(w_out_c[0])
    rel_scratch = nc.dram_tensor("rel_scratch", (8, P, 384), F32, kind="Internal").ap()
    dec_scratch = nc.dram_tensor("decay_scratch", (16, SEQ + PAST + DEC), F32, kind="Internal").ap()

    def tokcols(prompt, sample):
        p = prompt.rearrange("(t q) (f n) -> f q t n", q=P, n=P)
        s = sample.rearrange("q (f n) -> f q n", n=P)
        return p, s

    def flat(a):
        return a[0, 0].rearrange("t h d -> t (h d)")

    kv_out = {"a": (tokcols(flat(pa_k), flat(sa_k)), tokcols(flat(pa_v), flat(sa_v))),
              "b": (tokcols(flat(pb_k), flat(sb_k)), tokcols(flat(pb_v), flat(sb_v))),
              "c": (tokcols(flat(pc_k), flat(sc_k)), tokcols(flat(pc_v), flat(sc_v)))}
    cache_in = {n: [flat(a).rearrange("(t q) (f n) -> f q t n", q=P, n=P) for a in kv]
                for n, kv in (("a", (ca_k, ca_v)), ("b", (cb_k, cb_v)), ("c", (cc_k, cc_v)))}

    with ExitStack() as ctx:
        def sem(name):
            return ctx.enter_context(nc.semaphore(name))

        cursor = [((nc.sbuf_base + 63) // 64) * 64]

        def sb_at(name, shape, dt, offset):
            return nc.alloc_sbuf_tensor_at(name, shape, dt, offset=offset)

        def size(shape):
            return int(np.prod(shape[1:])) * 4

        def sb(name, shape, dt=F32):
            t = sb_at(name, shape, dt, cursor[0])
            cursor[0] += (size(shape) + 31) // 32 * 32
            return t

        raw = sb("raw", [P, NRAW, DK, P])
        w_hi = sb("w_hi", [P, NHL, DK, P], F32R)
        w_lo = sb("w_lo", [P, NHL, DK, P], F32R)
        x = sb("x", [P, KT, TOK])
        h_at = cursor[0]
        h_hi = sb("h_hi", [P, KT, TOK], F32R)
        h_lo = sb("h_lo", [P, KT, TOK], F32R)
        y = sb_at("y", [P, KT, TOK], F32, h_at)
        work = sb("work", [P, 2, TOK])
        prod = sb("prod", [P, 2, TOK])
        sq_sum = sb("sq_sum", [P, TOK])
        rstd = sb("rstd", [P, TOK])
        ident = sb("ident", [P, P])
        mean_w = sb("mean_w", [P, P])
        causal = sb("causal", [P, P])
        eps = sb("eps", [P, 1])
        warm = sb("warm", [P, NSUB])
        silu_c = sb("silu_c", [P, KT, 2])
        mod_out = sb("mod_out", [2, JOB])
        mod_in = sb("mod_in", [48, P])
        norms = sb("norms", [P, 2, NSUB, KT])
        ada_b = sb("ada_b", [P, 2, 9 * KT])
        co_scale = sb("co_scale", [P, KT, 2])
        co_shift = sb("co_shift", [P, KT, 2])
        co_gate = sb("co_gate", [P, KT, 2])
        co_tmp = sb("co_tmp", [P, 2 * KT, 2])
        neg_max = sb("neg_max", [P, 10])
        row_sum = sb("row_sum", [P, 10])
        row_inv = sb("row_inv", [P, 10])
        neg_slope = sb("neg_slope", [P, 4])
        lam = sb("lam", [P, 8])
        sub_g = sb("sub_g", [P, P])
        b_sq = sb("b_sq", [P, 4, QT + 1])
        union = cursor[0]
        act_hi = sb("act_hi", [P, FT, TOK], F32R)
        act_lo = sb("act_lo", [P, FT, TOK], F32R)
        end = cursor[0]
        assert end <= nc.sbuf_usable_end, (end, nc.sbuf_usable_end)

        x_nat = sb_at("x_nat", [P, QT + 1, DM], F32, union)
        rows_at = union + size([1, QT + 1, DM])
        c_rows = sb_at("c_rows", [16, P], F32, rows_at)
        norm_rows = sb_at("norm_rows", [96, P], F32, rows_at + 512)
        ada_rows = sb_at("ada_rows", [72, 2, P], F32, rows_at + 1024)
        lam_in = sb_at("lam_in", [P, 4, HD], F32, rows_at + 2048)
        rel_in = sb_at("rel_in", [8, 257], F32, rows_at + 3072)
        rel_rev = sb_at("rel_rev", [8, 384], F32, rows_at + 3072 + 1056)

        cursor[0] = union
        o_hi = sb("o_hi", [P, KT, TOK], F32R)
        o_lo = sb("o_lo", [P, KT, TOK], F32R)
        qT = sb("qT", [P, 2, TOK])
        kT = sb("kT", [P, 2, TOK])
        vT = sb("vT", [P, TOK])
        k_nat = sb("k_nat", [P, 2, QT + 1, P])
        v_nat = sb("v_nat", [P, 2, QT + 1, P])
        ck_nat = sb("ck_nat", [P, 2, 2, P])
        cv_nat = sb("cv_nat", [P, 2, 2, P])
        ckT = sb("ckT", [P, 2, PAST])
        probs = sb("probs", [P, PSLOTS, SEQ])
        probsT = sb("probsT", [P, 2, QT, P])
        o_nat = sb("o_nat", [P, 2, P])
        mixer_top = cursor[0]
        rel_bias = sb("rel_bias", [P, 8, 2 * P])
        dist = sb("dist", [P, SEQ])
        b_nat = sb("b_nat", [P, 4, QT + 1, P])
        assert cursor[0] <= nc.sbuf_usable_end, (cursor[0], end)
        dist_i = sb_at("dist_i", [P, SEQ], I32, mixer_top + 8 * 1024 + 2048)
        cursor[0] = mixer_top
        dk_b = sb("dk_b", [P, 2, 2, SEQ + PAST + DEC])
        dqT = sb("dqT", [P, QT + 1, 16])
        lf_nat = sb("lf_nat", [P, QT + 1, 16])
        clf_nat = sb("clf_nat", [P, 2, 16])
        bf_col = sb("bf_col", [16, 1])
        logf = sb("logf", [16, TOK])
        decay = sb("decay", [16, SEQ + PAST + DEC])
        assert cursor[0] <= nc.sbuf_usable_end, (cursor[0], end)
        z_t = sb_at("z_t", [16, TOK], F32, mixer_top)
        e_t = sb_at("e_t", [16, TOK], F32, mixer_top + 2176)
        u_t = sb_at("u_t", [16, TOK], F32, mixer_top + 2 * 2176)
        l_t = sb_at("l_t", [16, TOK], F32, mixer_top + 3 * 2176)
        ones16 = sb_at("ones16", [16, TOK], F32, mixer_top + 4 * 2176)

        lin = ctx.enter_context(nc.psum_tensor("lin", [P, 4, 512], F32))
        ps_s = ctx.enter_context(nc.psum_tensor("ps_s", [P, 2, 512], F32))
        ps_t = ctx.enter_context(nc.psum_tensor("ps_t", [P, 512], F32))
        ps_o = ctx.enter_context(nc.psum_tensor("ps_o", [P, 512], F32))
        mod_ps = ps_o[:, 0:48].rearrange("p (g q) -> p q g", g=2)
        mod_ps0 = ps_o[:, 0:32].rearrange("p (g q) -> p q g", g=2)

        def pair(a):
            return lin[:, 2 * a:2 * a + 2, 0:HALF]

        def two(ap):
            return ap.rearrange("p (a n) -> p a n", a=2)

        raw_in = [sem(f"raw_in{k}") for k in range(NRAW)]
        unit_done = sem("unit_done")
        hi_done = sem("hi_done")
        lo_done = sem("lo_done")
        const_in = sem("const_in")
        x_in = sem("x_in")
        pool_const = sem("pool_const")
        const_tr = sem("const_tr")
        silu_c_done = sem("silu_c_done")
        vec_const = sem("vec_const")
        xt_ps = sem("xt_ps")
        x_ready = sem("x_ready")
        gate_read = sem("gate_read")
        prod_done = sem("prod_done")
        act_hi_done = sem("act_hi_done")
        act_lo_done = sem("act_lo_done")
        sq_done = sem("sq_done")
        y_copied = sem("y_copied")
        sq_added = sem("sq_added")
        sq_used = sem("sq_used")
        mean_done = sem("mean_done")
        std_done = sem("std_done")
        rstd_done = sem("rstd_done")
        y_norm = sem("y_norm")
        t_done = sem("t_done")
        h_hi_done = sem("h_hi_done")
        h_lo_done = sem("h_lo_done")
        job_copied = sem("job_copied")
        job_stored = sem("job_stored")
        mod_loaded = sem("mod_loaded")
        mod_turned = sem("mod_turned")
        coef = sem("coef")
        kv_evac = sem("kv_evac")
        tr_ps = sem("tr_ps")
        tr_out = sem("tr_out")
        cache_k = [sem(f"cache_k{k}") for k in range(2)]
        cache_v = [sem(f"cache_v{k}") for k in range(2)]
        kv_stored = [sem(f"kv_stored{k}") for k in range(2)]
        lf_stored = sem("lf_stored")
        s_ps = sem("s_ps")
        s_added = sem("s_added")
        s_maxed = sem("s_maxed")
        exp_done = sem("exp_done")
        inv_done = sem("inv_done")
        comb_half = sem("comb_half")
        comb_done = sem("comb_done")
        pt_used = sem("pt_used")
        pv_done = sem("pv_done")
        o_read = sem("o_read")
        ot_ps = sem("ot_ps")
        o_hi_done = sem("o_hi_done")
        o_lo_done = sem("o_lo_done")
        b_sq_done = sem("b_sq_done")
        b_std = sem("b_std")
        b_inv = sem("b_inv")
        b_scaled = sem("b_scaled")
        rel_done = sem("rel_done")
        rel_dram = sem("rel_dram")
        rel_loaded = sem("rel_loaded")
        dist_done = sem("dist_done")
        lam_landed = sem("lam_landed")
        lam_done = sem("lam_done")
        fl_done = sem("fl_done")
        fl_act = sem("fl_act")
        fl_in = sem("fl_in")
        fl_ps = sem("fl_ps")
        fl_dram = sem("fl_dram")
        dk_in = [sem(f"dk_in{k}") for k in range(2)]
        masked = sem("masked")
        settled = sem("settled")
        nat_a = sem("nat_a")
        nat_ps = sem("nat_ps")
        nat_out = sem("nat_out")
        stored = sem("stored")

        block = ctx.enter_context(nc.Block())

        sq_base = [8 + 16 * j for j in range(NSUB)]

        def loop(eng, n, body):
            if n == 1:
                body(0)
            elif n > 1:
                with eng.Fori(0, n) as i:
                    body(i)

        def mixer_counts(kind):
            c = [dict(s=0, tr=0, pv=0, ot=0, comb=0) for _ in range(10)]
            for st in range(9):
                n = dict(c[st])
                k = who(kind, st - 1)
                if st >= 1:
                    n["s"] += 10
                    n["tr"] += 5 if k == "b" else 10
                    n["pv"] += 5 if k == "b" else 10
                    n["ot"] += 0 if k == "b" else 5
                    n["comb"] += 5 if k == "b" else 0
                if st < 8:
                    n["tr"] += 3
                c[st + 1] = n
            return c

        def who(kind, p):
            return "c" if kind == "c" else "ab"[p % 2]

        counts = {k: mixer_counts(k) for k in ("ab", "c")}
        off = {"ab": dict(s=0, tr=0, pv=0, ot=0, comb=0, ev=0), "c": dict(counts["ab"][9])}
        off["c"]["ev"] = 24
        off["c"]["ot"] += 8

        class Stage:

            def __init__(self, kind, st, i=None, trips=1):
                self.kind, self.st, self.i, self.trips = kind, st, i, trips
                self.ii = 0 if i is None else i
                self.att = who(kind, st - 1) if st >= 1 else None
                self.par = (st - 1) % 2 if st >= 1 else None
                self.new = st % 2 if st < 8 else None
                half = 0 if kind == "ab" else 4
                self.same_new = half + st // 2 + self.ii
                self.same_att = half + (st - 1) // 2 + self.ii
                self.order = [(t, hh) for t in (3, 2, 1, 0, QT) for hh in (0, 1)]

            def at(self, key):
                c = counts[self.kind]
                d = c[self.st + 2][key] - c[self.st][key] if self.i is not None else 0
                return off[self.kind][key] + c[self.st][key] + d * self.ii

            def ev(self):
                return off[self.kind]["ev"] + 3 * self.st + 6 * self.ii

            def pairs(self):
                return (0 if self.kind == "ab" else 8) + self.st + 2 * self.ii

            def tile_of(self, p_off):
                p = self.st + p_off
                return (p // 2 if self.kind == "ab" else p) + (1 if self.kind == "ab" else 2) * self.ii

            def unit(self, k):
                run = "qkv1" if self.kind == "ab" else "qkv4"
                if self.i is None:
                    return unit_at(ws, run, 3 * self.st + k)
                return unit_at(ws, run, 3 * self.st + k, self.i, 6, self.trips)

        def stages(eng, kind, emit, after_first=None):
            emit(Stage(kind, 0))
            if after_first is not None:
                after_first()
            with eng.Fori(0, 3) as i:
                emit(Stage(kind, 1, i, 3))
                emit(Stage(kind, 2, i, 3))
            emit(Stage(kind, 7))
            emit(Stage(kind, 8))

        def settle(eng):
            eng.sem_inc(settled, 1)

        def next_unit(st):
            return st.unit(3) if st.st < 7 else None

        def tr_plan(st):
            lag = 3 if st.att == "b" else 2
            found = []
            for s in range(STEPS + 2):
                if st.new is not None and s in (5, 9, 12):
                    found.append((s, "turn"))
                j = s - lag
                if st.att is not None and 0 <= j < 10 and (st.att != "b" or j % 2):
                    found.append((s, "probs"))
            return found

        def ffn_index(j):
            return KIND[:j].count("ffn")

        def segments(eng, j, emit):
            for seg, n in enumerate(GU_TRIPS[j]):
                if n:
                    t0 = GU_TRIPS[j][0] * seg
                    loop(eng, n - 1, lambda i, seg=seg, t0=t0: emit(seg, i, t0, False))
                    emit(seg, n - 1, t0, True)

        gu_loops = {0: [(0, 11)], 2: [(0, 2), (2, 11)], 3: [(0, 9), (9, 11)], 5: [(0, 11)]}

        def after_up(w_split, j, seg, i, a, last):
            if a == 0:
                w_split(gu_unit(ws, j, seg, "gate1", i), KT)
            elif not last:
                w_split(gu_unit(ws, j, seg, "up1", i, 1), KT)
            elif seg == 0 and GU_TRIPS[j][1]:
                w_split(unit_at(ws, f"gu{j}_1_0_gate0", 0), KT)
            elif j > 0:
                w_split(unit_at(ws, f"out{j}", 0), DK)

        def first_of(j):
            return first_gu(j) if KIND[j] == "ffn" else unit_at(ws, "forget" if KIND[j] == "c" else f"qkv{j}", 0)

        def first_gu(j):
            seg = 0 if GU_TRIPS[j][0] else 1
            return unit_at(ws, f"gu{j}_{seg}_0_gate0", 0)

        def next_down(j, i, a):
            return unit_at(ws, f"out{j}", 2 * a + 2, i, 4, KT // 2 - 1)

        def keys(t):
            return (t + 1) * P if t < QT else PAST + DEC

        def rows(t):
            return P if t < QT else DEC

        @block.sync
        def _(sp):
            def load(u, src, tiles, cols=P):
                sp.wait_ge(unit_done, u["raw_free"])
                sp.dma_start(raw[:, u["slot"], 0:tiles, 0:cols], src).then_inc(raw_in[u["slot"]], 16)

            def load_ada(u, layer, job, k):
                sp.wait_ge(unit_done, u["raw_free"])
                sp.dma_start(raw[:, u["slot"], 0:KT, :].rearrange("p (k a) n -> p k (a n)", k=2),
                             ada_d[layer][job, k]).then_inc(raw_in[u["slot"]], 16)

            sp.dma_start(c_rows[0:8, :], c_prompt.rearrange("g (k p) -> (g k) p", p=P)).then_inc(const_in, 16)
            sp.dma_start(c_rows[8:16, :], c_sample.rearrange("g (k p) -> (g k) p", p=P)).then_inc(const_in, 16)
            for k, src in enumerate((norm_pre, norm_post)):
                sp.dma_start(norm_rows[48 * k:48 * k + 48, :],
                             src.rearrange("l s (k p) -> (l s k) p", p=P)).then_inc(const_in, 16)
            for l in range(2):
                sp.dma_start(ada_rows[:, l, :], b_ada[l].rearrange("(f p) -> f p", p=P)).then_inc(const_in, 16)
            sp.dma_start(x_nat[:, 0:QT, :], x_prompt[0].rearrange("(t q) n -> q t n", q=P)).then_inc(x_in, 16)
            sp.dma_start(x_nat[0:DEC, QT, :], x_sample[0]).then_inc(x_in, 16)
            for n in range(FIRST_JOBS):
                for k in range(JOB_U):
                    load_ada(unit_at(ws, "ada_start", JOB_U * n + k), 0, n, k)
            for j, kind in enumerate(KIND):
                if kind == "ffn":
                    for t0, t1 in gu_loops[j]:
                        with_job = t1 <= GU_TRIPS[j][0]
                        seg = 0 if with_job else 1
                        base = t0 - GU_TRIPS[j][0] * seg
                        job0 = GU_JOB0[j] + t0
                        layer = job0 // (JOBS // 2)

                        def gu(i, j=j, t0=t0, base=base, with_job=with_job, seg=seg, job0=job0, layer=layer, n=t1 - t0):
                            for name in TRIP[with_job]:
                                u = unit_at(ws, ws.first[f"gu{j}_{seg}_{base}_{name}"], 0, i, len(TRIP[with_job]), n)
                                if name.startswith("ada"):
                                    load_ada(u, layer, job0 - layer * (JOBS // 2) + i, int(name[3]))
                                else:
                                    load(u, (gate_d if name.startswith("gate") else up_d)[j][2 * (t0 + i) + int(name[-1])], KT)
                        loop(sp, t1 - t0, gu)
                    if j == 0:
                        for k in range(JOB_U):
                            load_ada(unit_at(ws, "ada_15", k), 0, 15, k)

                    def down(i, j=j):
                        for k in range(4):
                            load(unit_at(ws, f"out{j}", k, i, 4, KT // 2), down_d[j][2 * i + k // 2, k % 2], DK)
                    loop(sp, KT // 2, down)
                else:
                    if kind == "c":
                        load(unit_at(ws, "forget", 0), wfl_d, KT, 16)

                    def qkv(st):
                        if st.st == 8:
                            return
                        if kind == "ab":
                            first = 12 * (st.new) + st.tile_of(0)
                            blocks = [first + 4, first + 8, first]
                            src = inab_d
                        else:
                            first = st.tile_of(0)
                            blocks = [first + 8, first + 16, first]
                            src = inc_d
                        for k in range(3):
                            load(st.unit(k), src[blocks[k]], KT)
                    stages(sp, kind, qkv)
                    for m in range(KT):
                        load(unit_at(ws, f"out{j}", m), (outab_d if kind == "ab" else outc_d)[m], KT)
            for t in range(QT + 1):
                sp.wait_ge(nat_out, 2 * t + 2)
                if t < QT:
                    sp.dma_start(y_p[0, t * P:(t + 1) * P, :], x_nat[:, t, :]).then_inc(stored, 16)
                else:
                    sp.dma_start(y_s[0], x_nat[0:DEC, t, :]).then_inc(stored, 16)
            sp.wait_ge(stored, 16 * (QT + 1))
            for par in range(2):
                sp.wait_ge(kv_stored[par], 64 * 8)
            sp.wait_ge(lf_stored, 32)

        @block.gpsimd
        def _(pool):
            nc.gpsimd.memset(ident[:], 0.0).then_inc(pool_const, 1)
            nc.gpsimd.memset(mean_w[:], 1.0 / DM).then_inc(pool_const, 1)
            nc.gpsimd.memset(causal[:], 0.0).then_inc(pool_const, 1)
            nc.gpsimd.memset(eps[:], EPS).then_inc(pool_const, 1)
            for h in range(4):
                nc.gpsimd.memset(neg_slope[:, h:h + 1], -(2.0 ** (-8.0 * (h + 1) / 4))).then_inc(pool_const, 1)
            pool.wait_ge(pool_const, 8)
            nc.gpsimd.affine_select(out=ident[:], in_=ident[:], compare_op=ALU.not_equal, fill=1.0, base=0,
                                    pattern=[[-1, P]], channel_multiplier=1).then_inc(pool_const, 1)
            nc.gpsimd.affine_select(out=causal[:], in_=causal[:], compare_op=ALU.is_ge, fill=NEG, base=0,
                                    pattern=[[-1, P]], channel_multiplier=1).then_inc(pool_const, 1)
            pool.dma_start(lam_in[:].rearrange("p a d -> p (a d)"),
                           lambda_b[0].rearrange("(o a) d -> o (a d)", o=1).broadcast_to([P, 4 * HD])).then_inc(lam_landed, 16)
            pool.dma_start(sub_g[:], subln_b[0:1, :].broadcast_to([P, P])).then_inc(lam_landed, 16)
            pool.dma_start(rel_in[:], relpos[0]).then_inc(rel_dram, 16)
            def store_job(job):
                pool.wait_ge(job_copied, job + 1)
                settle(pool)
                pool.dma_start(mod_dram[:, bass.ds(job * JOB, JOB)], mod_out[:, :]).then_inc(job_stored, 16)

            def store_jobs(first, n):
                loop(pool, n, lambda i: store_job(first + i))

            def load_mod(j, last_job):
                pool.wait_ge(job_stored, 16 * (last_job + 1))
                if j >= 0:
                    pool.wait_ge(mod_turned, j + 1)
                f0, n = (0, 16) if j < 0 else (24 * j + 16, 24 if j + 1 < NSUB else 8)
                for g in range(2):
                    pool.dma_start(mod_in[g * n:g * n + n, :],
                                   mod_dram[g, f0 * P:(f0 + n) * P].rearrange("(f p) -> f p", p=P)).then_inc(mod_loaded, 16)

            store_jobs(0, FIRST_JOBS)
            load_mod(-1, FIRST_JOBS - 1)
            pool.wait_ge(rel_done, 2)
            pool.dma_start(rel_scratch[:, :, :], rel_rev[:].rearrange("h (o n) -> h o n", o=1).broadcast_to([8, P, 384]))\
                .then_inc(rel_dram, 16)
            pool.wait_ge(rel_dram, 32)

            def kv(st):
                att = st.kind
                if st.st < 8:
                    n = who(st.kind, st.st)
                    pool.wait_ge(pv_done, st.at("pv"))
                    settle(pool)
                    pool.dma_start(ck_nat[:, st.new], cache_in[n][0][st.tile_of(0)]).then_inc(cache_k[st.new], 16)
                    pool.dma_start(cv_nat[:, st.new], cache_in[n][1][st.tile_of(0)]).then_inc(cache_v[st.new], 16)
                    if n == "c":
                        for hh in range(2):
                            pool.dma_start(dk_b[:, st.new, hh, :],
                                           dec_rows[2 * st.tile_of(0) + hh].broadcast_to([P, SEQ + PAST + DEC])
                                           ).then_inc(dk_in[st.new], 16)
                    pool.wait_ge(tr_out, st.at("tr") + (counts[st.kind][st.st + 1]["tr"] - counts[st.kind][st.st]["tr"]))
                    settle(pool)
                    for src, (dp, ds) in zip((k_nat, v_nat), kv_out[n]):
                        pool.dma_start(dp[st.tile_of(0)], src[:, st.new, 0:QT, :]).then_inc(kv_stored[st.new], 16)
                        pool.dma_start(ds[st.tile_of(0)], src[0:DEC, st.new, QT, :]).then_inc(kv_stored[st.new], 16)

            dec_rows = dec_scratch.rearrange("h (o n) -> h o n", o=1)
            store_jobs(4, 6)
            load_mod(0, 9)
            store_jobs(10, 6)
            load_mod(1, 15)
            pool.wait_ge(mean_done, 2)
            for hd in range(8):
                src = bass.AP(rel_scratch.tensor, 384 * P * hd + P - 1, [[384 - 1, P], [1, 2 * P]])
                pool.dma_start(rel_bias[:, hd, :], src).then_inc(rel_loaded, 16)
            nc.gpsimd.iota(dist_i[:], pattern=[[-1, SEQ]], base=SEQ - P, channel_multiplier=1).then_inc(pool_const, 1)
            stages(pool, "ab", kv)
            store_jobs(16, 6)
            load_mod(2, 21)
            store_jobs(22, 6)
            load_mod(3, 27)
            store_jobs(28, 8)
            load_mod(4, 35)
            pool.wait_ge(mean_done, 8)
            pool.dma_start(clf_nat[:], cc_logf[0, 0].rearrange("(t q) h -> q t h", q=P)).then_inc(fl_in, 16)
            pool.dma_start(bf_col[:], b_f.rearrange("a h -> h a")).then_inc(fl_in, 16)
            pool.wait_ge(fl_done, FL_DECAY)
            pool.dma_start(dec_scratch[:, :], decay[:]).then_inc(fl_dram, 16)
            pool.wait_ge(fl_dram, 16)
            stages(pool, "c", kv)
            load_mod(5, 35)
            pool.wait_ge(fl_act, 4)
            pool.dma_start(pc_lf[0, 0].rearrange("(t q) h -> q t h", q=P), lf_nat[:, 0:QT, :]).then_inc(lf_stored, 16)
            pool.dma_start(sc_lf[0, 0], lf_nat[0:DEC, QT, :]).then_inc(lf_stored, 16)

        @block.tensor
        def _(pe):
            def products(u, out, k, moving_hi, moving_lo, first, last):
                hl = u["hl"]
                m = None
                for n, (w, mv) in enumerate(((w_hi, moving_hi), (w_hi, moving_lo), (w_lo, moving_hi))):
                    for a in range(2):
                        m = nc.tensor.matmul(lin[:, 2 * out + a, 0:HALF], w[:, hl, k, :],
                                             mv[:, a * HALF:(a + 1) * HALF],
                                             start=first and n == 0, stop=last and n == 2)
                return m

            def unit(u, out, tiles, hi, lo, k0=0, first=True, last=True, gradual=None):
                pe.wait_ge(lo_done, u["idx"] + 1)
                for k in range(tiles):
                    if gradual is not None:
                        pe.wait_ge(h_lo_done, gradual + k + 1)
                    m = products(u, out, k, hi[:, k0 + k, :], lo[:, k0 + k, :],
                                 first and k == 0, last and k == tiles - 1)
                m.then_inc(unit_done, 1)

            def ada_unit(u, k, job):
                if k == 0:
                    pe.wait_ge(job_copied, job)
                pe.wait_ge(raw_in[u["slot"]], u["landed"])
                w = raw[:, u["slot"], 0:KT, :].rearrange("p (k a) n -> p k (a n)", k=2)
                for t in range(2):
                    kt = 2 * k + t
                    m = nc.tensor.matmul(ps_t[0:2, :], silu_c[:, kt, :], w[:, t, :], start=kt == 0, stop=kt == KT - 1)
                m.then_inc(unit_done, 1)

            def turn_mod(j):
                pe.wait_ge(mod_loaded, 32 * (j + 2))
                n = 32 if j < 0 else 48 if j + 1 < NSUB else 16
                nc.tensor.transpose(ps_o[:, 0:n], mod_in[0:n, :], ident[0:n, 0:n]).then_inc(mod_turned, 1)

            def mean(src, first, last):
                for a in range(2):
                    m = nc.tensor.matmul(ps_s[:, a, 0:HALF], mean_w[:], src[:, a * HALF:(a + 1) * HALF],
                                         start=first, stop=last)
                return m

            def post_norm(j):
                pe.wait_ge(sq_added, 9 * (j + 1))
                mean(sq_sum[:], True, True).then_inc(mean_done, 1)

            def pre_norm(j):
                for m in range(KT):
                    pe.wait_ge(sq_done, sq_base[j] - 8 + m + 1)
                    mm = mean(work[:, m % 2, :], m == 0, m == KT - 1)
                    if m < KT - 1:
                        mm.then_inc(sq_used, 1)
                mm.then_inc(mean_done, 1)

            pe.wait_ge(pool_const, 10)
            pe.wait_ge(const_in, 16 * 6)
            nc.tensor.transpose(ps_s[:, 0, 0:16], c_rows[:], ident[0:16, 0:16])
            nc.tensor.transpose(ps_s[:, 0, 16:112], norm_rows[:], ident[0:96, 0:96]).then_inc(const_tr, 1)
            nc.tensor.transpose(ps_s[:, 1, 0:72], ada_rows[:, 0, :], ident[0:72, 0:72])
            nc.tensor.transpose(ps_s[:, 1, 72:144], ada_rows[:, 1, :], ident[0:72, 0:72]).then_inc(const_tr, 1)
            pe.wait_ge(x_in, 32)
            for m in range(KT):
                if m >= 2:
                    pe.wait_ge(x_ready, m - 1)
                for t in range(QT):
                    nc.tensor.transpose(lin[:, 2 * (m % 2), t * P:(t + 1) * P], x_nat[:, t, m * P:(m + 1) * P], ident[:])
                nc.tensor.transpose(lin[:, 2 * (m % 2) + 1, 0:DEC], x_nat[0:DEC, QT, m * P:(m + 1) * P],
                                    ident[0:DEC, 0:DEC]).then_inc(xt_ps, 1)
            pe.wait_ge(silu_c_done, 1)
            for n in range(FIRST_JOBS):
                for k in range(JOB_U):
                    ada_unit(unit_at(ws, "ada_start", JOB_U * n + k), k, n)
            pe.wait_ge(vec_const, 2)
            pre_norm(0)
            turn_mod(-1)

            def stage(st):
                order = st.order
                att = st.att
                evs = st.ev()
                lag = 3 if att == "b" else 2

                def lin_chunk(s):
                    k, part = divmod(s, 4)
                    u = st.unit(k)
                    out = (0, 1, 0)[k]
                    if part == 0:
                        pe.wait_ge(lo_done, u["idx"] + 1)
                        if k == 2 or st.st > 0:
                            pe.wait_ge(kv_evac, evs + (0, -1, 1)[k])
                        elif k == 1 and st.kind == "c":
                            pe.wait_ge(fl_done, 1)
                    for kt in (2 * part, 2 * part + 1):
                        if st.st == 0 and k == 0 and st.i is None and (st.kind == "ab"):
                            pe.wait_ge(h_lo_done, 8 + kt + 1)
                        m = products(u, out, kt, h_hi[:, kt, :], h_lo[:, kt, :], kt == 0, kt == KT - 1)
                    if part == 3:
                        m.then_inc(unit_done, 1)

                def turn(step):
                    new, base = st.new, st.at("tr")
                    if st.st == 0 and st.kind == "c" and step == 5:
                        pe.wait_ge(fl_done, FL_DECAY - 2)
                    if step == 5:
                        pe.wait_ge(kv_evac, evs + 1)
                        src = kT[:, new, :]
                    elif step == 9:
                        pe.wait_ge(kv_evac, evs + 2)
                        src = vT[:, :]
                    n = tr_plan(st).index((step, "turn"))
                    wait_tr(base + n)
                    if step in (5, 9):
                        for t in range(QT):
                            m = nc.tensor.transpose(ps_t[:, t * P:(t + 1) * P], src[:, t * P:(t + 1) * P], ident[:])
                    else:
                        pe.wait_ge(cache_k[new], 16 * (st.same_new + 1))
                        nc.tensor.transpose(ps_t[0:DEC, 0:P], kT[:, new, SEQ:TOK], ident[:])
                        nc.tensor.transpose(ps_t[0:DEC, P:2 * P], vT[:, SEQ:TOK], ident[:])
                        for c in range(2):
                            m = nc.tensor.transpose(ps_t[:, (2 + c) * P:(3 + c) * P], ck_nat[:, new, c, :], ident[:])
                    m.then_inc(tr_ps, 1)

                def wait_tr(n):
                    pe.wait_ge(tr_out, n)

                def scores(j):
                    t, hh = order[j]
                    par, r = st.par, rows(order[j][0])
                    hs = slice(HD * hh, HD * hh + HD)
                    q0 = t * P if t < QT else SEQ
                    if j == 0:
                        pe.wait_ge(kv_evac, evs)
                        pe.wait_ge(tr_out, st.at("tr"))
                    if j >= 2:
                        pe.wait_ge(s_added, st.at("s") + j - 1)
                    lhs = qT[hs, par, q0:q0 + r]
                    if t == QT:
                        settle(pe)
                    if t < QT:
                        m = nc.tensor.matmul(ps_s[0:r, j % 2, 0:keys(t)], lhs, kT[hs, par, 0:keys(t)],
                                             start=True, stop=True)
                    else:
                        nc.tensor.matmul(ps_s[0:r, j % 2, 0:PAST], lhs, ckT[hs, par, :], start=True, stop=True)
                        m = nc.tensor.matmul(ps_s[0:r, j % 2, PAST:PAST + DEC], lhs, kT[hs, par, SEQ:TOK],
                                             start=True, stop=True)
                    m.then_inc(s_ps, 1)

                def transpose_probs(j, q):
                    t = order[j][0]
                    slot = (j - 1 if att == "b" else j) % PSLOTS
                    if att == "b":
                        pe.wait_ge(comb_done, st.at("comb") + q + 1)
                    else:
                        pe.wait_ge(exp_done, st.at("s") + j + 1)
                    wait_tr(st.at("tr") + tr_plan(st).index((j + lag, "probs")))
                    if t == QT:
                        settle(pe)
                    if t < QT:
                        for b in range(t + 1):
                            m = nc.tensor.transpose(ps_t[:, b * P:(b + 1) * P], probs[:, slot, b * P:(b + 1) * P], ident[:])
                    else:
                        for b in range(2):
                            nc.tensor.transpose(ps_t[:, b * P:b * P + DEC], probs[0:DEC, slot, b * P:(b + 1) * P],
                                                ident[0:DEC, 0:DEC])
                        m = nc.tensor.transpose(ps_t[0:DEC, 2 * P:2 * P + DEC], probs[0:DEC, slot, PAST:PAST + DEC],
                                                ident[0:DEC, 0:DEC])
                    m.then_inc(tr_ps, 1)

                def values(j, q):
                    t, hh = order[j]
                    r, par = rows(t), st.par
                    cols = slice(0, P) if att == "b" else slice(HD * hh, HD * hh + HD)
                    width = P if att == "b" else HD
                    pe.wait_ge(tr_out, st.at("tr") + tr_plan(st).index((j + lag, "probs")) + 1)
                    if q >= 1:
                        pe.wait_ge(o_read, st.at("pv") + q)
                    if att != "b" and j >= 2:
                        pe.wait_ge(o_lo_done, st.at("ot") + j // 2)
                    if t == QT:
                        pe.wait_ge(cache_v[par], 16 * (st.same_att + 1))
                    out = ps_o[0:r, (q % 2) * P:(q % 2) * P + width]
                    n = t + 1 if t < QT else 3
                    for b in range(n):
                        if t < QT:
                            lhs, rhs = probsT[:, q % 2, b, :], v_nat[:, par, b, cols]
                        elif b < 2:
                            lhs, rhs = probsT[:, q % 2, b, 0:DEC], cv_nat[:, par, b, cols]
                        else:
                            lhs, rhs = probsT[0:DEC, q % 2, b, 0:DEC], v_nat[0:DEC, par, QT, cols]
                        m = nc.tensor.matmul(out, lhs, rhs, start=b == 0, stop=b == n - 1)
                    m.then_inc(pv_done, 1)

                def turn_out(q):
                    t = order[2 * q][0]
                    r = rows(t)
                    pe.wait_ge(o_read, st.at("pv") + 2 * q + 2)
                    settle(pe)
                    nc.tensor.transpose(ps_o[:, (2 + q % 2) * P:(2 + q % 2) * P + r], o_nat[0:r, q % 2, :],
                                        ident[0:r, 0:r]).then_inc(ot_ps, 1)

                for s in range(STEPS + 2):
                    j = s - lag - 2
                    if att in ("a", "c") and 0 <= j < 10 and j % 2:
                        turn_out(j // 2)
                    if st.new is not None and s < LIN_STEPS:
                        lin_chunk(s)
                    if st.new is not None and s in (5, 9, 12):
                        turn(s)
                    if att is None:
                        continue
                    j = s - lag
                    if 0 <= j < 10 and (att != "b" or j % 2):
                        transpose_probs(j, j // 2 if att == "b" else j)
                    j = s - lag - 1
                    if 0 <= j < 10 and (att != "b" or j % 2):
                        values(j, j // 2 if att == "b" else j)
                    if s < 10:
                        scores(s)

            for j, kind in enumerate(KIND):
                if kind == "ffn":
                    np_ = 8 * j

                    def gu(seg, i, t0, j=j, first=False):
                        base = FT * ffn_index(j)
                        for name in TRIP[seg == 0]:
                            u = unit_at(ws, ws.first[f"gu{j}_{seg}_0_{name}"], 0, i, len(TRIP[seg == 0]),
                                        GU_TRIPS[j][seg])
                            if name.startswith("ada"):
                                ada_unit(u, int(name[3]), GU_JOB0[j] + i)
                                continue
                            f = 2 * (i + t0) + int(name[-1])
                            up = name.startswith("up")
                            pe.wait_ge(prod_done if up else gate_read, base + f)
                            unit(u, int(up), KT, h_hi, h_lo, gradual=8 * j if first and name == "gate0" else None)
                    n_job, n_plain = GU_TRIPS[j]
                    gu(0 if n_job else 1, 0, 0, first=True)
                    if n_job:
                        with pe.Fori(1, n_job) as i:
                            gu(0, i, 0)
                    if n_plain:
                        with pe.Fori(0 if n_job else 1, n_plain) as i:
                            gu(1, i, n_job)
                    if j == 0:
                        for k in range(JOB_U):
                            ada_unit(unit_at(ws, "ada_15", k), k, 15)
                    pe.wait_ge(act_lo_done, FT * (ffn_index(j) + 1))
                    turn_mod(j)

                    def down(i, j=j):
                        for k in range(4):
                            m = 2 * i + k // 2
                            if k % 2 == 0:
                                pe.wait_ge(y_copied, 1 + 8 * j + m - 1)
                            unit(unit_at(ws, f"out{j}", k, i, 4, KT // 2), k // 2, DK, act_hi, act_lo,
                                 k0=DK * (k % 2), first=k % 2 == 0, last=k % 2 == 1)
                    loop(pe, KT // 2, down)
                else:
                    if kind == "c":
                        unit(unit_at(ws, "forget", 0), 1, KT, h_hi, h_lo, gradual=8 * j)
                        pe.wait_ge(fl_in, 32)
                        for t in range(2):
                            m = nc.tensor.transpose(ps_t[0:16, t * P:(t + 1) * P], clf_nat[:, t, :], ident[:])
                        m.then_inc(fl_ps, 1)

                    def turn_forget():
                        pe.wait_ge(fl_done, FL_DECAY)
                        for t in range(QT + 1):
                            m = nc.tensor.transpose(ps_s[0:rows(t), 0, 16 * t:16 * t + 16],
                                                    logf[:, t * P:t * P + rows(t)], ident[0:16, 0:16])
                        m.then_inc(fl_ps, 1)
                        for t in range(QT + 1):
                            t0 = t * P if t < QT else SEQ + PAST
                            m = nc.tensor.transpose(ps_s[0:rows(t), 1, 16 * t:16 * t + 16],
                                                    decay[:, t0:t0 + rows(t)], ident[0:16, 0:16])
                        m.then_inc(fl_ps, 1)
                        pe.wait_ge(fl_act, 6)
                    stages(pe, kind, stage, turn_forget if kind == "c" else None)
                    if kind == "ab":
                        for hd in range(4):
                            pe.wait_ge(b_scaled, hd + 1)
                            if hd >= 1:
                                pe.wait_ge(o_lo_done, 20 + 2 * hd)
                            for t in range(QT):
                                m = nc.tensor.transpose(ps_s[:, 0, t * P:(t + 1) * P], b_nat[:, hd, t, :], ident[:])
                            m.then_inc(ot_ps, 1)
                            nc.tensor.transpose(ps_s[:, 1, 0:DEC], b_nat[0:DEC, hd, QT, :],
                                                ident[0:DEC, 0:DEC]).then_inc(ot_ps, 1)
                    n_ot = off["c"]["ot"] if kind == "ab" else off["c"]["ot"] + 40
                    pe.wait_ge(o_lo_done, n_ot)
                    turn_mod(j)
                    for m in range(KT):
                        pe.wait_ge(y_copied, 1 + 8 * j + m - 1)
                        unit(unit_at(ws, f"out{j}", m), m % 2, KT, o_hi, o_lo)
                post_norm(j)
                if j + 1 < NSUB:
                    pe.wait_ge(std_done, 2 * j + 2)
                    pre_norm(j + 1)

            pe.wait_ge(x_ready, 8 * (NSUB + 1))
            for t in range(QT + 1):
                for a in range(2):
                    n = 2 * t + a
                    if n >= 4:
                        pe.wait_ge(nat_out, 2 * (n // 2) - 2)
                    for k in range(4):
                        m = nc.tensor.transpose(lin[0:rows(t), n % 4, k * P:(k + 1) * P],
                                                x[:, 4 * a + k, t * P:t * P + rows(t)], ident[:])
                    m.then_inc(nat_ps, 1)

        @block.scalar
        def _(act):
            def w_split(u, tiles):
                act.wait_ge(raw_in[u["slot"]], u["landed"])
                act.wait_ge(unit_done, u["hl_free"])
                nc.scalar.activation(w_hi[:, u["hl"], 0:tiles, :], raw[:, u["slot"], 0:tiles, :], ACT.Copy)\
                    .then_inc(hi_done, 1)

            def std(n):
                act.wait_ge(mean_done, n)
                if n > 1:
                    act.wait_ge(rstd_done, n - 1)
                nc.scalar.activation(two(rstd[:]), ps_s[:, :, 0:HALF], ACT.Sqrt, bias=eps[:, 0:1]).then_inc(std_done, 1)

            def pre_norm(j, early):
                for m in range(KT):
                    if m == 4:
                        early()
                    act.wait_ge(x_ready, 8 * j + m + 1)
                    if m >= 2:
                        act.wait_ge(sq_used, 7 * j + m - 1)
                    nc.scalar.activation(work[:, m % 2, :], x[:, m, :], ACT.Square).then_inc(sq_done, 1)
                std(2 * j + 1)
                for m in range(KT):
                    act.wait_ge(t_done, 8 * j + m + 1)
                    for g, c in ((0, slice(0, SEQ)), (1, slice(SEQ, TOK))):
                        i = nc.scalar.activation(h_hi[:, m, c], prod[:, m % 2, c], ACT.Identity,
                                                 bias=co_shift[:, m, g:g + 1])
                    i.then_inc(h_hi_done, 1)

            def square_out(j, m, a):
                act.wait_ge(y_copied, 1 + 8 * j + m + 1)
                act.wait_ge(sq_added, 9 * j + 1 + m - 1)
                nc.scalar.activation(work[:, a, :], y[:, m, :], ACT.Square).then_inc(sq_done, 1)

            def copy_job(u, job):
                act.wait_ge(unit_done, u["n"] + 1)
                act.wait_ge(job_stored, 16 * job)
                nc.scalar.activation(mod_out[:, :], ps_t[0:2, :], ACT.Copy).then_inc(job_copied, 1)

            def warm_sqrt(n):
                nc.scalar.activation(warm[:, n:n + 1], eps[:, 0:1], ACT.Sqrt)

            act.wait_ge(const_tr, 1)
            nc.scalar.activation(silu_c[:].rearrange("p k g -> p g k"),
                                 ps_s[:, 0, 0:16].rearrange("p (g k) -> p g k", g=2), ACT.Silu).then_inc(silu_c_done, 1)
            act.wait_ge(lam_done, 2)
            nc.scalar.activation(lam[:, 2:4], lam[:, 0:2], ACT.Exp).then_inc(lam_done, 1)
            act.wait_ge(pool_const, 4)
            for n in range(FIRST_JOBS):
                copy_job(unit_at(ws, "ada_start", JOB_U * n + JOB_U - 1), n)
            pre_norm(0, lambda: w_split(first_gu(0), KT))
            act.wait_ge(rel_dram, 32)

            def stage(st):
                order, att = st.order, st.att
                evs = st.ev()
                plan_t = tr_plan(st)

                def evac(k):
                    u = st.unit(k)
                    act.wait_ge(unit_done, u["n"] + 1)
                    dst = (kT[:, st.new, :], vT[:], qT[:, st.new, :])[k]
                    nc.scalar.activation(two(dst), pair((0, 1, 0)[k]), ACT.Copy,
                                         scale=HD ** -0.5 if k == 2 else 1.0).then_inc(kv_evac, 1)

                def empty_turn(step):
                    n = plan_t.index((step, "turn"))
                    act.wait_ge(tr_ps, st.at("tr") + n + 1)
                    if step in (5, 9):
                        if step == 5:
                            act.wait_ge(kv_stored[st.new], 64 * st.same_new)
                        dst = (k_nat if step == 5 else v_nat)[:, st.new, 0:QT, :].rearrange("p t n -> p (t n)")
                        nc.scalar.activation(dst, ps_t[:, :], ACT.Copy).then_inc(tr_out, 1)
                    else:
                        nc.scalar.activation(k_nat[0:DEC, st.new, QT, :], ps_t[0:DEC, 0:P], ACT.Copy)
                        nc.scalar.activation(v_nat[0:DEC, st.new, QT, :], ps_t[0:DEC, P:2 * P], ACT.Copy)
                        nc.scalar.activation(ckT[:, st.new, :], ps_t[:, 2 * P:4 * P], ACT.Copy).then_inc(tr_out, 1)

                def empty_probs(j, q, lag):
                    t = order[j][0]
                    act.wait_ge(tr_ps, st.at("tr") + plan_t.index((j + lag, "probs")) + 1)
                    if q >= 2:
                        act.wait_ge(pv_done, st.at("pv") + q - 1)
                    if t < QT:
                        nc.scalar.activation(probsT[:, q % 2, 0:t + 1, :].rearrange("p b n -> p (b n)"),
                                             ps_t[:, 0:(t + 1) * P], ACT.Copy).then_inc(tr_out, 1)
                    else:
                        nc.scalar.activation(probsT[:, q % 2, 0:2, 0:DEC],
                                             ps_t[:, 0:2 * P].rearrange("p (b n) -> p b n", b=2)[:, :, 0:DEC], ACT.Copy)
                        nc.scalar.activation(probsT[0:DEC, q % 2, 2, 0:DEC], ps_t[0:DEC, 2 * P:2 * P + DEC], ACT.Copy)\
                            .then_inc(tr_out, 1)

                def exps(j):
                    t = order[j][0]
                    r, n = rows(t), keys(t)
                    act.wait_ge(s_maxed, st.at("s") + j + 1)
                    nc.scalar.activation(probs[0:r, j % PSLOTS, 0:n], probs[0:r, j % PSLOTS, 0:n], ACT.Exp,
                                         bias=neg_max[0:r, j:j + 1], accum_out=row_sum[0:r, j:j + 1])\
                        .then_inc(exp_done, 1)

                def out_hi(q):
                    t = order[2 * q][0]
                    r = rows(t)
                    act.wait_ge(ot_ps, st.at("ot") + q + 1)
                    nc.scalar.activation(o_hi[:, st.tile_of(-1), t * P:t * P + r],
                                         ps_o[:, (2 + q % 2) * P:(2 + q % 2) * P + r], ACT.Copy).then_inc(o_hi_done, 1)

                def b_square(q):
                    t = order[2 * q][0]
                    r = rows(t)
                    act.wait_ge(o_read, st.at("pv") + q + 1)
                    act.wait_ge(b_sq_done, 5 * st.tile_of(-1) + q)
                    nc.scalar.activation(o_nat[0:r, 0, :], b_nat[0:r, st.tile_of(-1), t, :], ACT.Square,
                                         accum_out=b_sq[0:r, st.tile_of(-1), t:t + 1]).then_inc(b_sq_done, 1)

                lag = 3 if att == "b" else 2
                for s in range(STEPS + 2):
                    j = s - lag - 2
                    if att in ("a", "c") and 0 <= j < 10 and j % 2:
                        out_hi(j // 2)
                    if st.new is not None:
                        if s in (4, 8, 12):
                            evac(s // 4 - 1)
                        if s in (0, 4):
                            w_split(st.unit(s // 4 + 1), KT)
                        if s == 8:
                            nxt = next_unit(st)
                            if nxt is not None:
                                w_split(nxt, KT)
                        if s in (5, 9, 12):
                            empty_turn(s)
                    if att is None:
                        continue
                    j = s - lag
                    if 0 <= j < 10 and (att != "b" or j % 2):
                        empty_probs(j, j // 2 if att == "b" else j, lag)
                    j = s - lag - 2
                    if 0 <= j < 10 and j % 2 and att == "b":
                        b_square(j // 2)
                    if s < 10:
                        exps(s)

            for j, kind in enumerate(KIND):
                if kind == "ffn":
                    base = FT * ffn_index(j)

                    if j in (2, 5):
                        for par in range(2):
                            act.wait_ge(kv_stored[par], 256 * (1 + (j == 5)))
                    if j == 5:
                        act.wait_ge(lf_stored, 32)

                    def gu(seg, i, t0, last, j=j, base=base):
                        for a in range(2):
                            f = 2 * (i + t0) + a
                            w_split(gu_unit(ws, j, seg, f"up{a}", i), KT)
                            act.wait_ge(unit_done, gu_unit(ws, j, seg, f"gate{a}", i)["n"] + 1)
                            nc.scalar.activation(two(work[:, a, :]), pair(0), ACT.Silu).then_inc(gate_read, 1)
                            after_up(w_split, j, seg, i, a, last)
                            if a == 1 and seg == 0:
                                copy_job(gu_unit(ws, j, seg, "ada3", i), GU_JOB0[j] + i)
                            act.wait_ge(prod_done, base + f + 1)
                            nc.scalar.activation(act_hi[:, f, :], prod[:, a, :], ACT.Copy).then_inc(act_hi_done, 1)
                    segments(act, j, gu)
                    if j == 0:
                        w_split(unit_at(ws, "out0", 0), DK)
                        copy_job(unit_at(ws, "ada_15", JOB_U - 1), 15)

                    def down(i, last=False, j=j):
                        for a in range(2):
                            w_split(unit_at(ws, f"out{j}", 2 * a + 1, i, 4, KT // 2 - 1), DK)
                            if not (last and a == 1):
                                w_split(next_down(j, i, a), DK)
                            square_out(j, 2 * i + a, a)
                    with act.Fori(0, KT // 2 - 1) as i:
                        down(i)
                    warm_sqrt(j)
                    down(KT // 2 - 1, last=True)
                else:
                    if kind == "c":
                        w_split(unit_at(ws, "qkv4", 0), KT)
                        act.wait_ge(fl_done, 2)
                        nc.scalar.activation(e_t[:], e_t[:], ACT.Exp).then_inc(fl_act, 1)
                        act.wait_ge(fl_done, 3)
                        nc.scalar.activation(l_t[:], u_t[:], ACT.Ln).then_inc(fl_act, 1)

                    def empty_forget():
                        for n, (dst, k) in enumerate(((lf_nat, 0), (dqT, 1))):
                            act.wait_ge(fl_ps, 2 + n)
                            nc.scalar.activation(dst[:, 0:QT, :], ps_s[:, k, 0:64].rearrange("p (t h) -> p t h", h=16),
                                                 ACT.Copy).then_inc(fl_act, 1)
                            nc.scalar.activation(dst[0:DEC, QT, :], ps_s[0:DEC, k, 64:80], ACT.Copy).then_inc(fl_act, 1)
                    stages(act, kind, stage, empty_forget if kind == "c" else None)
                    if kind == "ab":
                        act.wait_ge(b_sq_done, 20)
                        act.wait_ge(b_inv, 1)
                        nc.scalar.activation(b_sq[:].rearrange("p h t -> p (h t)"), b_sq[:].rearrange("p h t -> p (h t)"),
                                             ACT.Sqrt, scale=1.0 / P, bias=eps[:, 0:1]).then_inc(b_std, 1)
                        for hd in range(4):
                            act.wait_ge(ot_ps, 20 + 2 * hd + 1)
                            nc.scalar.activation(o_hi[:, 4 + hd, 0:SEQ], ps_s[:, 0, :], ACT.Copy).then_inc(o_hi_done, 1)
                            act.wait_ge(ot_ps, 20 + 2 * hd + 2)
                            nc.scalar.activation(o_hi[:, 4 + hd, SEQ:TOK], ps_s[:, 1, 0:DEC], ACT.Copy)\
                                .then_inc(o_hi_done, 1)
                    w_split(unit_at(ws, f"out{j}", 0), KT)
                    for m in range(KT):
                        if m + 1 < KT:
                            w_split(unit_at(ws, f"out{j}", m + 1), KT)
                        if m == 6:
                            warm_sqrt(j)
                        square_out(j, m, m % 2)
                std(2 * j + 2)
                if j + 1 < NSUB:
                    pre_norm(j + 1, lambda j=j: w_split(first_of(j + 1), KT))
            for n in range(0, 2 * QT + 2, 2):
                r = rows(n // 2)
                act.wait_ge(nat_ps, n + 1)
                nc.scalar.activation(x_nat[0:r, n // 2, 0:SEQ], lin[0:r, n % 4, :], ACT.Copy).then_inc(nat_a, 1)

        @block.vector
        def _(dve):
            def w_split(u, tiles):
                dve.wait_ge(hi_done, u["idx"] + 1)
                nc.vector.tensor_tensor(w_lo[:, u["hl"], 0:tiles, :], raw[:, u["slot"], 0:tiles, :],
                                        w_hi[:, u["hl"], 0:tiles, :].bitcast(F32), ALU.subtract).then_inc(lo_done, 1)

            coef_n = [0]

            def step(ins):
                ins.then_inc(coef, 1)
                coef_n[0] += 1
                dve.wait_ge(coef, coef_n[0])

            def bias(j, c, n):
                f0 = (3 * (j % 3) + c) * KT
                return ada_b[:, j // 3, f0:f0 + n].rearrange("p (k o) -> p k o", o=1).broadcast_to([P, n, 2])

            def gain(a, j):
                return norms[:, a, j, :].rearrange("p (k o) -> p k o", o=1).broadcast_to([P, KT, 2])

            def coef_in(j):
                dve.wait_ge(mod_turned, j + 1)
                dve.wait_ge(h_hi_done, 8 * j)
                src = mod_ps[:, 8:24, :] if j > 0 else mod_ps0
                step(nc.vector.tensor_tensor(co_tmp[:], src, bias(j, 0, 16), ALU.add))
                step(nc.vector.tensor_copy(co_shift[:], co_tmp[:, 0:KT, :]))
                step(nc.vector.scalar_tensor_tensor(co_scale[:], co_tmp[:, KT:2 * KT, :], 1.0, gain(0, j), ALU.add, ALU.mult))

            def coef_gate(j):
                dve.wait_ge(mod_turned, j + 2)
                src = mod_ps if j + 1 < NSUB else ps_o[:, 0:16].rearrange("p (g q) -> p q g", g=2)
                step(nc.vector.tensor_tensor(co_tmp[:, 0:KT, :], src[:, 0:8, :], bias(j, 2, 8), ALU.add))
                step(nc.vector.scalar_tensor_tensor(co_gate[:], co_tmp[:, 0:KT, :], 1.0, gain(1, j), ALU.add, ALU.mult))
                if KIND[j] == "ffn":
                    step(nc.vector.tensor_scalar(co_gate[:], co_gate[:], 0.5, None, ALU.mult))

            groups = ((0, slice(0, SEQ)), (1, slice(SEQ, TOK)))

            def inverse(n):
                dve.wait_ge(std_done, n)
                nc.vector.reciprocal(rstd[:], rstd[:]).then_inc(rstd_done, 1)
                dve.wait_ge(rstd_done, n)

            def pre_norm(j):
                w_split(first_of(j), KT)
                inverse(2 * j + 1)
                for m in range(KT + 1):
                    if m < KT:
                        if m >= 2:
                            dve.wait_ge(h_lo_done, 8 * j + m - 1)
                        for g, c in groups:
                            i = nc.vector.scalar_tensor_tensor(prod[:, m % 2, c], x[:, m, c], co_scale[:, m, g:g + 1],
                                                               rstd[:, c], ALU.mult, ALU.mult)
                        i.then_inc(t_done, 1)
                    if m > 0:
                        dve.wait_ge(h_hi_done, 8 * j + m)
                        dve.wait_ge(t_done, 8 * j + m)
                        for g, c in groups:
                            i = nc.vector.scalar_tensor_tensor(h_lo[:, m - 1, c], prod[:, (m - 1) % 2, c],
                                                               co_shift[:, m - 1, g:g + 1],
                                                               h_hi[:, m - 1, c].bitcast(F32), ALU.add, ALU.subtract)
                        i.then_inc(h_lo_done, 1)

            def post_norm(j):
                inverse(2 * j + 2)
                for m in range(KT + 1):
                    if m < KT:
                        nc.vector.tensor_tensor(y[:, m, :], y[:, m, :], rstd[:], ALU.mult).then_inc(y_norm, 1)
                    if m > 0:
                        dve.wait_ge(y_norm, 8 * j + m)
                        for g, c in groups:
                            i = nc.vector.scalar_tensor_tensor(x[:, m - 1, c], y[:, m - 1, c], co_gate[:, m - 1, g:g + 1],
                                                               x[:, m - 1, c], ALU.mult, ALU.add)
                        i.then_inc(x_ready, 1)

            def take_out(j, m, a):
                dve.wait_ge(unit_done, take_out.n + 1)
                nc.vector.tensor_copy(two(y[:, m, :]), pair(a)).then_inc(y_copied, 1)
                dve.wait_ge(sq_done, sq_base[j] + m + 1)
                dve.wait_ge(sq_added, 9 * j + 1 + m)
                nc.vector.tensor_tensor(sq_sum[:], sq_sum[:], work[:, a, :], ALU.add).then_inc(sq_added, 1)

            dve.wait_ge(silu_c_done, 1)
            nc.vector.tensor_copy(norms[:].rearrange("p a s k -> p (a s k)"), ps_s[:, 0, 16:112]).then_inc(vec_const, 1)
            dve.wait_ge(const_tr, 2)
            nc.vector.tensor_copy(ada_b[:].rearrange("p l f -> p (l f)"), ps_s[:, 1, 0:144]).then_inc(vec_const, 1)
            dve.wait_ge(vec_const, 2)
            for m in range(KT):
                dve.wait_ge(xt_ps, m + 1)
                nc.vector.tensor_copy(x[:, m, 0:SEQ], lin[:, 2 * (m % 2), :])
                nc.vector.tensor_copy(x[:, m, SEQ:TOK], lin[:, 2 * (m % 2) + 1, 0:DEC]).then_inc(x_ready, 1)
            dve.wait_ge(lam_landed, 32)
            lam_p = prod[:, 0, 0:2 * HD].rearrange("p (a d) -> p a d", a=2)
            nc.vector.tensor_tensor(lam_p, lam_in[:, 0:4:2, :], lam_in[:, 1:4:2, :], ALU.mult).then_inc(lam_done, 1)
            dve.wait_ge(lam_done, 1)
            nc.vector.tensor_reduce(lam[:, 0:2], lam_p, AX.X, ALU.add).then_inc(lam_done, 1)
            dve.wait_ge(lam_done, 3)
            step(nc.vector.tensor_tensor(lam[:, 4:5], lam[:, 3:4], lam[:, 2:3], ALU.subtract))
            step(nc.vector.tensor_scalar(lam[:, 7:8], lam[:, 4:5], -LAM_INIT, None, ALU.add))
            step(nc.vector.tensor_scalar(sub_g[:], sub_g[:], 1.0 - LAM_INIT, None, ALU.mult))
            dve.wait_ge(rel_dram, 16)
            nc.vector.tensor_copy(rel_rev[:, P - 1:3 * P], rel_in[:, ::-1]).then_inc(rel_done, 1)
            nc.vector.tensor_copy(rel_rev[:, 0:P - 1], rel_in[:, 2 * REL:2 * REL + 1].broadcast_to([8, P - 1]))\
                .then_inc(rel_done, 1)
            coef_in(0)
            pre_norm(0)

            def stage(st):
                order, att = st.order, st.att
                lag = 3 if att == "b" else 2

                def add_bias(j):
                    t, hh = order[j]
                    r, n = rows(t), keys(t)
                    dst = probs[0:r, j % PSLOTS, :]
                    src = ps_s[0:r, j % 2, :]
                    dve.wait_ge(s_ps, st.at("s") + j + 1)
                    if j >= PSLOTS and (att != "b" or j % 2 == 0):
                        at = j - PSLOTS + lag + (att == "b")
                        dve.wait_ge(tr_ps, st.at("tr") + tr_plan(st).index((at, "probs")) + 1)
                    if att == "a":
                        hd = 2 * st.tile_of(-1) + hh
                        near = 2 * P if 0 < t < QT else P if t == 0 else P + DEC
                        if n > near:
                            nc.vector.tensor_scalar(dst[:, 0:n - near], src[:, 0:n - near], rel_bias[0:r, hd, 0:1],
                                                    None, ALU.add)
                        lo = 0 if t else P
                        i = nc.vector.tensor_tensor(dst[:, n - near:n], src[:, n - near:n],
                                                    rel_bias[0:r, hd, lo:lo + near], ALU.add)
                    elif att == "b":
                        d0 = SEQ - P - (t * P if t < QT else PAST)
                        i = nc.vector.scalar_tensor_tensor(dst[:, 0:n], dist[0:r, d0:d0 + n],
                                                           neg_slope[0:r, bass.ds(st.tile_of(-1), 1)],
                                                           src[:, 0:n], ALU.mult, ALU.add)
                    else:
                        hd = 2 * st.tile_of(-1) + hh
                        k0 = 0 if t < QT else SEQ
                        if j == 0:
                            dve.wait_ge(dk_in[st.par], 32 * (st.same_att - 3))
                        i = nc.vector.scalar_tensor_tensor(dst[:, 0:n], src[:, 0:n], dqT[0:r, t, bass.ds(hd, 1)],
                                                           dk_b[0:r, st.par, hh, k0:k0 + n], ALU.add, ALU.subtract)
                    i.then_inc(s_added, 1)
                    dve.wait_ge(s_added, st.at("s") + j + 1)
                    if att == "c":
                        nc.vector.tensor_tensor(dst[:, n - r:n], dst[:, n - r:n], causal[0:r, 0:r], ALU.add)\
                            .then_inc(masked, 1)
                        dve.wait_ge(masked, st.at("s") - off["c"]["s"] + j + 1)
                    nc.vector.tensor_reduce(neg_max[0:r, j:j + 1], dst[:, 0:n], AX.X, ALU.max, negate=True)\
                        .then_inc(s_maxed, 1)

                def invert(j):
                    r = rows(order[j][0])
                    dve.wait_ge(exp_done, st.at("s") + j + 1)
                    nc.vector.reciprocal(row_inv[0:r, j:j + 1], row_sum[0:r, j:j + 1]).then_inc(inv_done, 1)

                def combine(q):
                    t = order[2 * q][0]
                    r, n = rows(t), keys(t)
                    a, b = (2 * q) % PSLOTS, (2 * q + 1) % PSLOTS
                    dve.wait_ge(inv_done, st.at("s") + 2 * q + 2)
                    nc.vector.tensor_scalar(probs[0:r, b, 0:n], probs[0:r, b, 0:n], row_inv[0:r, 2 * q + 1:2 * q + 2],
                                            lam[0:r, 7:8], ALU.mult, ALU.mult).then_inc(comb_half, 1)
                    dve.wait_ge(comb_half, st.at("comb") + q + 1)
                    nc.vector.scalar_tensor_tensor(probs[0:r, a, 0:n], probs[0:r, a, 0:n], row_inv[0:r, 2 * q:2 * q + 1],
                                                   probs[0:r, b, 0:n], ALU.mult, ALU.add).then_inc(comb_done, 1)

                def take(j, q):
                    t, hh = order[j]
                    r = rows(t)
                    dve.wait_ge(pv_done, st.at("pv") + q + 1)
                    if att == "b":
                        nc.vector.tensor_copy(b_nat[0:r, st.tile_of(-1), t, :], ps_o[0:r, (q % 2) * P:(q % 2) * P + P])\
                            .then_inc(o_read, 1)
                        return
                    nq = q // 2
                    if nq >= 2:
                        dve.wait_ge(ot_ps, st.at("ot") + nq - 1)
                    dve.wait_ge(inv_done, st.at("s") + j + 1)
                    nc.vector.tensor_scalar(o_nat[0:r, nq % 2, HD * hh:HD * hh + HD],
                                            ps_o[0:r, (q % 2) * P:(q % 2) * P + HD], row_inv[0:r, j:j + 1],
                                            None, ALU.mult).then_inc(o_read, 1)

                def out_lo(q):
                    t = order[2 * q][0]
                    r = rows(t)
                    dve.wait_ge(o_hi_done, st.at("ot") + q + 1)
                    c = slice(t * P, t * P + r)
                    nc.vector.tensor_tensor(o_lo[:, st.tile_of(-1), c], ps_o[:, (2 + q % 2) * P:(2 + q % 2) * P + r],
                                            o_hi[:, st.tile_of(-1), c].bitcast(F32), ALU.subtract).then_inc(o_lo_done, 1)

                lag = 3 if att == "b" else 2
                for s in range(STEPS + 2):
                    if st.new is not None:
                        if s in (0, 4):
                            w_split(st.unit(s // 4 + 1), KT)
                        if s == 8:
                            nxt = next_unit(st)
                            if nxt is not None:
                                w_split(nxt, KT)
                    if att is None:
                        continue
                    j = s - 2
                    if 0 <= j < 10:
                        invert(j)
                        if att == "b" and j % 2:
                            combine(j // 2)
                    j = s - lag - 2
                    if att != "b" and 0 <= j < 10 and j % 2:
                        out_lo(j // 2)
                    j = s - lag - 1
                    if 0 <= j < 10 and (att != "b" or j % 2):
                        take(j, j // 2 if att == "b" else j)
                    if s < 10:
                        add_bias(s)

            def forget_gate():
                count = [0]

                def fl(ins, wait=True):
                    count[0] += 1
                    ins.then_inc(fl_done, 1)
                    if wait:
                        dve.wait_ge(fl_done, count[0])
                dve.wait_ge(fl_in, 32)
                dve.wait_ge(unit_done, unit_at(ws, "forget", 0)["n"] + 1)
                fl(nc.vector.tensor_scalar(two(z_t[:]), pair(1)[0:16], bf_col[:, 0:1], None, ALU.add))
                fl(nc.vector.scalar_tensor_tensor(e_t[:], z_t[:], -1.0, z_t[:], ALU.mult, ALU.min))
                dve.wait_ge(fl_act, 1)
                fl(nc.vector.tensor_scalar(u_t[:], e_t[:], 1.0, None, ALU.add))
                fl(nc.vector.scalar_tensor_tensor(logf[:], u_t[:], -1.0, e_t[:], ALU.add, ALU.subtract))
                dve.wait_ge(fl_act, 2)
                fl(nc.vector.reciprocal(u_t[:], u_t[:]))
                fl(nc.vector.tensor_tensor(logf[:], logf[:], u_t[:], ALU.mult))
                fl(nc.vector.tensor_tensor(l_t[:], l_t[:], logf[:], ALU.subtract))
                fl(nc.vector.scalar_tensor_tensor(logf[:], z_t[:], 0.0, l_t[:], ALU.min, ALU.subtract))
                fl(nc.vector.memset(ones16[:], 1.0))
                fl(nc.vector.tensor_tensor_scan(decay[:, 0:SEQ], ones16[:, 0:SEQ], logf[:, 0:SEQ], 0.0,
                                                ALU.mult, ALU.add), False)
                fl(nc.vector.tensor_tensor_scan(decay[:, SEQ + PAST:], ones16[:, 0:DEC], logf[:, SEQ:TOK], 0.0,
                                                ALU.mult, ALU.add), False)
                dve.wait_ge(fl_ps, 1)
                fl(nc.vector.tensor_tensor_scan(decay[:, SEQ:SEQ + PAST], ones16[:, 0:PAST], ps_t[0:16, 0:PAST], 0.0,
                                                ALU.mult, ALU.add))
                fl(nc.vector.tensor_copy(l_t[:, 0:1], decay[:, SEQ + PAST - 1:SEQ + PAST]))
                fl(nc.vector.tensor_scalar(decay[:, SEQ:SEQ + PAST], decay[:, SEQ:SEQ + PAST], l_t[:, 0:1], None,
                                           ALU.subtract))
                assert count[0] == FL_DECAY

            def coefs_after(j):
                if j + 1 < NSUB:
                    coef_in(j + 1)
                coef_gate(j)

            for j, kind in enumerate(KIND):
                if kind == "ffn":
                    base = FT * ffn_index(j)

                    def gu(seg, i, t0, last, j=j, base=base):
                        for a in range(2):
                            f = 2 * (i + t0) + a
                            u = gu_unit(ws, j, seg, f"up{a}", i)
                            w_split(u, KT)
                            after_up(w_split, j, seg, i, a, last)
                            dve.wait_ge(gate_read, base + f + 1)
                            dve.wait_ge(unit_done, u["n"] + 1)
                            dve.wait_ge(act_lo_done, base + f)
                            nc.vector.tensor_tensor(two(prod[:, a, :]), two(work[:, a, :]), pair(1), ALU.mult)\
                                .then_inc(prod_done, 1)
                            dve.wait_ge(act_hi_done, base + f + 1)
                            dve.wait_ge(prod_done, base + f + 1)
                            nc.vector.tensor_tensor(act_lo[:, f, :], prod[:, a, :], act_hi[:, f, :].bitcast(F32),
                                                    ALU.subtract).then_inc(act_lo_done, 1)
                    segments(dve, j, gu)
                    if j == 0:
                        w_split(unit_at(ws, f"out{j}", 0), DK)
                    coefs_after(j)
                    nc.vector.memset(sq_sum[:], 0.0).then_inc(sq_added, 1)
                    if j == 0:
                        nc.vector.memset(co_tmp[:], 0.0).then_inc(y_copied, 1)

                    def down(i, last=False, j=j):
                        for a in range(2):
                            u = unit_at(ws, f"out{j}", 2 * a + 1, i, 4, KT // 2 - 1)
                            w_split(u, DK)
                            if not (last and a == 1):
                                w_split(next_down(j, i, a), DK)
                            take_out.n = u["n"]
                            take_out(j, 2 * i + a, a)
                    with dve.Fori(0, KT // 2 - 1) as i:
                        down(i)
                    down(KT // 2 - 1, last=True)
                else:
                    if kind == "ab":
                        dve.wait_ge(rel_loaded, 16 * 8)
                        dve.wait_ge(pool_const, 11)
                        step(nc.vector.memset(rel_bias[0:HD, :, 2 * P - HD:2 * P], NEG))
                        step(nc.vector.tensor_copy(dist[:], dist_i[:]))
                        step(nc.vector.scalar_tensor_tensor(dist[:], dist[:], -1.0, dist[:], ALU.mult, ALU.max))
                        step(nc.vector.memset(dist[0:HD, SEQ - HD:SEQ], 1e35))
                        nc.vector.memset(b_sq[:], 1.0).then_inc(b_inv, 1)
                        dve.wait_ge(b_inv, 1)
                    else:
                        w_split(unit_at(ws, "qkv4", 0), KT)
                        forget_gate()
                    stages(dve, kind, stage)
                    if kind == "ab":
                        dve.wait_ge(b_std, 1)
                        nc.vector.reciprocal(b_sq[:].rearrange("p h t -> p (h t)"), b_sq[:].rearrange("p h t -> p (h t)"))\
                            .then_inc(b_inv, 1)
                        dve.wait_ge(b_inv, 2)
                        for hd in range(5):
                            if hd < 4:
                                for t in range(QT + 1):
                                    r = rows(t)
                                    i = nc.vector.scalar_tensor_tensor(b_nat[0:r, hd, t, :], b_nat[0:r, hd, t, :],
                                                                       b_sq[0:r, hd, t:t + 1], sub_g[0:r, :],
                                                                       ALU.mult, ALU.mult)
                                i.then_inc(b_scaled, 1)
                            if hd > 0:
                                p = hd - 1
                                dve.wait_ge(o_hi_done, 20 + 2 * p + 1)
                                nc.vector.tensor_tensor(o_lo[:, 4 + p, 0:SEQ], ps_s[:, 0, :],
                                                        o_hi[:, 4 + p, 0:SEQ].bitcast(F32), ALU.subtract)\
                                    .then_inc(o_lo_done, 1)
                                dve.wait_ge(o_hi_done, 20 + 2 * p + 2)
                                nc.vector.tensor_tensor(o_lo[:, 4 + p, SEQ:TOK], ps_s[:, 1, 0:DEC],
                                                        o_hi[:, 4 + p, SEQ:TOK].bitcast(F32), ALU.subtract)\
                                    .then_inc(o_lo_done, 1)
                    w_split(unit_at(ws, f"out{j}", 0), KT)
                    coefs_after(j)
                    nc.vector.memset(sq_sum[:], 0.0).then_inc(sq_added, 1)
                    for m in range(KT):
                        if m + 1 < KT:
                            w_split(unit_at(ws, f"out{j}", m + 1), KT)
                        take_out.n = unit_at(ws, f"out{j}", m)["n"]
                        take_out(j, m, m % 2)
                post_norm(j)
                if j + 1 < NSUB:
                    pre_norm(j + 1)
            for n in range(1, 2 * QT + 2, 2):
                r = rows(n // 2)
                dve.wait_ge(nat_ps, n + 1)
                dve.wait_ge(nat_a, n // 2 + 1)
                nc.vector.tensor_copy(x_nat[0:r, n // 2, SEQ:DM], lin[0:r, n % 4, :]).then_inc(nat_out, 2)


_INS = ["x_prompt", "x_sample", "c_prompt", "c_sample", "cache_a_k", "cache_a_v", "cache_b_k", "cache_b_v",
        "cache_c_k", "cache_c_v", "cache_c_logf", "w_ada", "b_ada", "norm_pre", "norm_post", "ffn_w_gate",
        "ffn_w_up", "ffn_w_down", "w_in_ab", "w_out_ab", "relpos_a", "lambda_b", "subln_b", "w_in_c", "b_f",
        "w_out_c"]
_OUTS = [(1, SEQ, DM), (1, DEC, DM),
         (1, 1, SEQ, 8, HD), (1, 1, SEQ, 8, HD), (1, 1, SEQ, 4, 2 * HD), (1, 1, SEQ, 4, 2 * HD),
         (1, 1, SEQ, 16, HD), (1, 1, SEQ, 16, HD), (1, 1, SEQ, 16),
         (1, 1, DEC, 8, HD), (1, 1, DEC, 8, HD), (1, 1, DEC, 4, 2 * HD), (1, 1, DEC, 4, 2 * HD),
         (1, 1, DEC, 16, HD), (1, 1, DEC, 16, HD), (1, 1, DEC, 16)]


def kernel(**inputs):
    import concourse.bacc as bacc
    from concourse.bass_utils import run_bass_kernel_spmd

    nc = bacc.Bacc("TRN2", target_bir_lowering=False, num_devices=1)
    arrays, ins = {}, []
    for name in _INS:
        a = np.ascontiguousarray(inputs[name])
        arrays[f"in_{name}"] = a
        ins.append(nc.dram_tensor(f"in_{name}", a.shape, mybir.dt.from_np(a.dtype), kind="ExternalInput").ap())
    outs = [nc.dram_tensor(f"out_{i}", shape, F32, kind="ExternalOutput").ap() for i, shape in enumerate(_OUTS)]
    program(nc, ins, outs)
    r = run_bass_kernel_spmd(nc, [arrays], core_ids=[0])
    return tuple(r.results[0][f"out_{i}"] for i in range(len(_OUTS)))
```

```python
from contextlib import ExitStack

import numpy as np

import concourse.bass as bass
from concourse import mybir

F32 = mybir.dt.float32
F32R = mybir.dt.float32r
I32 = mybir.dt.int32
ALU = mybir.AluOpType
ACT = mybir.ActivationFunctionType
AX = mybir.AxisListType

P = 128
DM = 1024
KT = DM // P
SEQ, DEC, PAST = 512, 32, 256
TOK = SEQ + DEC
HALF = TOK // 2
QT = SEQ // P
D_FF = 2816
FT = D_FF // P
DK = FT // 2
HD = 64
REL = 128
NSUB = 6
EPS = 1e-6
NEG = -1e30
LAM_INIT = 0.2
PSLOTS = 4
POOL_Y = (2, 3, 4, 6)
POOL_X = (4, 6)
POOL_H = (1, 3, 5)
NRAW, NHL = 4, 2
KIND = ["ffn", "ab", "ffn", "ffn", "c", "ffn"]
JOB = 512
JOB_U = 4
JOBS = 2 * 9 * DM // JOB
FIRST_JOBS = 2 * DM // JOB
GU_TRIPS = {0: (10, 1), 2: (6, 5), 3: (6, 5), 5: (0, 11)}
GU_JOB0 = {0: 4, 2: 18, 3: 26, 5: 36}
ACC0 = {0: 0, 2: 10, 3: 16}
GAP_JOBS = 2
GAP_JOB0 = {0: 14, 1: 16, 2: 24, 3: 32, 4: 34}
TRIP = {True: ["gate0", "up0", "ada0", "ada1", "gate1", "ada2", "up1", "ada3"],
        False: ["gate0", "up0", "gate1", "up1"]}
FL_DECAY = 14
STEPS = 14
LIN_STEPS = 12


class Stream:

    def __init__(self):
        self.units = []
        self.used = [0] * NRAW
        self.last = [None] * NRAW
        self.split = 0
        self.done = 0
        self.acc = 0
        self.first = {}

    def add(self, name, n, split=True, ring=NRAW, acc=False, counted=True):
        self.first[name] = len(self.units)
        for k in range(n):
            slot = k % ring if ring != NRAW else (self.start + k) % NRAW
            self.used[slot] += 1
            self.acc += acc
            self.units.append(dict(slot=slot, use=self.used[slot], idx=self.split if split else None,
                                   done=self.done, acc=4 * self.acc if acc else None, prev=self.last[slot]))
            self.last[slot] = len(self.units) - 1
            self.split += split
            self.done += counted
        if ring == NRAW:
            self.start = (self.start + n) % NRAW

    start = 0


def plan():
    s = Stream()
    s.add("ada_start", JOB_U * FIRST_JOBS, split=False)
    for j, kind in enumerate(KIND):
        if kind == "ffn":
            for seg, job in enumerate((True, False)):
                for t in range(GU_TRIPS[j][seg]):
                    for name in TRIP[job]:
                        ada = name.startswith("ada")
                        s.add(f"gu{j}_{seg}_{t}_{name}", 1, split=not ada, acc=ada, counted=not ada or name == "ada3")
            s.add(f"out{j}", 2 * KT)
        else:
            if kind == "c":
                s.add("forget", 1)
            s.add(f"qkv{j}", 3 * KT, ring=3)
            s.add(f"out{j}", KT)
        if j + 1 < NSUB:
            s.add(f"gap{j}", JOB_U * GAP_JOBS, split=False)
    return s


def unit_at(s, run, k, i=None, step=0, count=1):
    n = (s.first[run] if isinstance(run, str) else run) + k

    def hl_free(m):
        idx = s.units[m]["idx"]
        if idx is None or idx < NHL:
            return 0
        return 1 + next(s.units[q]["done"] for q in range(m, -1, -1) if s.units[q]["idx"] == idx - NHL)

    def raw_free(m):
        if s.units[m]["prev"] is None:
            return 0, 0, 0
        prev = s.units[s.units[m]["prev"]]
        if prev["acc"] is not None:
            return 0, 0, prev["acc"]
        return (prev["done"] + 1, 0, 0) if prev["idx"] is None else (0, prev["idx"] + 1, 0)

    if i is None or isinstance(i, int):
        trips, i = [n + step * (i or 0)], 0
    else:
        trips = [n + step * t for t in range(count)]
    us = [s.units[m] for m in trips]

    def line(values, exact=True):
        slope = values[-1] - values[-2] if len(values) > 1 else 0
        if exact:
            assert all(v == values[0] + slope * t for t, v in enumerate(values))
            return values[0] + slope * i
        slope = max(0, slope)
        return max(0, max(v - slope * t for t, v in enumerate(values))) + slope * i if any(values) else 0

    slot, idx = us[0]["slot"], us[0]["idx"]
    assert all(u["slot"] == slot for u in us)
    assert idx is None or all(u["idx"] % NHL == idx % NHL for u in us)
    return dict(n=line([u["done"] for u in us]), slot=slot, landed=line([16 * u["use"] for u in us]),
                idx=None if idx is None else line([u["idx"] for u in us]), hl=None if idx is None else idx % NHL,
                raw_free=tuple(line(v, False) for v in zip(*map(raw_free, trips))),
                hl_free=line(list(map(hl_free, trips)), False))


def gu_unit(s, j, seg, name, i, more=0):
    trip = TRIP[seg == 0]
    first = s.first[f"gu{j}_{seg}_0_{name}"] + more
    return unit_at(s, first, 0, i, len(trip), GU_TRIPS[j][seg] - 1)


def program(nc, ins, outs):
    (x_prompt, x_sample, c_prompt, c_sample, ca_k, ca_v, cb_k, cb_v, cc_k, cc_v, cc_logf,
     w_ada, b_ada, norm_pre, norm_post, ffn_wg, ffn_wu, ffn_wd, w_in_ab, w_out_ab, relpos,
     lambda_b, subln_b, w_in_c, b_f, w_out_c) = ins
    (y_p, y_s, pa_k, pa_v, pb_k, pb_v, pc_k, pc_v, pc_lf, sa_k, sa_v, sb_k, sb_v, sc_k, sc_v, sc_lf) = outs
    ws = plan()

    def colblocks(w):
        return w.rearrange("(k p) (f n) -> f p k n", p=P, n=P)

    ada_d = [w_ada[l].rearrange("(u k p) (c n) -> c u p k n", p=P, n=JOB, k=2) for l in range(2)]
    mod_dram = nc.dram_tensor("mod_rows", (2, JOBS * JOB), F32, kind="Internal").ap()
    gate_d = {j: colblocks(ffn_wg[j // 3, (j % 3) // 2]) for j in (0, 2, 3, 5)}
    up_d = {j: colblocks(ffn_wu[j // 3, (j % 3) // 2]) for j in (0, 2, 3, 5)}
    down_d = {j: ffn_wd[j // 3, (j % 3) // 2].rearrange("(h k p) (m n) -> m h p k n", p=P, n=P, h=2)
              for j in (0, 2, 3, 5)}
    inab_d = colblocks(w_in_ab[0])
    outab_d = colblocks(w_out_ab[0])
    inc_d = colblocks(w_in_c[0][:, 0:3 * DM])
    wfl_d = w_in_c[0][:, 3 * DM:3 * DM + 16].rearrange("(k p) n -> p k n", p=P)
    outc_d = colblocks(w_out_c[0])
    rel_scratch = nc.dram_tensor("rel_scratch", (8, P, 384), F32, kind="Internal").ap()
    dec_scratch = nc.dram_tensor("decay_scratch", (16, SEQ + PAST + DEC), F32, kind="Internal").ap()

    def tokcols(prompt, sample):
        p = prompt.rearrange("(t q) (f n) -> f q t n", q=P, n=P)
        s = sample.rearrange("q (f n) -> f q n", n=P)
        return p, s

    def flat(a):
        return a[0, 0].rearrange("t h d -> t (h d)")

    kv_out = {"a": (tokcols(flat(pa_k), flat(sa_k)), tokcols(flat(pa_v), flat(sa_v))),
              "b": (tokcols(flat(pb_k), flat(sb_k)), tokcols(flat(pb_v), flat(sb_v))),
              "c": (tokcols(flat(pc_k), flat(sc_k)), tokcols(flat(pc_v), flat(sc_v)))}
    cache_in = {n: [flat(a).rearrange("(t q) (f n) -> f q t n", q=P, n=P) for a in kv]
                for n, kv in (("a", (ca_k, ca_v)), ("b", (cb_k, cb_v)), ("c", (cc_k, cc_v)))}

    with ExitStack() as ctx:
        def sem(name):
            return ctx.enter_context(nc.semaphore(name))

        cursor = [((nc.sbuf_base + 63) // 64) * 64]

        def sb_at(name, shape, dt, offset):
            return nc.alloc_sbuf_tensor_at(name, shape, dt, offset=offset)

        def size(shape):
            return int(np.prod(shape[1:])) * 4

        def sb(name, shape, dt=F32):
            t = sb_at(name, shape, dt, cursor[0])
            cursor[0] += (size(shape) + 31) // 32 * 32
            return t

        raw = sb("raw", [P, NRAW, DK, P])
        w_hi = sb("w_hi", [P, NHL, DK, P], F32R)
        w_lo = sb("w_lo", [P, NHL, DK, P], F32R)
        x = sb("x", [P, KT, TOK])
        h_at = cursor[0]
        h_hi = sb("h_hi", [P, KT, TOK], F32R)
        h_lo = sb("h_lo", [P, KT, TOK], F32R)
        y = sb_at("y", [P, KT, TOK], F32, h_at)
        work = sb("work", [P, 2, TOK])
        prod = sb("prod", [P, 2, TOK])
        acc_at = cursor[0]
        sq_sum = sb("sq_sum", [P, TOK])
        rstd = sb("rstd", [P, TOK])
        acc = sb_at("acc", [P, 2, JOB], F32, acc_at)
        ident = sb("ident", [P, P])
        pick = sb("pick", [P, 4])
        mean_w = sb("mean_w", [P, P])
        causal = sb("causal", [P, P])
        eps = sb("eps", [P, 1])
        warm = sb("warm", [P, NSUB + 1])
        silu_c = sb("silu_c", [P, KT, 2])
        mod_out = sb("mod_out", [2, JOB])
        mod_in = sb("mod_in", [48, P])
        norms = sb("norms", [P, 2, NSUB, KT])
        ada_b = sb("ada_b", [P, 2, 9 * KT])
        co_scale = sb("co_scale", [P, KT, 2])
        co_shift = sb("co_shift", [P, KT, 2])
        co_gate = sb("co_gate", [P, KT, 2])
        co_tmp = sb("co_tmp", [P, 2 * KT, 2])
        neg_max = sb("neg_max", [P, 10])
        row_sum = sb("row_sum", [P, 10])
        row_inv = sb("row_inv", [P, 10])
        neg_slope = sb("neg_slope", [P, 4])
        lam = sb("lam", [P, 8])
        sub_g = sb("sub_g", [P, P])
        b_sq = sb("b_sq", [P, 4, QT + 1])
        union = cursor[0]
        act_hi = sb("act_hi", [P, FT, TOK], F32R)
        act_lo = sb("act_lo", [P, FT, TOK], F32R)
        end = cursor[0]
        assert end <= nc.sbuf_usable_end, (end, nc.sbuf_usable_end)

        x_nat = sb_at("x_nat", [P, QT + 1, DM], F32, union)
        rows_at = union + size([1, QT + 1, DM])
        c_rows = sb_at("c_rows", [16, P], F32, rows_at)
        norm_rows = sb_at("norm_rows", [96, P], F32, rows_at + 512)
        ada_rows = sb_at("ada_rows", [72, 2, P], F32, rows_at + 1024)
        lam_in = sb_at("lam_in", [P, 4, HD], F32, rows_at + 2048)
        rel_in = sb_at("rel_in", [8, 257], F32, rows_at + 3072)
        rel_rev = sb_at("rel_rev", [8, 384], F32, rows_at + 3072 + 1056)

        cursor[0] = union
        o_hi = sb("o_hi", [P, KT, TOK], F32R)
        o_lo = sb("o_lo", [P, KT, TOK], F32R)
        qT = sb("qT", [P, 2, TOK])
        kT = sb("kT", [P, 2, TOK])
        vT = sb("vT", [P, TOK])
        k_nat = sb("k_nat", [P, 2, QT + 1, P])
        v_nat = sb("v_nat", [P, 2, QT + 1, P])
        ck_nat = sb("ck_nat", [P, 2, 2, P])
        cv_nat = sb("cv_nat", [P, 2, 2, P])
        ckT = sb("ckT", [P, 2, PAST])
        probs = sb("probs", [P, PSLOTS, SEQ])
        probsT = sb("probsT", [P, 2, QT, P])
        o_nat = sb("o_nat", [P, 2, P])
        mixer_top = cursor[0]
        rel_bias = sb("rel_bias", [P, 8, 2 * P])
        dist = sb("dist", [P, SEQ])
        b_nat = sb("b_nat", [P, 4, QT + 1, P])
        assert cursor[0] <= nc.sbuf_usable_end, (cursor[0], end)
        dist_i = sb_at("dist_i", [P, SEQ], I32, mixer_top + 8 * 1024 + 2048)
        cursor[0] = mixer_top
        dk_b = sb("dk_b", [P, 2, 2, SEQ + PAST + DEC])
        dqT = sb("dqT", [P, QT + 1, 16])
        lf_nat = sb("lf_nat", [P, QT + 1, 16])
        clf_nat = sb("clf_nat", [P, 2, 16])
        bf_col = sb("bf_col", [16, 1])
        logf = sb("logf", [16, TOK])
        decay = sb("decay", [16, SEQ + PAST + DEC])
        assert cursor[0] <= nc.sbuf_usable_end, (cursor[0], end)
        z_t = sb_at("z_t", [16, TOK], F32, mixer_top)
        e_t = sb_at("e_t", [16, TOK], F32, mixer_top + 2176)
        u_t = sb_at("u_t", [16, TOK], F32, mixer_top + 2 * 2176)
        l_t = sb_at("l_t", [16, TOK], F32, mixer_top + 3 * 2176)
        ones16 = sb_at("ones16", [16, TOK], F32, mixer_top + 4 * 2176)

        lin = ctx.enter_context(nc.psum_tensor("lin", [P, 4, 512], F32))
        ps_s = ctx.enter_context(nc.psum_tensor("ps_s", [P, 2, 512], F32))
        ps_t = ctx.enter_context(nc.psum_tensor("ps_t", [P, 512], F32))
        ps_o = ctx.enter_context(nc.psum_tensor("ps_o", [P, 512], F32))
        mod_ps = ps_o[:, 0:48].rearrange("p (g q) -> p q g", g=2)
        mod_ps0 = ps_o[:, 0:32].rearrange("p (q g) -> p q g", g=2)

        def pair(a):
            return lin[:, 2 * a:2 * a + 2, 0:HALF]

        def start_bank(n):
            return lin[0:2, n % 2, :]

        def slot4(m):
            return (prod, work)[m % 4 // 2][:, m % 2, :]

        def tiles_of(engine_tiles, m):
            return sum(t <= m for t in engine_tiles)

        def two(ap):
            return ap.rearrange("p (a n) -> p a n", a=2)

        raw_in = [sem(f"raw_in{k}") for k in range(NRAW)]
        unit_done = sem("unit_done")
        hi_done = sem("hi_done")
        hi_half = sem("hi_half")
        lo_done = sem("lo_done")
        const_in = sem("const_in")
        x_in = sem("x_in")
        pool_const = sem("pool_const")
        const_tr = sem("const_tr")
        silu_c_done = sem("silu_c_done")
        vec_const = sem("vec_const")
        xt_ps = sem("xt_ps")
        x_ready = sem("x_ready")
        gate_read = sem("gate_read")
        prod_done = sem("prod_done")
        act_hi_done = sem("act_hi_done")
        act_lo_done = sem("act_lo_done")
        sq_done = sem("sq_done")
        y_copied = sem("y_copied")
        sq_added = sem("sq_added")
        sq_used = sem("sq_used")
        mean_done = sem("mean_done")
        std_done = sem("std_done")
        rstd_done = sem("rstd_done")
        y_norm = sem("y_norm")
        y_norm_p = sem("y_norm_p")
        t_done = sem("t_done")
        t_done_p = sem("t_done_p")
        h_done_p = sem("h_done_p")
        h_done = sem("h_done")
        h_hi_done = sem("h_hi_done")
        h_lo_done = sem("h_lo_done")
        first_turned = sem("first_turned")
        acc_step = sem("acc_step")
        job_copied = sem("job_copied")
        job_stored = sem("job_stored")
        mod_loaded = sem("mod_loaded")
        mod_turned = sem("mod_turned")
        coef = sem("coef")
        kv_evac = sem("kv_evac")
        tr_ps = sem("tr_ps")
        tr_out = sem("tr_out")
        cache_k = [sem(f"cache_k{k}") for k in range(2)]
        cache_v = [sem(f"cache_v{k}") for k in range(2)]
        kv_stored = [sem(f"kv_stored{k}") for k in range(2)]
        lf_stored = sem("lf_stored")
        s_ps = sem("s_ps")
        s_added = sem("s_added")
        s_maxed = sem("s_maxed")
        exp_done = sem("exp_done")
        inv_done = sem("inv_done")
        comb_half = sem("comb_half")
        comb_done = sem("comb_done")
        pt_used = sem("pt_used")
        pv_done = sem("pv_done")
        o_read = sem("o_read")
        ot_ps = sem("ot_ps")
        o_hi_done = sem("o_hi_done")
        o_lo_done = sem("o_lo_done")
        b_sq_done = sem("b_sq_done")
        b_std = sem("b_std")
        b_inv = sem("b_inv")
        b_scaled = sem("b_scaled")
        rel_done = sem("rel_done")
        rel_dram = sem("rel_dram")
        rel_loaded = sem("rel_loaded")
        dist_done = sem("dist_done")
        lam_landed = sem("lam_landed")
        lam_done = sem("lam_done")
        fl_done = sem("fl_done")
        fl_act = sem("fl_act")
        fl_in = sem("fl_in")
        fl_ps = sem("fl_ps")
        fl_dram = sem("fl_dram")
        dk_in = [sem(f"dk_in{k}") for k in range(2)]
        masked = sem("masked")
        settled = sem("settled")
        nat_a = sem("nat_a")
        nat_ps = sem("nat_ps")
        nat_v = sem("nat_v")
        stored = sem("stored")

        block = ctx.enter_context(nc.Block())

        sq_base = [8 + 16 * j for j in range(NSUB)]

        def loop(eng, n, body):
            if n == 1:
                body(0)
            elif n > 1:
                with eng.Fori(0, n) as i:
                    body(i)

        def mixer_counts(kind):
            c = [dict(s=0, tr=0, pv=0, ot=0, comb=0) for _ in range(10)]
            for st in range(9):
                n = dict(c[st])
                k = who(kind, st - 1)
                if st >= 1:
                    n["s"] += 10
                    n["tr"] += 5 if k == "b" else 10
                    n["pv"] += 5 if k == "b" else 10
                    n["ot"] += 0 if k == "b" else 5
                    n["comb"] += 5 if k == "b" else 0
                if st < 8:
                    n["tr"] += 3
                c[st + 1] = n
            return c

        def who(kind, p):
            return "c" if kind == "c" else "ab"[p % 2]

        counts = {k: mixer_counts(k) for k in ("ab", "c")}
        off = {"ab": dict(s=0, tr=0, pv=0, ot=0, comb=0, ev=0), "c": dict(counts["ab"][9])}
        off["c"]["ev"] = 24
        off["c"]["ot"] += 8

        class Stage:

            def __init__(self, kind, st, i=None, trips=1):
                self.kind, self.st, self.i, self.trips = kind, st, i, trips
                self.ii = 0 if i is None else i
                self.att = who(kind, st - 1) if st >= 1 else None
                self.par = (st - 1) % 2 if st >= 1 else None
                self.new = st % 2 if st < 8 else None
                half = 0 if kind == "ab" else 4
                self.same_new = half + st // 2 + self.ii
                self.same_att = half + (st - 1) // 2 + self.ii
                self.order = [(t, hh) for t in (3, 2, 1, 0, QT) for hh in (0, 1)]

            def at(self, key):
                c = counts[self.kind]
                d = c[self.st + 2][key] - c[self.st][key] if self.i is not None else 0
                return off[self.kind][key] + c[self.st][key] + d * self.ii

            def ev(self):
                return off[self.kind]["ev"] + 3 * self.st + 6 * self.ii

            def pairs(self):
                return (0 if self.kind == "ab" else 8) + self.st + 2 * self.ii

            def tile_of(self, p_off):
                p = self.st + p_off
                return (p // 2 if self.kind == "ab" else p) + (1 if self.kind == "ab" else 2) * self.ii

            def unit(self, k):
                run = "qkv1" if self.kind == "ab" else "qkv4"
                if self.i is None:
                    return unit_at(ws, run, 3 * self.st + k)
                return unit_at(ws, run, 3 * self.st + k, self.i, 6, self.trips)

        def stages(eng, kind, emit, after_first=None):
            emit(Stage(kind, 0))
            if after_first is not None:
                after_first()
            with eng.Fori(0, 3) as i:
                emit(Stage(kind, 1, i, 3))
                emit(Stage(kind, 2, i, 3))
            emit(Stage(kind, 7))
            emit(Stage(kind, 8))

        def settle(eng):
            eng.sem_inc(settled, 1)

        def next_unit(st):
            return st.unit(3) if st.st < 7 else None

        def split_next(half_split, st, s):
            if st.kind == "c" and st.i is None and st.st == 0 and s < 2:
                return
            if st.new is not None and s >= 0 and s % 4 < 2 and s < 10:
                u = st.unit(s // 4 + 1) if s < 8 else next_unit(st)
                if u is not None:
                    halves = st.ev() - 2 * (st.kind == "c") + s // 4
                    half_split(u, s % 4, halves)

        def tr_plan(st):
            lag = 3 if st.att == "b" else 2
            found = []
            for s in range(STEPS + 2):
                if st.new is not None and s in (5, 9, 12):
                    found.append((s, "turn"))
                j = s - lag
                if st.att is not None and 0 <= j < 10 and (st.att != "b" or j % 2):
                    found.append((s, "probs"))
            return found

        def ffn_index(j):
            return KIND[:j].count("ffn")

        def segments(eng, j, emit):
            for seg, n in enumerate(GU_TRIPS[j]):
                if n:
                    t0 = GU_TRIPS[j][0] * seg
                    loop(eng, n - 1, lambda i, seg=seg, t0=t0: emit(seg, i, t0, False))
                    emit(seg, n - 1, t0, True)

        def after_up(w_split, j, seg, i, a, last):
            if a == 0:
                w_split(gu_unit(ws, j, seg, "gate1", i), KT)
            elif not last:
                w_split(gu_unit(ws, j, seg, "gate0", i, len(TRIP[seg == 0])), KT)
            elif seg == 0 and GU_TRIPS[j][1]:
                w_split(unit_at(ws, f"gu{j}_1_0_gate0", 0), KT)
            else:
                w_split(unit_at(ws, f"out{j}", 0), DK)

        def first_of(j):
            return first_gu(j) if KIND[j] == "ffn" else unit_at(ws, "forget" if KIND[j] == "c" else f"qkv{j}", 0)

        def first_gu(j):
            seg = 0 if GU_TRIPS[j][0] else 1
            return unit_at(ws, f"gu{j}_{seg}_0_gate0", 0)

        def next_down(j, i, a):
            return unit_at(ws, f"out{j}", 2 * a + 2, i, 4, KT // 2 - 1)

        def by_vector(n):
            return n > QT and (n - QT) % 2 == 0

        def copies_to(n):
            return sum(by_vector(q) == by_vector(n) for q in range(n + 1))

        def keys(t):
            return (t + 1) * P if t < QT else PAST + DEC

        def rows(t):
            return P if t < QT else DEC

        coef_ready = {0: 8}
        for n in range(1, NSUB):
            coef_ready[n] = coef_ready[n - 1] + 3 + (0 if n == 1 else 3 if KIND[n - 2] == "ffn" else 2) \
                + (4 if KIND[n - 1] == "ab" else 0)

        @block.sync
        def _(sp):
            def slot_free(u):
                for signal, value in zip((unit_done, lo_done, acc_step), u["raw_free"]):
                    if not isinstance(value, int) or value > 0:
                        sp.wait_ge(signal, value)

            def load(u, src, tiles, cols=P):
                slot_free(u)
                sp.dma_start(raw[:, u["slot"], 0:tiles, 0:cols], src).then_inc(raw_in[u["slot"]], 16)

            def load_ada(u, layer, job, k):
                slot_free(u)
                sp.dma_start(raw[:, u["slot"], 0:KT, :].rearrange("p (k a) n -> p k (a n)", k=2),
                             ada_d[layer][job, k]).then_inc(raw_in[u["slot"]], 16)

            sp.dma_start(c_rows[0:8, :], c_prompt.rearrange("g (k p) -> (g k) p", p=P)).then_inc(const_in, 16)
            sp.dma_start(c_rows[8:16, :], c_sample.rearrange("g (k p) -> (g k) p", p=P)).then_inc(const_in, 16)
            for k, src in enumerate((norm_pre, norm_post)):
                sp.dma_start(norm_rows[48 * k:48 * k + 48, :],
                             src.rearrange("l s (k p) -> (l s k) p", p=P)).then_inc(const_in, 16)
            for l in range(2):
                sp.dma_start(ada_rows[:, l, :], b_ada[l].rearrange("(f p) -> f p", p=P)).then_inc(const_in, 16)
            sp.dma_start(x_nat[:, 0:QT, :], x_prompt[0].rearrange("(t q) n -> q t n", q=P)).then_inc(x_in, 16)
            sp.dma_start(x_nat[0:DEC, QT, :], x_sample[0]).then_inc(x_in, 16)
            for n in range(FIRST_JOBS):
                for k in range(JOB_U):
                    load_ada(unit_at(ws, "ada_start", JOB_U * n + k), 0, n, k)
            for j, kind in enumerate(KIND):
                if kind == "ffn":
                    for seg, n in enumerate(GU_TRIPS[j]):
                        t0 = GU_TRIPS[j][0] * seg
                        layer, job0 = divmod(GU_JOB0[j], JOBS // 2)
                        assert seg == 1 or job0 + n <= JOBS // 2

                        def gu(i, j=j, t0=t0, seg=seg, job0=job0, layer=layer, n=n):
                            for name in TRIP[seg == 0]:
                                u = unit_at(ws, ws.first[f"gu{j}_{seg}_0_{name}"], 0, i, len(TRIP[seg == 0]), n)
                                if name.startswith("ada"):
                                    load_ada(u, layer, job0 + i, int(name[3]))
                                else:
                                    load(u, (gate_d if name.startswith("gate") else up_d)[j][2 * (t0 + i) + int(name[-1])], KT)
                        loop(sp, n, gu)

                    def down(i, j=j):
                        for k in range(4):
                            load(unit_at(ws, f"out{j}", k, i, 4, KT // 2), down_d[j][2 * i + k // 2, k % 2], DK)
                    loop(sp, KT // 2, down)
                else:
                    if kind == "c":
                        load(unit_at(ws, "forget", 0), wfl_d, KT, 16)

                    def qkv(st):
                        if st.st == 8:
                            return
                        if kind == "ab":
                            first = 12 * (st.new) + st.tile_of(0)
                            blocks = [first + 4, first + 8, first]
                            src = inab_d
                        else:
                            first = st.tile_of(0)
                            blocks = [first + 8, first + 16, first]
                            src = inc_d
                        for k in range(3):
                            load(st.unit(k), src[blocks[k]], KT)
                    stages(sp, kind, qkv)
                    for m in range(KT):
                        load(unit_at(ws, f"out{j}", m), (outab_d if kind == "ab" else outc_d)[m], KT)
                if j + 1 < NSUB:
                    for k in range(JOB_U * GAP_JOBS):
                        if j == 0 and k == JOB_U:
                            sp.wait_ge(rel_dram, 32)
                            sp.wait_ge(mean_done, 2)
                            for hd in range(8):
                                src = bass.AP(rel_scratch.tensor, 384 * P * hd + P - 1, [[384 - 1, P], [1, 2 * P]])
                                sp.dma_start(rel_bias[:, hd, :], src).then_inc(rel_loaded, 16)
                        layer, job = divmod(GAP_JOB0[j] + k // JOB_U, JOBS // 2)
                        load_ada(unit_at(ws, f"gap{j}", k), layer, job, k % JOB_U)
            for n in range(2 * (QT + 1)):
                a, t = divmod(n, QT + 1)
                c = slice(a * SEQ, a * SEQ + DM // 2)
                sp.wait_ge(nat_v if by_vector(n) else nat_a, copies_to(n))
                if t < QT:
                    sp.dma_start(y_p[0, t * P:(t + 1) * P, c], x_nat[:, t, c]).then_inc(stored, 16)
                else:
                    sp.dma_start(y_s[0, :, c], x_nat[0:DEC, t, c]).then_inc(stored, 16)
            sp.wait_ge(stored, 32 * (QT + 1))
            for par in range(2):
                sp.wait_ge(kv_stored[par], 64 * 8)
            sp.wait_ge(lf_stored, 32)

        @block.gpsimd
        def _(pool):
            nc.gpsimd.memset(ident[:], 0.0).then_inc(pool_const, 1)
            nc.gpsimd.memset(mean_w[:], 1.0 / DM).then_inc(pool_const, 1)
            nc.gpsimd.memset(causal[:], 0.0).then_inc(pool_const, 1)
            nc.gpsimd.memset(eps[:], EPS).then_inc(pool_const, 1)
            for h in range(4):
                nc.gpsimd.memset(neg_slope[:, h:h + 1], -(2.0 ** (-8.0 * (h + 1) / 4))).then_inc(pool_const, 1)
            pool.wait_ge(pool_const, 8)
            nc.gpsimd.affine_select(out=ident[:], in_=ident[:], compare_op=ALU.not_equal, fill=1.0, base=0,
                                    pattern=[[-1, P]], channel_multiplier=1).then_inc(pool_const, 1)
            nc.gpsimd.affine_select(out=causal[:], in_=causal[:], compare_op=ALU.is_ge, fill=NEG, base=0,
                                    pattern=[[-1, P]], channel_multiplier=1).then_inc(pool_const, 1)
            pool.dma_start(lam_in[:].rearrange("p a d -> p (a d)"),
                           lambda_b[0].rearrange("(o a) d -> o (a d)", o=1).broadcast_to([P, 4 * HD])).then_inc(lam_landed, 16)
            pool.dma_start(sub_g[:], subln_b[0:1, :].broadcast_to([P, P])).then_inc(lam_landed, 16)
            pool.dma_start(rel_in[:], relpos[0]).then_inc(rel_dram, 16)
            def store_job(job):
                pool.wait_ge(job_copied, job + 1)
                settle(pool)
                pool.dma_start(mod_dram[:, bass.ds(job * JOB, JOB)], mod_out[:, :]).then_inc(job_stored, 16)

            def store_jobs(first, n):
                loop(pool, n, lambda i: store_job(first + i))

            def load_mod(j, last_job):
                pool.wait_ge(job_stored, 16 * (last_job + 1 - FIRST_JOBS))
                pool.wait_ge(mod_turned, j + 1)
                f0, n = 24 * j + 16, 24 if j + 1 < NSUB else 8
                for g in range(2):
                    pool.dma_start(mod_in[g * n:g * n + n, :],
                                   mod_dram[g, f0 * P:(f0 + n) * P].rearrange("(f p) -> f p", p=P)).then_inc(mod_loaded, 16)

            def post_norm(j):
                pool.wait_ge(rstd_done, 2 * j + 2)
                pool.wait_ge(y_copied, 1 + 8 * (j + 1))
                for m in POOL_Y:
                    nc.gpsimd.tensor_tensor(y[:, m, :], y[:, m, :], rstd[:], ALU.mult).then_inc(y_norm_p, 1)

            def pre_norm(j):
                pool.wait_ge(rstd_done, 2 * j + 1)
                pool.wait_ge(coef, coef_ready[j])
                for m in sorted(POOL_X + POOL_H):
                    if m in POOL_X:
                        pool.wait_ge(h_lo_done, 8 * j + m - 3)
                        nc.gpsimd.tensor_tensor(slot4(m), x[:, m, :], rstd[:], ALU.mult).then_inc(t_done_p, 1)
                    else:
                        pool.wait_ge(t_done, (KT - len(POOL_X)) * j + m + 1 - tiles_of(POOL_X, m))
                        h = slot4(m)
                        for g, c in ((0, slice(0, SEQ)), (1, slice(SEQ, TOK))):
                            i = nc.gpsimd.tensor_scalar(h[:, c], h[:, c], co_scale[:, m, g:g + 1],
                                                        co_shift[:, m, g:g + 1], ALU.mult, ALU.add)
                        i.then_inc(h_done_p, 1)

            def gap(j):
                post_norm(j)
                store_job(GAP_JOB0[j])
                pre_norm(j + 1)
                if j == 0:
                    nc.gpsimd.iota(dist_i[:], pattern=[[-1, SEQ]], base=SEQ - P, channel_multiplier=1)\
                        .then_inc(pool_const, 1)
                if j == 3:
                    pool.dma_start(clf_nat[:], cc_logf[0, 0].rearrange("(t q) h -> q t h", q=P)).then_inc(fl_in, 16)
                    pool.dma_start(bf_col[:], b_f.rearrange("a h -> h a")).then_inc(fl_in, 16)
                store_job(GAP_JOB0[j] + 1)

            pool.wait_ge(rel_done, 2)
            pool.dma_start(rel_scratch[:, :, :], rel_rev[:].rearrange("h (o n) -> h o n", o=1).broadcast_to([8, P, 384]))\
                .then_inc(rel_dram, 16)
            pre_norm(0)

            def kv(st):
                att = st.kind
                if st.st < 8:
                    n = who(st.kind, st.st)
                    pool.wait_ge(pv_done, st.at("pv"))
                    settle(pool)
                    pool.dma_start(ck_nat[:, st.new], cache_in[n][0][st.tile_of(0)]).then_inc(cache_k[st.new], 16)
                    pool.dma_start(cv_nat[:, st.new], cache_in[n][1][st.tile_of(0)]).then_inc(cache_v[st.new], 16)
                    if n == "c":
                        for hh in range(2):
                            pool.dma_start(dk_b[:, st.new, hh, :],
                                           dec_rows[2 * st.tile_of(0) + hh].broadcast_to([P, SEQ + PAST + DEC])
                                           ).then_inc(dk_in[st.new], 16)
                    pool.wait_ge(tr_out, st.at("tr") + (counts[st.kind][st.st + 1]["tr"] - counts[st.kind][st.st]["tr"]))
                    settle(pool)
                    for src, (dp, ds) in zip((k_nat, v_nat), kv_out[n]):
                        pool.dma_start(dp[st.tile_of(0)], src[:, st.new, 0:QT, :]).then_inc(kv_stored[st.new], 16)
                        pool.dma_start(ds[st.tile_of(0)], src[0:DEC, st.new, QT, :]).then_inc(kv_stored[st.new], 16)

            dec_rows = dec_scratch.rearrange("h (o n) -> h o n", o=1)
            store_jobs(4, 6)
            load_mod(0, 9)
            store_jobs(10, 4)
            gap(0)
            load_mod(1, 15)
            stages(pool, "ab", kv)
            gap(1)
            store_jobs(18, 4)
            load_mod(2, 21)
            store_jobs(22, 2)
            gap(2)
            store_jobs(26, 2)
            load_mod(3, 27)
            store_jobs(28, 4)
            gap(3)
            load_mod(4, 33)
            pool.wait_ge(fl_done, FL_DECAY)
            pool.dma_start(dec_scratch[:, :], decay[:]).then_inc(fl_dram, 16)
            pool.wait_ge(fl_dram, 16)
            stages(pool, "c", kv)
            pool.wait_ge(fl_act, 4)
            pool.dma_start(pc_lf[0, 0].rearrange("(t q) h -> q t h", q=P), lf_nat[:, 0:QT, :]).then_inc(lf_stored, 16)
            pool.dma_start(sc_lf[0, 0], lf_nat[0:DEC, QT, :]).then_inc(lf_stored, 16)
            gap(4)
            load_mod(5, 35)
            post_norm(5)

        @block.tensor
        def _(pe):
            def products(u, out, k, moving_hi, moving_lo, first, last):
                hl = u["hl"]
                m = None
                for n, (w, mv) in enumerate(((w_hi, moving_hi), (w_hi, moving_lo), (w_lo, moving_hi))):
                    for a in range(2):
                        m = nc.tensor.matmul(lin[:, 2 * out + a, 0:HALF], w[:, hl, k, :],
                                             mv[:, a * HALF:(a + 1) * HALF],
                                             start=first and n == 0, stop=last and n == 2)
                return m

            def unit(u, out, tiles, hi, lo, k0=0, first=True, last=True, gradual=None):
                pe.wait_ge(lo_done, u["idx"] + 1)
                for k in range(tiles):
                    if gradual is not None:
                        pe.wait_ge(h_lo_done, gradual + k + 1)
                    m = products(u, out, k, hi[:, k0 + k, :], lo[:, k0 + k, :],
                                 first and k == 0, last and k == tiles - 1)
                m.then_inc(unit_done, 1)

            def ada_unit(u, k, job, out=ps_t[0:2, :]):
                if k == 0 and job >= FIRST_JOBS:
                    pe.wait_ge(job_copied, job)
                pe.wait_ge(raw_in[u["slot"]], u["landed"])
                w = raw[:, u["slot"], 0:KT, :].rearrange("p (k a) n -> p k (a n)", k=2)
                for t in range(2):
                    kt = 2 * k + t
                    m = nc.tensor.matmul(out, silu_c[:, kt, :], w[:, t, :], start=kt == 0, stop=kt == KT - 1)
                m.then_inc(unit_done, 1)

            def sum_job(job, nth):
                pe.wait_ge(acc_step, 16 * (nth + 1))
                pe.wait_ge(job_copied, job)
                for g in range(2):
                    m = nc.tensor.matmul(ps_t[0:2, :], pick[:, 2 * g:2 * g + 2], acc[:, g, :], start=g == 0, stop=g == 1)
                m.then_inc(unit_done, 1)

            def turn_first(n):
                pe.wait_ge(job_copied, n + 1)
                for b in range(JOB // P):
                    q = 2 * (JOB // P * n + b)
                    m = nc.tensor.transpose(ps_o[:, q:q + 2], mod_out[:, b * P:(b + 1) * P], ident[0:2, 0:2])
                m.then_inc(mod_turned if n == FIRST_JOBS - 1 else first_turned, 1)

            def turn_mod(j):
                pe.wait_ge(mod_loaded, 32 * (j + 1))
                n = 48 if j + 1 < NSUB else 16
                nc.tensor.transpose(ps_o[:, 0:n], mod_in[0:n, :], ident[0:n, 0:n]).then_inc(mod_turned, 1)

            def mean(src, first, last):
                for a in range(2):
                    m = nc.tensor.matmul(ps_s[:, a, 0:HALF], mean_w[:], src[:, a * HALF:(a + 1) * HALF],
                                         start=first, stop=last)
                return m

            def post_norm(j):
                pe.wait_ge(sq_added, 8 * (j + 1))
                mean(sq_sum[:], True, False)
                pe.wait_ge(sq_done, sq_base[j] + 8)
                mean(work[:, 1, :], False, True).then_inc(mean_done, 1)

            def gap_units(j, first, n):
                for k in range(first, first + n):
                    ada_unit(unit_at(ws, f"gap{j}", k), k % JOB_U, GAP_JOB0[j] + k // JOB_U)

            def pre_norm(j):
                for m in range(KT):
                    if m == 4 and j > 0:
                        gap_units(j - 1, JOB_U, 1)
                    pe.wait_ge(sq_done, sq_base[j] - 8 + m + 1)
                    mm = mean(slot4(m), m == 0, m == KT - 1)
                    if m < KT - 1:
                        mm.then_inc(sq_used, 1)
                mm.then_inc(mean_done, 1)

            pe.wait_ge(pool_const, 10)
            pe.wait_ge(const_in, 16 * 6)
            nc.tensor.transpose(ps_s[:, 0, 0:16], c_rows[:], ident[0:16, 0:16])
            nc.tensor.transpose(ps_s[:, 0, 16:112], norm_rows[:], ident[0:96, 0:96]).then_inc(const_tr, 1)
            nc.tensor.transpose(ps_s[:, 1, 0:72], ada_rows[:, 0, :], ident[0:72, 0:72])
            nc.tensor.transpose(ps_s[:, 1, 72:144], ada_rows[:, 1, :], ident[0:72, 0:72]).then_inc(const_tr, 1)
            pe.wait_ge(x_in, 32)
            for m in range(KT):
                if m >= 2:
                    pe.wait_ge(x_ready, m - 1)
                for t in range(QT):
                    nc.tensor.transpose(lin[:, 2 * (m % 2), t * P:(t + 1) * P], x_nat[:, t, m * P:(m + 1) * P], ident[:])
                nc.tensor.transpose(lin[:, 2 * (m % 2) + 1, 0:DEC], x_nat[0:DEC, QT, m * P:(m + 1) * P],
                                    ident[0:DEC, 0:DEC]).then_inc(xt_ps, 1)
            pe.wait_ge(vec_const, 2)
            pre_norm(0)
            pe.wait_ge(silu_c_done, 1)
            pe.wait_ge(x_ready, KT)
            for n in range(FIRST_JOBS):
                for k in range(JOB_U):
                    ada_unit(unit_at(ws, "ada_start", JOB_U * n + k), k, n, start_bank(n))
                if n > 0:
                    turn_first(n - 1)
            turn_first(FIRST_JOBS - 1)

            def stage(st):
                order = st.order
                att = st.att
                evs = st.ev()
                lag = 3 if att == "b" else 2

                def lin_chunk(s, half):
                    k, part = divmod(s, 4)
                    u = st.unit(k)
                    out = (0, 1, 0)[k]
                    if part == 0 and half == 0:
                        pe.wait_ge(lo_done, u["idx"] + 1)
                        if k == 2 or st.st > 0:
                            pe.wait_ge(kv_evac, evs + (0, -1, 1)[k])
                        elif k == 1 and st.kind == "c":
                            pe.wait_ge(fl_done, 1)
                    kt = 2 * part + half
                    if st.st == 0 and k == 0 and st.i is None and (st.kind == "ab"):
                        pe.wait_ge(h_lo_done, 8 + kt + 1)
                    m = products(u, out, kt, h_hi[:, kt, :], h_lo[:, kt, :], kt == 0, kt == KT - 1)
                    if kt == KT - 1:
                        m.then_inc(unit_done, 1)

                def turn(step):
                    new, base = st.new, st.at("tr")
                    if st.st == 0 and step == 5:
                        pe.wait_ge(job_copied, GAP_JOB0[0 if st.kind == "ab" else 3] + GAP_JOBS)
                    if step == 5:
                        pe.wait_ge(kv_evac, evs + 1)
                        src = kT[:, new, :]
                    elif step == 9:
                        pe.wait_ge(kv_evac, evs + 2)
                        src = vT[:, :]
                    n = tr_plan(st).index((step, "turn"))
                    wait_tr(base + n)
                    if step in (5, 9):
                        for t in range(QT):
                            m = nc.tensor.transpose(ps_t[:, t * P:(t + 1) * P], src[:, t * P:(t + 1) * P], ident[:])
                    else:
                        pe.wait_ge(cache_k[new], 16 * (st.same_new + 1))
                        nc.tensor.transpose(ps_t[0:DEC, 0:P], kT[:, new, SEQ:TOK], ident[:])
                        nc.tensor.transpose(ps_t[0:DEC, P:2 * P], vT[:, SEQ:TOK], ident[:])
                        for c in range(2):
                            m = nc.tensor.transpose(ps_t[:, (2 + c) * P:(3 + c) * P], ck_nat[:, new, c, :], ident[:])
                    m.then_inc(tr_ps, 1)

                def wait_tr(n):
                    pe.wait_ge(tr_out, n)

                def scores(j):
                    t, hh = order[j]
                    par, r = st.par, rows(order[j][0])
                    hs = slice(HD * hh, HD * hh + HD)
                    q0 = t * P if t < QT else SEQ
                    if j == 0:
                        pe.wait_ge(kv_evac, evs)
                        pe.wait_ge(tr_out, st.at("tr"))
                    if j >= 2:
                        pe.wait_ge(s_added, st.at("s") + j - 1)
                    lhs = qT[hs, par, q0:q0 + r]
                    if t == QT:
                        settle(pe)
                    if t < QT:
                        m = nc.tensor.matmul(ps_s[0:r, j % 2, 0:keys(t)], lhs, kT[hs, par, 0:keys(t)],
                                             start=True, stop=True)
                    else:
                        nc.tensor.matmul(ps_s[0:r, j % 2, 0:PAST], lhs, ckT[hs, par, :], start=True, stop=True)
                        m = nc.tensor.matmul(ps_s[0:r, j % 2, PAST:PAST + DEC], lhs, kT[hs, par, SEQ:TOK],
                                             start=True, stop=True)
                    m.then_inc(s_ps, 1)

                def transpose_probs(j, q):
                    t = order[j][0]
                    slot = (j - 1 if att == "b" else j) % PSLOTS
                    if att == "b":
                        pe.wait_ge(comb_done, st.at("comb") + q + 1)
                    else:
                        pe.wait_ge(exp_done, st.at("s") + j + 1)
                    wait_tr(st.at("tr") + tr_plan(st).index((j + lag, "probs")))
                    if t == QT:
                        settle(pe)
                    if t < QT:
                        for b in range(t + 1):
                            m = nc.tensor.transpose(ps_t[:, b * P:(b + 1) * P], probs[:, slot, b * P:(b + 1) * P], ident[:])
                    else:
                        for b in range(2):
                            nc.tensor.transpose(ps_t[:, b * P:b * P + DEC], probs[0:DEC, slot, b * P:(b + 1) * P],
                                                ident[0:DEC, 0:DEC])
                        m = nc.tensor.transpose(ps_t[0:DEC, 2 * P:2 * P + DEC], probs[0:DEC, slot, PAST:PAST + DEC],
                                                ident[0:DEC, 0:DEC])
                    m.then_inc(tr_ps, 1)

                def values(j, q):
                    t, hh = order[j]
                    r, par = rows(t), st.par
                    cols = slice(0, P) if att == "b" else slice(HD * hh, HD * hh + HD)
                    width = P if att == "b" else HD
                    pe.wait_ge(tr_out, st.at("tr") + tr_plan(st).index((j + lag, "probs")) + 1)
                    if q >= 1:
                        pe.wait_ge(o_read, st.at("pv") + q)
                    if att != "b" and j >= 2:
                        pe.wait_ge(o_lo_done, st.at("ot") + j // 2)
                    if t == QT:
                        pe.wait_ge(cache_v[par], 16 * (st.same_att + 1))
                    out = ps_o[0:r, (q % 2) * P:(q % 2) * P + width]
                    n = t + 1 if t < QT else 3
                    for b in range(n):
                        if t < QT:
                            lhs, rhs = probsT[:, q % 2, b, :], v_nat[:, par, b, cols]
                        elif b < 2:
                            lhs, rhs = probsT[:, q % 2, b, 0:DEC], cv_nat[:, par, b, cols]
                        else:
                            lhs, rhs = probsT[0:DEC, q % 2, b, 0:DEC], v_nat[0:DEC, par, QT, cols]
                        m = nc.tensor.matmul(out, lhs, rhs, start=b == 0, stop=b == n - 1)
                    m.then_inc(pv_done, 1)

                def turn_out(q):
                    t = order[2 * q][0]
                    r = rows(t)
                    pe.wait_ge(o_read, st.at("pv") + 2 * q + 2)
                    settle(pe)
                    nc.tensor.transpose(ps_o[:, (2 + q % 2) * P:(2 + q % 2) * P + r], o_nat[0:r, q % 2, :],
                                        ident[0:r, 0:r]).then_inc(ot_ps, 1)

                for s in range(STEPS + 2):
                    if st.new is not None and s in (5, 9, 12):
                        turn(s)
                    for half in (0, 1):
                        if st.new is not None and s < LIN_STEPS:
                            lin_chunk(s, half)
                        j = s - lag - 2
                        if half == 0 and att in ("a", "c") and 0 <= j < 10 and j % 2:
                            turn_out(j // 2)
                    if att is None:
                        continue
                    j = s - lag
                    if 0 <= j < 10 and (att != "b" or j % 2):
                        transpose_probs(j, j // 2 if att == "b" else j)
                    j = s - lag - 1
                    if 0 <= j < 10 and (att != "b" or j % 2):
                        values(j, j // 2 if att == "b" else j)
                    if s < 10:
                        scores(s)

            for j, kind in enumerate(KIND):
                if kind == "ffn":
                    def gu(seg, i, t0, j=j, first=False):
                        base = FT * ffn_index(j)
                        for name in TRIP[seg == 0]:
                            u = unit_at(ws, ws.first[f"gu{j}_{seg}_0_{name}"], 0, i, len(TRIP[seg == 0]),
                                        GU_TRIPS[j][seg])
                            if name.startswith("ada"):
                                if name == "ada3":
                                    sum_job(GU_JOB0[j] + i, ACC0[j] + i)
                                continue
                            f = 2 * (i + t0) + int(name[-1])
                            up = name.startswith("up")
                            pe.wait_ge(prod_done if up else gate_read, base + f)
                            unit(u, int(up), KT, h_hi, h_lo, gradual=8 * j if first and name == "gate0" else None)
                    n_job, n_plain = GU_TRIPS[j]
                    gu(0 if n_job else 1, 0, 0, first=True)
                    if n_job:
                        with pe.Fori(1, n_job) as i:
                            gu(0, i, 0)
                    if not n_job:
                        with pe.Fori(1, n_plain) as i:
                            gu(1, i, n_job)
                    else:
                        loop(pe, n_plain, lambda i: gu(1, i, n_job))
                    turn_mod(j)

                    def down(i, j=j):
                        for k in range(4):
                            m = 2 * i + k // 2
                            if k % 2 == 0:
                                pe.wait_ge(y_copied, 1 + 8 * j + m - 1)
                            pe.wait_ge(act_lo_done, FT * ffn_index(j) + DK * (1 + k % 2))
                            unit(unit_at(ws, f"out{j}", k, i, 4, KT // 2), k // 2, DK, act_hi, act_lo,
                                 k0=DK * (k % 2), first=k % 2 == 0, last=k % 2 == 1)
                    loop(pe, KT // 2, down)
                else:
                    if kind == "c":
                        unit(unit_at(ws, "forget", 0), 1, KT, h_hi, h_lo, gradual=8 * j)
                        pe.wait_ge(fl_in, 32)
                        for t in range(2):
                            m = nc.tensor.transpose(ps_s[0:16, 0, t * P:(t + 1) * P], clf_nat[:, t, :], ident[:])
                        m.then_inc(fl_ps, 1)

                    def turn_forget():
                        pe.wait_ge(fl_done, FL_DECAY)
                        for t in range(QT + 1):
                            m = nc.tensor.transpose(ps_s[0:rows(t), 0, 16 * t:16 * t + 16],
                                                    logf[:, t * P:t * P + rows(t)], ident[0:16, 0:16])
                        m.then_inc(fl_ps, 1)
                        for t in range(QT + 1):
                            t0 = t * P if t < QT else SEQ + PAST
                            m = nc.tensor.transpose(ps_s[0:rows(t), 1, 16 * t:16 * t + 16],
                                                    decay[:, t0:t0 + rows(t)], ident[0:16, 0:16])
                        m.then_inc(fl_ps, 1)
                        pe.wait_ge(fl_act, 6)
                    stages(pe, kind, stage, turn_forget if kind == "c" else None)
                    if kind == "ab":
                        for hd in range(4):
                            pe.wait_ge(b_scaled, hd + 1)
                            if hd >= 1:
                                pe.wait_ge(o_lo_done, 20 + 2 * hd)
                            for t in range(QT):
                                m = nc.tensor.transpose(ps_s[:, 0, t * P:(t + 1) * P], b_nat[:, hd, t, :], ident[:])
                            m.then_inc(ot_ps, 1)
                            nc.tensor.transpose(ps_s[:, 1, 0:DEC], b_nat[0:DEC, hd, QT, :],
                                                ident[0:DEC, 0:DEC]).then_inc(ot_ps, 1)
                    n_ot = off["c"]["ot"] if kind == "ab" else off["c"]["ot"] + 40
                    pe.wait_ge(o_lo_done, n_ot)
                    turn_mod(j)
                    for m in range(KT):
                        pe.wait_ge(y_copied, 1 + 8 * j + m - 1)
                        unit(unit_at(ws, f"out{j}", m), m % 2, KT, o_hi, o_lo)
                post_norm(j)
                if j + 1 < NSUB:
                    gap_units(j, 0, JOB_U)
                    pe.wait_ge(std_done, 2 * j + 2)
                    pre_norm(j + 1)
                    gap_units(j, JOB_U + 1, JOB_U - 1)

            for n in range(2 * (QT + 1)):
                a, t = divmod(n, QT + 1)
                pe.wait_ge(x_ready, 8 * NSUB + 4 * (a + 1))
                if n >= 4:
                    pe.wait_ge(nat_v if by_vector(n - 4) else nat_a, copies_to(n - 4))
                for k in range(4):
                    m = nc.tensor.transpose(lin[0:rows(t), n % 4, k * P:(k + 1) * P],
                                            x[:, 4 * a + k, t * P:t * P + rows(t)], ident[:])
                m.then_inc(nat_ps, 1)

        @block.scalar
        def _(act):
            def w_split(u, tiles):
                act.wait_ge(raw_in[u["slot"]], u["landed"])
                act.wait_ge(unit_done, u["hl_free"])
                nc.scalar.activation(w_hi[:, u["hl"], 0:tiles, :], raw[:, u["slot"], 0:tiles, :], ACT.Copy)\
                    .then_inc(hi_done, 1)

            def half_split(u, half, halves):
                if half == 0:
                    act.wait_ge(raw_in[u["slot"]], u["landed"])
                    act.wait_ge(unit_done, u["hl_free"])
                t = slice(4 * half, 4 * half + 4)
                nc.scalar.activation(w_hi[:, u["hl"], t, :], raw[:, u["slot"], t, :], ACT.Copy)\
                    .then_inc(hi_done if half else hi_half, 1)

            def std(n):
                act.wait_ge(mean_done, n)
                if n > 1:
                    act.wait_ge(rstd_done, n - 1)
                nc.scalar.activation(two(rstd[:]), ps_s[:, :, 0:HALF], ACT.Sqrt, bias=eps[:, 0:1]).then_inc(std_done, 1)

            def copy_gap_job(j, k):
                copy_job(unit_at(ws, f"gap{j}", JOB_U * k + JOB_U - 1), GAP_JOB0[j] + k)

            def squares(j):
                for m in range(KT):
                    if m == 2 and j > 0:
                        copy_gap_job(j - 1, 0)
                    act.wait_ge(x_ready, 8 * j + m + 1)
                    if m >= 4:
                        act.wait_ge(sq_used, 7 * j + m - 3)
                    nc.scalar.activation(slot4(m), x[:, m, :], ACT.Square).then_inc(sq_done, 1)
                std(2 * j + 1)

            def hidden(j):
                own = KT - len(POOL_H)
                act.wait_ge(coef, coef_ready[j])
                for m in range(KT):
                    h = slot4(m)
                    if m in POOL_H:
                        act.wait_ge(h_done_p, len(POOL_H) * j + tiles_of(POOL_H, m))
                    else:
                        if m in POOL_X:
                            act.wait_ge(t_done_p, len(POOL_X) * j + tiles_of(POOL_X, m))
                        else:
                            act.wait_ge(t_done, (KT - len(POOL_X)) * j + m + 1 - tiles_of(POOL_X, m))
                        for g, c in ((0, slice(0, SEQ)), (1, slice(SEQ, TOK))):
                            i = nc.scalar.activation(h[:, c], h[:, c], ACT.Identity, scale=co_scale[:, m, g:g + 1],
                                                     bias=co_shift[:, m, g:g + 1])
                        i.then_inc(h_done, 1)
                        act.wait_ge(h_done, own * j + m + 1 - tiles_of(POOL_H, m))
                    nc.scalar.activation(h_hi[:, m, :], h, ACT.Copy).then_inc(h_hi_done, 1)

            def square_out(j, m, a, u):
                act.wait_ge(unit_done, u["n"] + 1)
                act.wait_ge(sq_added, 8 * j + 1 + m - 1)
                nc.scalar.activation(two(work[:, a, :]), pair(a), ACT.Square).then_inc(sq_done, 1)

            def copy_job(u, job):
                act.wait_ge(unit_done, u["n"] + 1)
                if isinstance(job, int) and job < FIRST_JOBS:
                    act.wait_ge(first_turned, job)
                else:
                    act.wait_ge(job_stored, 16 * (job - FIRST_JOBS))
                    act.wait_ge(mod_turned, 1)
                src = start_bank(job) if isinstance(job, int) and job < FIRST_JOBS else ps_t[0:2, :]
                nc.scalar.activation(mod_out[:, :], src, ACT.Copy).then_inc(job_copied, 1)

            def warm_sqrt(n):
                nc.scalar.activation(warm[:, n:n + 1], eps[:, 0:1], ACT.Sqrt)

            act.wait_ge(const_tr, 1)
            nc.scalar.activation(silu_c[:].rearrange("p k g -> p g k"),
                                 ps_s[:, 0, 0:16].rearrange("p (g k) -> p g k", g=2), ACT.Silu).then_inc(silu_c_done, 1)
            act.wait_ge(pool_const, 4)
            squares(0)
            act.wait_ge(lam_done, 2)
            nc.scalar.activation(lam[:, 2:4], lam[:, 0:2], ACT.Exp).then_inc(lam_done, 1)
            for n in range(FIRST_JOBS):
                copy_job(unit_at(ws, "ada_start", JOB_U * n + JOB_U - 1), n)
            w_split(first_gu(0), KT)
            hidden(0)
            act.wait_ge(rel_dram, 32)

            def stage(st):
                order, att = st.order, st.att
                evs = st.ev()
                plan_t = tr_plan(st)

                def evac(k):
                    u = st.unit(k)
                    act.wait_ge(unit_done, u["n"] + 1)
                    dst = (kT[:, st.new, :], vT[:], qT[:, st.new, :])[k]
                    nc.scalar.activation(two(dst), pair((0, 1, 0)[k]), ACT.Copy,
                                         scale=HD ** -0.5 if k == 2 else 1.0).then_inc(kv_evac, 1)

                def empty_turn(step):
                    n = plan_t.index((step, "turn"))
                    act.wait_ge(tr_ps, st.at("tr") + n + 1)
                    if step in (5, 9):
                        if step == 5:
                            act.wait_ge(kv_stored[st.new], 64 * st.same_new)
                        dst = (k_nat if step == 5 else v_nat)[:, st.new, 0:QT, :].rearrange("p t n -> p (t n)")
                        nc.scalar.activation(dst, ps_t[:, :], ACT.Copy).then_inc(tr_out, 1)
                    else:
                        nc.scalar.activation(k_nat[0:DEC, st.new, QT, :], ps_t[0:DEC, 0:P], ACT.Copy)
                        nc.scalar.activation(v_nat[0:DEC, st.new, QT, :], ps_t[0:DEC, P:2 * P], ACT.Copy)
                        nc.scalar.activation(ckT[:, st.new, :], ps_t[:, 2 * P:4 * P], ACT.Copy).then_inc(tr_out, 1)

                def empty_probs(j, q, lag):
                    t = order[j][0]
                    act.wait_ge(tr_ps, st.at("tr") + plan_t.index((j + lag, "probs")) + 1)
                    if q >= 2:
                        act.wait_ge(pv_done, st.at("pv") + q - 1)
                    if t < QT:
                        nc.scalar.activation(probsT[:, q % 2, 0:t + 1, :].rearrange("p b n -> p (b n)"),
                                             ps_t[:, 0:(t + 1) * P], ACT.Copy).then_inc(tr_out, 1)
                    else:
                        nc.scalar.activation(probsT[:, q % 2, 0:2, 0:DEC],
                                             ps_t[:, 0:2 * P].rearrange("p (b n) -> p b n", b=2)[:, :, 0:DEC], ACT.Copy)
                        nc.scalar.activation(probsT[0:DEC, q % 2, 2, 0:DEC], ps_t[0:DEC, 2 * P:2 * P + DEC], ACT.Copy)\
                            .then_inc(tr_out, 1)

                def exps(j):
                    t = order[j][0]
                    r, n = rows(t), keys(t)
                    act.wait_ge(s_maxed, st.at("s") + j + 1)
                    nc.scalar.activation(probs[0:r, j % PSLOTS, 0:n], probs[0:r, j % PSLOTS, 0:n], ACT.Exp,
                                         bias=neg_max[0:r, j:j + 1], accum_out=row_sum[0:r, j:j + 1])\
                        .then_inc(exp_done, 1)

                def out_hi(q):
                    t = order[2 * q][0]
                    r = rows(t)
                    act.wait_ge(ot_ps, st.at("ot") + q + 1)
                    nc.scalar.activation(o_hi[:, st.tile_of(-1), t * P:t * P + r],
                                         ps_o[:, (2 + q % 2) * P:(2 + q % 2) * P + r], ACT.Copy).then_inc(o_hi_done, 1)

                def b_square(q):
                    t = order[2 * q][0]
                    r = rows(t)
                    act.wait_ge(o_read, st.at("pv") + q + 1)
                    act.wait_ge(b_sq_done, 5 * st.tile_of(-1) + q)
                    nc.scalar.activation(o_nat[0:r, 0, :], b_nat[0:r, st.tile_of(-1), t, :], ACT.Square,
                                         accum_out=b_sq[0:r, st.tile_of(-1), t:t + 1]).then_inc(b_sq_done, 1)

                lag = 3 if att == "b" else 2
                for s in range(STEPS + 2):
                    if st.new is not None:
                        if s in (4, 8, 12):
                            evac(s // 4 - 1)
                        if s in (5, 9, 12):
                            empty_turn(s)
                    if att is None:
                        split_next(half_split, st, s)
                        continue
                    j = s - lag - 2
                    if att != "b" and 0 <= j < 10 and j % 2:
                        out_hi(j // 2)
                    j = s - lag
                    if 0 <= j < 10 and (att != "b" or j % 2):
                        empty_probs(j, j // 2 if att == "b" else j, lag)
                    j = s - lag - 2
                    if 0 <= j < 10 and j % 2 and att == "b":
                        b_square(j // 2)
                    if s < 10:
                        exps(s)
                    split_next(half_split, st, s)

            for j, kind in enumerate(KIND):
                if kind == "ffn":
                    base = FT * ffn_index(j)

                    if j in (2, 5):
                        for par in range(2):
                            act.wait_ge(kv_stored[par], 256 * (1 + (j == 5)))
                    if j == 5:
                        act.wait_ge(lf_stored, 32)

                    def gu(seg, i, t0, last, j=j, base=base):
                        if not isinstance(i, int):
                            act.wait_ge(act_hi_done, base + 2 * (i + t0))
                            nc.scalar.activation(warm[:, NSUB:NSUB + 1], eps[:, 0:1], ACT.Silu)
                        for a in range(2):
                            f = 2 * (i + t0) + a
                            w_split(gu_unit(ws, j, seg, f"up{a}", i), KT)
                            act.wait_ge(unit_done, gu_unit(ws, j, seg, f"gate{a}", i)["n"] + 1)
                            nc.scalar.activation(two(work[:, a, :]), pair(0), ACT.Silu).then_inc(gate_read, 1)
                            after_up(w_split, j, seg, i, a, last)
                            act.wait_ge(prod_done, base + f + 1)
                            nc.scalar.activation(act_hi[:, f, :], prod[:, a, :], ACT.Copy).then_inc(act_hi_done, 1)
                            if a == 1 and seg == 0:
                                copy_job(gu_unit(ws, j, seg, "ada3", i), GU_JOB0[j] + i)
                    segments(act, j, gu)

                    def down(i, last=False, j=j):
                        for a in range(2):
                            w_split(unit_at(ws, f"out{j}", 2 * a + 1, i, 4, KT // 2 - 1), DK)
                            if not (last and a == 1):
                                w_split(next_down(j, i, a), DK)
                            square_out(j, 2 * i + a, a, unit_at(ws, f"out{j}", 2 * a + 1, i, 4, KT // 2 - 1))
                    with act.Fori(0, KT // 2 - 1) as i:
                        down(i)
                    warm_sqrt(j)
                    down(KT // 2 - 1, last=True)
                else:
                    if kind == "c":
                        w_split(unit_at(ws, "qkv4", 0), KT)
                        w_split(unit_at(ws, "qkv4", 1), KT)
                        act.wait_ge(fl_done, 2)
                        nc.scalar.activation(e_t[:], e_t[:], ACT.Exp).then_inc(fl_act, 1)
                        act.wait_ge(fl_done, 3)
                        nc.scalar.activation(l_t[:], u_t[:], ACT.Ln).then_inc(fl_act, 1)

                    def empty_forget():
                        for n, (dst, k) in enumerate(((lf_nat, 0), (dqT, 1))):
                            act.wait_ge(fl_ps, 2 + n)
                            nc.scalar.activation(dst[:, 0:QT, :], ps_s[:, k, 0:64].rearrange("p (t h) -> p t h", h=16),
                                                 ACT.Copy).then_inc(fl_act, 1)
                            nc.scalar.activation(dst[0:DEC, QT, :], ps_s[0:DEC, k, 64:80], ACT.Copy).then_inc(fl_act, 1)
                    stages(act, kind, stage, empty_forget if kind == "c" else None)
                    if kind == "ab":
                        act.wait_ge(b_sq_done, 20)
                        act.wait_ge(b_inv, 1)
                        nc.scalar.activation(b_sq[:].rearrange("p h t -> p (h t)"), b_sq[:].rearrange("p h t -> p (h t)"),
                                             ACT.Sqrt, scale=1.0 / P, bias=eps[:, 0:1]).then_inc(b_std, 1)
                        for hd in range(4):
                            act.wait_ge(ot_ps, 20 + 2 * hd + 1)
                            nc.scalar.activation(o_hi[:, 4 + hd, 0:SEQ], ps_s[:, 0, :], ACT.Copy).then_inc(o_hi_done, 1)
                            act.wait_ge(ot_ps, 20 + 2 * hd + 2)
                            nc.scalar.activation(o_hi[:, 4 + hd, SEQ:TOK], ps_s[:, 1, 0:DEC], ACT.Copy)\
                                .then_inc(o_hi_done, 1)
                    w_split(unit_at(ws, f"out{j}", 0), KT)
                    for m in range(KT):
                        if m + 1 < KT:
                            w_split(unit_at(ws, f"out{j}", m + 1), KT)
                        if m == 6:
                            warm_sqrt(j)
                        square_out(j, m, m % 2, unit_at(ws, f"out{j}", m))
                std(2 * j + 2)
                if j + 1 < NSUB:
                    squares(j + 1)
                    w_split(first_of(j + 1), KT)
                    hidden(j + 1)
                    copy_gap_job(j, 1)
            for n in range(2 * (QT + 1)):
                if not by_vector(n):
                    a, t = divmod(n, QT + 1)
                    act.wait_ge(nat_ps, n + 1)
                    nc.scalar.activation(x_nat[0:rows(t), t, a * 512:a * 512 + 512], lin[0:rows(t), n % 4, :], ACT.Copy)\
                        .then_inc(nat_a, 1)

        @block.vector
        def _(dve):
            def w_split(u, tiles):
                dve.wait_ge(hi_done, u["idx"] + 1)
                nc.vector.tensor_tensor(w_lo[:, u["hl"], 0:tiles, :], raw[:, u["slot"], 0:tiles, :],
                                        w_hi[:, u["hl"], 0:tiles, :].bitcast(F32), ALU.subtract).then_inc(lo_done, 1)

            def half_split(u, half, halves):
                dve.wait_ge(*((hi_done, u["idx"] + 1) if half else (hi_half, halves + 1)))
                t = slice(4 * half, 4 * half + 4)
                i = nc.vector.tensor_tensor(w_lo[:, u["hl"], t, :], raw[:, u["slot"], t, :],
                                            w_hi[:, u["hl"], t, :].bitcast(F32), ALU.subtract)
                if half:
                    i.then_inc(lo_done, 1)

            coef_n = [0]

            def step(ins):
                ins.then_inc(coef, 1)
                coef_n[0] += 1
                dve.wait_ge(coef, coef_n[0])

            def accumulate(u, k, nth):
                dve.wait_ge(raw_in[u["slot"]], u["landed"])
                w = raw[:, u["slot"], 0:KT, :].rearrange("p (k a) n -> p k (a n)", k=2)
                for r in range(4):
                    kt, g = 2 * k + r // 2, r % 2
                    if kt == 0:
                        i = nc.vector.tensor_scalar(acc[:, g, :], w[:, 0, :], silu_c[:, 0, g:g + 1], None, ALU.mult)
                    else:
                        dve.wait_ge(acc_step, 16 * nth + 4 * k + r - 1)
                        i = nc.vector.scalar_tensor_tensor(acc[:, g, :], w[:, r // 2, :], silu_c[:, kt, g:g + 1],
                                                           acc[:, g, :], ALU.mult, ALU.add)
                    i.then_inc(acc_step, 1)

            def bias(j, c, n):
                f0 = (3 * (j % 3) + c) * KT
                return ada_b[:, j // 3, f0:f0 + n].rearrange("p (k o) -> p k o", o=1).broadcast_to([P, n, 2])

            def gain(a, j):
                return norms[:, a, j, :].rearrange("p (k o) -> p k o", o=1).broadcast_to([P, KT, 2])

            def coef_in(j):
                dve.wait_ge(mod_turned, j + 1)
                dve.wait_ge(h_hi_done, 8 * j)
                src = mod_ps[:, 8:24, :] if j > 0 else mod_ps0
                step(nc.vector.tensor_tensor(co_tmp[:], src, bias(j, 0, 16), ALU.add))
                step(nc.vector.tensor_copy(co_shift[:], co_tmp[:, 0:KT, :]))
                step(nc.vector.scalar_tensor_tensor(co_scale[:], co_tmp[:, KT:2 * KT, :], 1.0, gain(0, j), ALU.add, ALU.mult))
                assert coef_n[0] == coef_ready[j], (j, coef_n[0], coef_ready[j])

            def coef_gate(j):
                dve.wait_ge(mod_turned, j + 2)
                src = mod_ps if j + 1 < NSUB else ps_o[:, 0:16].rearrange("p (g q) -> p q g", g=2)
                step(nc.vector.tensor_tensor(co_tmp[:, 0:KT, :], src[:, 0:8, :], bias(j, 2, 8), ALU.add))
                step(nc.vector.scalar_tensor_tensor(co_gate[:], co_tmp[:, 0:KT, :], 1.0, gain(1, j), ALU.add, ALU.mult))
                if KIND[j] == "ffn":
                    step(nc.vector.tensor_scalar(co_gate[:], co_gate[:], 0.5, None, ALU.mult))

            groups = ((0, slice(0, SEQ)), (1, slice(SEQ, TOK)))

            def inverse(n):
                dve.wait_ge(std_done, n)
                nc.vector.reciprocal(rstd[:], rstd[:]).then_inc(rstd_done, 1)
                dve.wait_ge(rstd_done, n)

            def pre_norm(j):
                if j > 0:
                    inverse(2 * j + 1)
                for m in range(KT + 1):
                    if m == 1 and j > 0:
                        w_split(first_of(j), KT)
                    if m < KT and m not in POOL_X:
                        if m >= 4:
                            dve.wait_ge(h_lo_done, 8 * j + m - 3)
                        nc.vector.tensor_tensor(slot4(m), x[:, m, :], rstd[:], ALU.mult).then_inc(t_done, 1)
                    if m > 0:
                        dve.wait_ge(h_hi_done, 8 * j + m)
                        nc.vector.tensor_tensor(h_lo[:, m - 1, :], slot4(m - 1), h_hi[:, m - 1, :].bitcast(F32),
                                                ALU.subtract).then_inc(h_lo_done, 1)

            def post_norm(j):
                own = KT - len(POOL_Y)
                dve.wait_ge(y_copied, 1 + 8 * (j + 1))
                inverse(2 * j + 2)
                for m in range(KT + 1):
                    if m < KT and m not in POOL_Y:
                        nc.vector.tensor_tensor(y[:, m, :], y[:, m, :], rstd[:], ALU.mult).then_inc(y_norm, 1)
                    if m > 0:
                        if m - 1 in POOL_Y:
                            dve.wait_ge(y_norm_p, len(POOL_Y) * j + tiles_of(POOL_Y, m - 1))
                        else:
                            dve.wait_ge(y_norm, own * j + m - tiles_of(POOL_Y, m - 1))
                        for g, c in groups:
                            i = nc.vector.scalar_tensor_tensor(x[:, m - 1, c], y[:, m - 1, c], co_gate[:, m - 1, g:g + 1],
                                                               x[:, m - 1, c], ALU.mult, ALU.add)
                        i.then_inc(x_ready, 1)

            def take_out(j, m, a, last):
                dve.wait_ge(sq_done, sq_base[j] + m + 1)
                nc.vector.tensor_copy(two(y[:, m, :]), pair(a)).then_inc(y_copied, 1)
                if not last:
                    dve.wait_ge(sq_added, 8 * j + 1 + m)
                    nc.vector.tensor_tensor(sq_sum[:], sq_sum[:], work[:, a, :], ALU.add).then_inc(sq_added, 1)

            dve.wait_ge(silu_c_done, 1)
            nc.vector.tensor_copy(norms[:].rearrange("p a s k -> p (a s k)"), ps_s[:, 0, 16:112]).then_inc(vec_const, 1)
            dve.wait_ge(const_tr, 2)
            nc.vector.tensor_copy(ada_b[:].rearrange("p l f -> p (l f)"), ps_s[:, 1, 0:144]).then_inc(vec_const, 1)
            dve.wait_ge(vec_const, 2)
            for m in range(KT):
                dve.wait_ge(xt_ps, m + 1)
                nc.vector.tensor_copy(x[:, m, 0:SEQ], lin[:, 2 * (m % 2), :])
                nc.vector.tensor_copy(x[:, m, SEQ:TOK], lin[:, 2 * (m % 2) + 1, 0:DEC]).then_inc(x_ready, 1)
            dve.wait_ge(lam_landed, 32)
            step(nc.vector.memset(pick[:], 0.0))
            step(nc.vector.memset(pick[:, 0:4:3], 1.0))
            lam_p = sq_sum[:, 0:2 * HD].rearrange("p (a d) -> p a d", a=2)
            nc.vector.tensor_tensor(lam_p, lam_in[:, 0:4:2, :], lam_in[:, 1:4:2, :], ALU.mult).then_inc(lam_done, 1)
            dve.wait_ge(lam_done, 1)
            nc.vector.tensor_reduce(lam[:, 0:2], lam_p, AX.X, ALU.add).then_inc(lam_done, 1)
            inverse(1)
            dve.wait_ge(lam_done, 3)
            step(nc.vector.tensor_tensor(lam[:, 4:5], lam[:, 3:4], lam[:, 2:3], ALU.subtract))
            step(nc.vector.tensor_scalar(lam[:, 7:8], lam[:, 4:5], -LAM_INIT, None, ALU.add))
            step(nc.vector.tensor_scalar(sub_g[:], sub_g[:], 1.0 - LAM_INIT, None, ALU.mult))
            dve.wait_ge(rel_dram, 16)
            nc.vector.tensor_copy(rel_rev[:, P - 1:3 * P], rel_in[:, ::-1]).then_inc(rel_done, 1)
            nc.vector.tensor_copy(rel_rev[:, 0:P - 1], rel_in[:, 2 * REL:2 * REL + 1].broadcast_to([8, P - 1]))\
                .then_inc(rel_done, 1)
            coef_in(0)
            w_split(first_of(0), KT)
            pre_norm(0)

            def stage(st):
                order, att = st.order, st.att
                lag = 3 if att == "b" else 2

                def add_bias(j):
                    t, hh = order[j]
                    r, n = rows(t), keys(t)
                    dst = probs[0:r, j % PSLOTS, :]
                    src = ps_s[0:r, j % 2, :]
                    dve.wait_ge(s_ps, st.at("s") + j + 1)
                    if j >= PSLOTS and (att != "b" or j % 2 == 0):
                        at = j - PSLOTS + lag + (att == "b")
                        dve.wait_ge(tr_ps, st.at("tr") + tr_plan(st).index((at, "probs")) + 1)
                    if att == "a":
                        hd = 2 * st.tile_of(-1) + hh
                        near = 2 * P if 0 < t < QT else P if t == 0 else P + DEC
                        if n > near:
                            nc.vector.tensor_scalar(dst[:, 0:n - near], src[:, 0:n - near], rel_bias[0:r, hd, 0:1],
                                                    None, ALU.add)
                        lo = 0 if t else P
                        i = nc.vector.tensor_tensor(dst[:, n - near:n], src[:, n - near:n],
                                                    rel_bias[0:r, hd, lo:lo + near], ALU.add)
                    elif att == "b":
                        d0 = SEQ - P - (t * P if t < QT else PAST)
                        i = nc.vector.scalar_tensor_tensor(dst[:, 0:n], dist[0:r, d0:d0 + n],
                                                           neg_slope[0:r, bass.ds(st.tile_of(-1), 1)],
                                                           src[:, 0:n], ALU.mult, ALU.add)
                    else:
                        hd = 2 * st.tile_of(-1) + hh
                        k0 = 0 if t < QT else SEQ
                        if j == 0:
                            dve.wait_ge(dk_in[st.par], 32 * (st.same_att - 3))
                        i = nc.vector.scalar_tensor_tensor(dst[:, 0:n], src[:, 0:n], dqT[0:r, t, bass.ds(hd, 1)],
                                                           dk_b[0:r, st.par, hh, k0:k0 + n], ALU.add, ALU.subtract)
                    i.then_inc(s_added, 1)
                    dve.wait_ge(s_added, st.at("s") + j + 1)
                    if att == "c":
                        nc.vector.tensor_tensor(dst[:, n - r:n], dst[:, n - r:n], causal[0:r, 0:r], ALU.add)\
                            .then_inc(masked, 1)
                        dve.wait_ge(masked, st.at("s") - off["c"]["s"] + j + 1)
                    nc.vector.tensor_reduce(neg_max[0:r, j:j + 1], dst[:, 0:n], AX.X, ALU.max, negate=True)\
                        .then_inc(s_maxed, 1)

                def invert(j):
                    r = rows(order[j][0])
                    dve.wait_ge(exp_done, st.at("s") + j + 1)
                    nc.vector.reciprocal(row_inv[0:r, j:j + 1], row_sum[0:r, j:j + 1]).then_inc(inv_done, 1)

                def combine(q):
                    t = order[2 * q][0]
                    r, n = rows(t), keys(t)
                    a, b = (2 * q) % PSLOTS, (2 * q + 1) % PSLOTS
                    dve.wait_ge(inv_done, st.at("s") + 2 * q + 2)
                    nc.vector.tensor_scalar(probs[0:r, b, 0:n], probs[0:r, b, 0:n], row_inv[0:r, 2 * q + 1:2 * q + 2],
                                            lam[0:r, 7:8], ALU.mult, ALU.mult).then_inc(comb_half, 1)
                    dve.wait_ge(comb_half, st.at("comb") + q + 1)
                    nc.vector.scalar_tensor_tensor(probs[0:r, a, 0:n], probs[0:r, a, 0:n], row_inv[0:r, 2 * q:2 * q + 1],
                                                   probs[0:r, b, 0:n], ALU.mult, ALU.add).then_inc(comb_done, 1)

                def take(j, q):
                    t, hh = order[j]
                    r = rows(t)
                    dve.wait_ge(pv_done, st.at("pv") + q + 1)
                    if att == "b":
                        nc.vector.tensor_copy(b_nat[0:r, st.tile_of(-1), t, :], ps_o[0:r, (q % 2) * P:(q % 2) * P + P])\
                            .then_inc(o_read, 1)
                        return
                    nq = q // 2
                    if nq >= 2:
                        dve.wait_ge(ot_ps, st.at("ot") + nq - 1)
                    dve.wait_ge(inv_done, st.at("s") + j + 1)
                    nc.vector.tensor_scalar(o_nat[0:r, nq % 2, HD * hh:HD * hh + HD],
                                            ps_o[0:r, (q % 2) * P:(q % 2) * P + HD], row_inv[0:r, j:j + 1],
                                            None, ALU.mult).then_inc(o_read, 1)

                def out_lo(q):
                    t = order[2 * q][0]
                    r = rows(t)
                    dve.wait_ge(o_hi_done, st.at("ot") + q + 1)
                    c = slice(t * P, t * P + r)
                    nc.vector.tensor_tensor(o_lo[:, st.tile_of(-1), c], ps_o[:, (2 + q % 2) * P:(2 + q % 2) * P + r],
                                            o_hi[:, st.tile_of(-1), c].bitcast(F32), ALU.subtract).then_inc(o_lo_done, 1)

                lag = 3 if att == "b" else 2
                for s in range(STEPS + 2):
                    if att is None:
                        split_next(half_split, st, s - 1)
                        continue
                    j = s - 2
                    if 0 <= j < 10:
                        invert(j)
                        if att == "b" and j % 2:
                            combine(j // 2)
                    j = s - lag - 2
                    if att != "b" and 0 <= j < 10 and j % 2:
                        out_lo(j // 2)
                    j = s - lag - 1
                    if 0 <= j < 10 and (att != "b" or j % 2):
                        take(j, j // 2 if att == "b" else j)
                    if s < 10:
                        add_bias(s)
                    split_next(half_split, st, s - 1)

            def forget_gate():
                count = [0]

                def fl(ins, wait=True):
                    count[0] += 1
                    ins.then_inc(fl_done, 1)
                    if wait:
                        dve.wait_ge(fl_done, count[0])
                dve.wait_ge(fl_in, 32)
                dve.wait_ge(unit_done, unit_at(ws, "forget", 0)["n"] + 1)
                fl(nc.vector.tensor_scalar(two(z_t[:]), pair(1)[0:16], bf_col[:, 0:1], None, ALU.add))
                fl(nc.vector.scalar_tensor_tensor(e_t[:], z_t[:], -1.0, z_t[:], ALU.mult, ALU.min))
                dve.wait_ge(fl_act, 1)
                fl(nc.vector.tensor_scalar(u_t[:], e_t[:], 1.0, None, ALU.add))
                fl(nc.vector.scalar_tensor_tensor(logf[:], u_t[:], -1.0, e_t[:], ALU.add, ALU.subtract))
                dve.wait_ge(fl_act, 2)
                fl(nc.vector.reciprocal(u_t[:], u_t[:]))
                fl(nc.vector.tensor_tensor(logf[:], logf[:], u_t[:], ALU.mult))
                fl(nc.vector.tensor_tensor(l_t[:], l_t[:], logf[:], ALU.subtract))
                fl(nc.vector.scalar_tensor_tensor(logf[:], z_t[:], 0.0, l_t[:], ALU.min, ALU.subtract))
                fl(nc.vector.memset(ones16[:], 1.0))
                fl(nc.vector.tensor_tensor_scan(decay[:, 0:SEQ], ones16[:, 0:SEQ], logf[:, 0:SEQ], 0.0,
                                                ALU.mult, ALU.add), False)
                fl(nc.vector.tensor_tensor_scan(decay[:, SEQ + PAST:], ones16[:, 0:DEC], logf[:, SEQ:TOK], 0.0,
                                                ALU.mult, ALU.add), False)
                dve.wait_ge(fl_ps, 1)
                fl(nc.vector.tensor_tensor_scan(decay[:, SEQ:SEQ + PAST], ones16[:, 0:PAST], ps_s[0:16, 0, 0:PAST], 0.0,
                                                ALU.mult, ALU.add))
                fl(nc.vector.tensor_copy(l_t[:, 0:1], decay[:, SEQ + PAST - 1:SEQ + PAST]))
                fl(nc.vector.tensor_scalar(decay[:, SEQ:SEQ + PAST], decay[:, SEQ:SEQ + PAST], l_t[:, 0:1], None,
                                           ALU.subtract))
                assert count[0] == FL_DECAY

            def coefs_after(j):
                if j + 1 < NSUB:
                    coef_in(j + 1)
                coef_gate(j)

            for j, kind in enumerate(KIND):
                if kind == "ffn":
                    base = FT * ffn_index(j)

                    def gu(seg, i, t0, last, j=j, base=base):
                        for a in range(2):
                            f = 2 * (i + t0) + a
                            u = gu_unit(ws, j, seg, f"up{a}", i)
                            w_split(u, KT)
                            if seg == 0:
                                if a == 0:
                                    dve.wait_ge(unit_done, gu_unit(ws, j, seg, "gate0", i)["n"])
                                for k in ((0, 1), (3,))[a]:
                                    accumulate(gu_unit(ws, j, seg, f"ada{k}", i), k, ACC0[j] + i)
                            after_up(w_split, j, seg, i, a, last)
                            if seg == 0 and a == 0:
                                accumulate(gu_unit(ws, j, seg, "ada2", i), 2, ACC0[j] + i)
                            dve.wait_ge(gate_read, base + f + 1)
                            dve.wait_ge(unit_done, u["n"] + 1)
                            dve.wait_ge(act_lo_done, base + f)
                            nc.vector.tensor_tensor(two(prod[:, a, :]), two(work[:, a, :]), pair(1), ALU.mult)\
                                .then_inc(prod_done, 1)
                            dve.wait_ge(act_hi_done, base + f + 1)
                            dve.wait_ge(prod_done, base + f + 1)
                            nc.vector.tensor_tensor(act_lo[:, f, :], prod[:, a, :], act_hi[:, f, :].bitcast(F32),
                                                    ALU.subtract).then_inc(act_lo_done, 1)
                    segments(dve, j, gu)
                    coefs_after(j)
                    nc.vector.memset(sq_sum[:], 0.0).then_inc(sq_added, 1)
                    if j == 0:
                        nc.vector.memset(co_tmp[:], 0.0).then_inc(y_copied, 1)

                    def down(i, last=False, j=j):
                        for a in range(2):
                            u = unit_at(ws, f"out{j}", 2 * a + 1, i, 4, KT // 2 - 1)
                            w_split(u, DK)
                            if not (last and a == 1):
                                w_split(next_down(j, i, a), DK)
                            take_out(j, 2 * i + a, a, last and a == 1)
                    with dve.Fori(0, KT // 2 - 1) as i:
                        down(i)
                    down(KT // 2 - 1, last=True)
                else:
                    if kind == "ab":
                        dve.wait_ge(rel_loaded, 16 * 8)
                        dve.wait_ge(pool_const, 11)
                        step(nc.vector.memset(rel_bias[0:HD, :, 2 * P - HD:2 * P], NEG))
                        step(nc.vector.tensor_copy(dist[:], dist_i[:]))
                        step(nc.vector.scalar_tensor_tensor(dist[:], dist[:], -1.0, dist[:], ALU.mult, ALU.max))
                        step(nc.vector.memset(dist[0:HD, SEQ - HD:SEQ], 1e35))
                        nc.vector.memset(b_sq[:], 1.0).then_inc(b_inv, 1)
                        dve.wait_ge(b_inv, 1)
                    else:
                        w_split(unit_at(ws, "qkv4", 0), KT)
                        w_split(unit_at(ws, "qkv4", 1), KT)
                        forget_gate()
                    stages(dve, kind, stage)
                    if kind == "ab":
                        dve.wait_ge(b_std, 1)
                        nc.vector.reciprocal(b_sq[:].rearrange("p h t -> p (h t)"), b_sq[:].rearrange("p h t -> p (h t)"))\
                            .then_inc(b_inv, 1)
                        dve.wait_ge(b_inv, 2)
                        for hd in range(5):
                            if hd < 4:
                                for t in range(QT + 1):
                                    r = rows(t)
                                    i = nc.vector.scalar_tensor_tensor(b_nat[0:r, hd, t, :], b_nat[0:r, hd, t, :],
                                                                       b_sq[0:r, hd, t:t + 1], sub_g[0:r, :],
                                                                       ALU.mult, ALU.mult)
                                i.then_inc(b_scaled, 1)
                            if hd > 0:
                                p = hd - 1
                                dve.wait_ge(o_hi_done, 20 + 2 * p + 1)
                                nc.vector.tensor_tensor(o_lo[:, 4 + p, 0:SEQ], ps_s[:, 0, :],
                                                        o_hi[:, 4 + p, 0:SEQ].bitcast(F32), ALU.subtract)\
                                    .then_inc(o_lo_done, 1)
                                dve.wait_ge(o_hi_done, 20 + 2 * p + 2)
                                nc.vector.tensor_tensor(o_lo[:, 4 + p, SEQ:TOK], ps_s[:, 1, 0:DEC],
                                                        o_hi[:, 4 + p, SEQ:TOK].bitcast(F32), ALU.subtract)\
                                    .then_inc(o_lo_done, 1)
                    w_split(unit_at(ws, f"out{j}", 0), KT)
                    coefs_after(j)
                    nc.vector.memset(sq_sum[:], 0.0).then_inc(sq_added, 1)
                    for m in range(KT):
                        if m + 1 < KT:
                            w_split(unit_at(ws, f"out{j}", m + 1), KT)
                        take_out(j, m, m % 2, m == KT - 1)
                post_norm(j)
                if j + 1 < NSUB:
                    pre_norm(j + 1)
            for n in range(2 * (QT + 1)):
                if by_vector(n):
                    a, t = divmod(n, QT + 1)
                    dve.wait_ge(nat_ps, n + 1)
                    nc.vector.tensor_copy(x_nat[0:rows(t), t, a * 512:a * 512 + 512], lin[0:rows(t), n % 4, :])\
                        .then_inc(nat_v, 1)


_INS = ["x_prompt", "x_sample", "c_prompt", "c_sample", "cache_a_k", "cache_a_v", "cache_b_k", "cache_b_v",
        "cache_c_k", "cache_c_v", "cache_c_logf", "w_ada", "b_ada", "norm_pre", "norm_post", "ffn_w_gate",
        "ffn_w_up", "ffn_w_down", "w_in_ab", "w_out_ab", "relpos_a", "lambda_b", "subln_b", "w_in_c", "b_f",
        "w_out_c"]
_OUTS = [(1, SEQ, DM), (1, DEC, DM),
         (1, 1, SEQ, 8, HD), (1, 1, SEQ, 8, HD), (1, 1, SEQ, 4, 2 * HD), (1, 1, SEQ, 4, 2 * HD),
         (1, 1, SEQ, 16, HD), (1, 1, SEQ, 16, HD), (1, 1, SEQ, 16),
         (1, 1, DEC, 8, HD), (1, 1, DEC, 8, HD), (1, 1, DEC, 4, 2 * HD), (1, 1, DEC, 4, 2 * HD),
         (1, 1, DEC, 16, HD), (1, 1, DEC, 16, HD), (1, 1, DEC, 16)]


def kernel(**inputs):
    import concourse.bacc as bacc
    from concourse.bass_utils import run_bass_kernel_spmd

    nc = bacc.Bacc("TRN2", target_bir_lowering=False, num_devices=1)
    arrays, ins = {}, []
    for name in _INS:
        a = np.ascontiguousarray(inputs[name])
        arrays[f"in_{name}"] = a
        ins.append(nc.dram_tensor(f"in_{name}", a.shape, mybir.dt.from_np(a.dtype), kind="ExternalInput").ap())
    outs = [nc.dram_tensor(f"out_{i}", shape, F32, kind="ExternalOutput").ap() for i, shape in enumerate(_OUTS)]
    program(nc, ins, outs)
    r = run_bass_kernel_spmd(nc, [arrays], core_ids=[0])
    return tuple(r.results[0][f"out_{i}"] for i in range(len(_OUTS)))
```
